# Optimizing a Trainium2 kernel written in Bass

```python
import math
import jax, jax.numpy as jnp
from jax import lax
import numpy as np

'''Two consecutive layers of a hybrid autoregressive decoder trunk with sandwich RMSNorm.

Layer 0 (even): RWKV-7 time mixing (A) and sliding-window GQA with learned sinks and a
  shared T5 relative-position bias (B), as parallel head groups behind one combined input
  projection and one output projection.
Layer 1 (odd): HGRN2 gated linear recurrence with state expansion and a layer-dependent
  forget-gate lower bound (C), computed chunkwise.
Every branch has a SiLU gate path of its own width (Mamba-block style) multiplying the
branch output before the output projection; there is no separate channel mixer.

Input  x: (BATCH, SEQ, D_MODEL) float32.
Output  : (BATCH, SEQ, D_MODEL).
'''

D_MODEL = 1024
BATCH = 1
SEQ = 1024
DEPTH = 2

A_HEAD_DIM = 64
A_WIDTH = D_MODEL // 2
A_HEADS = A_WIDTH // A_HEAD_DIM
A_DECAY_LORA = 32
A_ICLR_LORA = 32
A_COLS = 4 * A_WIDTH + A_DECAY_LORA + A_ICLR_LORA
A_GN_EPS = 64e-5

B_HEAD_DIM = 64
B_WIDTH = D_MODEL // 2
B_HEADS = B_WIDTH // B_HEAD_DIM
B_KV_HEADS = 2
B_GROUP = B_HEADS // B_KV_HEADS
B_KV_WIDTH = B_KV_HEADS * B_HEAD_DIM
B_COLS = 2 * B_WIDTH + 2 * B_KV_WIDTH
WINDOW = 128
BLOCK = 128

REL_BUCKETS = 32
REL_MAX_DIST = 128

C_KEY_DIM = 128
C_VAL_DIM = 128
C_HEADS = D_MODEL // C_KEY_DIM
C_WIDTH = C_HEADS * C_VAL_DIM
C_COLS = 4 * C_WIDTH
CHUNK = 64

NORM_EPS = 1e-6
NEG_INF = -1e30

kernel_name = 'hybrid_rwkv7_swa_hgrn2_trunk'

def _split(x, sizes):
    idx = [int(i) for i in np.cumsum(sizes)[:-1]]
    return jnp.split(x, idx, axis=-1)

def rms_norm(x, w):
    xf = x.astype(jnp.float32)
    y = xf * lax.rsqrt(jnp.mean(xf * xf, axis=-1, keepdims=True) + NORM_EPS)
    return y * w.astype(jnp.float32)

def token_shift(feats, mu):
    prev = jnp.pad(feats, ((0, 0), (1, 0), (0, 0)))[:, :-1]
    return feats + mu * (prev - feats)

def t5_bucket(dist):
    max_exact = REL_BUCKETS // 2
    d = jnp.maximum(dist, 0)
    large = max_exact + (jnp.log(jnp.maximum(d, 1).astype(jnp.float32) / max_exact)
                         / math.log(REL_MAX_DIST / max_exact)
                         * (REL_BUCKETS - max_exact)).astype(jnp.int32)
    large = jnp.minimum(large, REL_BUCKETS - 1)
    return jnp.where(d < max_exact, d, large)

def rwkv7_scan(r, decay, k, v, kk, a):
    bsz, _, heads, n = r.shape
    xs = tuple(jnp.moveaxis(z, 1, 0) for z in (r, decay, k, v, kk, a))

    def step(state, inp):
        r_t, w_t, k_t, v_t, kk_t, a_t = inp
        sa = jnp.einsum('bhvk,bhk->bhv', state, -kk_t)
        state = (state * w_t[:, :, None, :]
                 + sa[..., None] * (kk_t * a_t)[:, :, None, :]
                 + v_t[..., None] * k_t[:, :, None, :])
        return state, jnp.einsum('bhvk,bhk->bhv', state, r_t)

    s0 = jnp.zeros((bsz, heads, n, n), jnp.float32)
    _, ys = lax.scan(step, s0, xs)
    return jnp.moveaxis(ys, 0, 1)

def rwkv7_branch(feats, a_w0, a_w2, a_a0, a_a2, a_k_k, a_k_a, a_r_k, a_ln_w, a_ln_b):
    bsz, t = feats.shape[:2]
    r, k, v, w_lr, a_lr = _split(feats, [A_WIDTH, A_WIDTH, A_WIDTH, A_DECAY_LORA, A_ICLR_LORA])
    w = -jax.nn.softplus(-(a_w0 + jnp.tanh(w_lr) @ a_w2)) - 0.5
    decay = jnp.exp(-jnp.exp(w))
    a = jax.nn.sigmoid(a_a0 + a_lr @ a_a2)
    kk = k * a_k_k
    k = k * (1.0 + (a - 1.0) * a_k_a)

    def hs(z):
        return z.reshape(bsz, t, A_HEADS, A_HEAD_DIM)

    kk = hs(kk)
    kk = kk / jnp.maximum(jnp.sqrt(jnp.sum(kk * kk, axis=-1, keepdims=True)), 1e-12)
    r, k, v, decay, a = hs(r), hs(k), hs(v), hs(decay), hs(a)
    y = rwkv7_scan(r, decay, k, v, kk, a)
    mean = jnp.mean(y, axis=-1, keepdims=True)
    var = jnp.mean(jnp.square(y - mean), axis=-1, keepdims=True)
    y = ((y - mean) * lax.rsqrt(var + A_GN_EPS) * a_ln_w.reshape(A_HEADS, A_HEAD_DIM)
         + a_ln_b.reshape(A_HEADS, A_HEAD_DIM))
    y = y + jnp.sum(r * k * a_r_k, axis=-1, keepdims=True) * v
    return y.reshape(bsz, t, A_WIDTH)

def swa_sink_attention(q, k, v, sinks, rel_bias_table):
    bsz, t = q.shape[:2]
    nb = t // BLOCK
    q = q.reshape(bsz, nb, BLOCK, B_KV_HEADS, B_GROUP, B_HEAD_DIM)
    pad = ((0, 0), (BLOCK, 0), (0, 0), (0, 0))
    kp = jnp.pad(k.reshape(bsz, t, B_KV_HEADS, B_HEAD_DIM), pad).reshape(bsz, nb + 1, BLOCK, B_KV_HEADS, B_HEAD_DIM)
    vp = jnp.pad(v.reshape(bsz, t, B_KV_HEADS, B_HEAD_DIM), pad).reshape(bsz, nb + 1, BLOCK, B_KV_HEADS, B_HEAD_DIM)
    kb = jnp.concatenate([kp[:, :-1], kp[:, 1:]], axis=2)
    vb = jnp.concatenate([vp[:, :-1], vp[:, 1:]], axis=2)
    scores = jnp.einsum('bnqhgd,bnkhd->bnhgqk', q, kb) * (B_HEAD_DIM ** -0.5)

    qi = jnp.arange(BLOCK)[:, None]
    kj = jnp.arange(2 * BLOCK)[None, :]
    dist = qi + BLOCK - kj
    bias = rel_bias_table[t5_bucket(dist)]
    bias = jnp.transpose(bias, (2, 0, 1)).reshape(B_KV_HEADS, B_GROUP, BLOCK, 2 * BLOCK)
    in_window = (dist >= 0) & (dist < WINDOW)
    key_pos = jnp.arange(nb)[:, None, None] * BLOCK - BLOCK + kj[None]
    valid = in_window[None] & (key_pos >= 0)
    scores = jnp.where(valid[None, :, None, None], scores + bias, NEG_INF)

    sink = sinks.reshape(B_KV_HEADS, B_GROUP)[None, None, :, :, None, None]
    m = jnp.maximum(jnp.max(scores, axis=-1, keepdims=True), sink)
    p = jnp.exp(scores - m)
    denom = jnp.sum(p, axis=-1, keepdims=True) + jnp.exp(sink - m)
    out = jnp.einsum('bnhgqk,bnkhd->bnqhgd', p / denom, vb)
    return out.reshape(bsz, t, B_WIDTH)

def rwkv_swa_layer(h, w_in, w_out, a_mu, a_w0, a_w2, a_a0, a_a2, a_k_k, a_k_a, a_r_k,
                   a_ln_w, a_ln_b, b_sinks, rel_bias_table):
    proj = h @ w_in
    a_feats = token_shift(proj[..., :A_COLS], a_mu)
    a_core, a_gate = a_feats[..., :-A_WIDTH], a_feats[..., -A_WIDTH:]
    q_b, k_b, v_b, b_gate = _split(proj[..., A_COLS:], [B_WIDTH, B_KV_WIDTH, B_KV_WIDTH, B_WIDTH])
    y_a = rwkv7_branch(a_core, a_w0, a_w2, a_a0, a_a2, a_k_k, a_k_a, a_r_k, a_ln_w, a_ln_b)
    y_b = swa_sink_attention(q_b, k_b, v_b, b_sinks, rel_bias_table)
    y = jnp.concatenate([y_a * jax.nn.silu(a_gate), y_b * jax.nn.silu(b_gate)], axis=-1)
    return y @ w_out

def hgrn2_chunkwise(q, k, v, log_f):
    bsz, t, heads, dk = q.shape
    dv = v.shape[-1]
    nc = t // CHUNK

    def chunked(z):
        return jnp.moveaxis(z.reshape(bsz, nc, CHUNK, heads, z.shape[-1]), 1, 0)

    causal = jnp.tril(jnp.ones((CHUNK, CHUNK), dtype=bool))

    def step(state, inp):
        q_c, k_c, v_c, g_c = inp
        g_cum = jnp.cumsum(g_c, axis=1)
        g_last = g_cum[:, -1]
        q_dec = q_c * jnp.exp(g_cum)
        k_inv = k_c * jnp.exp(-g_cum)
        scores = jnp.where(causal, jnp.einsum('bihk,bjhk->bhij', q_dec, k_inv), 0.0)
        o = (jnp.einsum('bhij,bjhv->bihv', scores, v_c)
             + jnp.einsum('bihk,bhkv->bihv', q_dec, state))
        k_tail = k_c * jnp.exp(g_last[:, None] - g_cum)
        state = state * jnp.exp(g_last)[..., None] + jnp.einsum('bjhk,bjhv->bhkv', k_tail, v_c)
        return state, o

    s0 = jnp.zeros((bsz, heads, dk, dv), jnp.float32)
    _, o = lax.scan(step, s0, (chunked(q), chunked(k), chunked(v), chunked(log_f)))
    return jnp.moveaxis(o, 0, 1).reshape(bsz, t, heads, dv)

def hgrn2_layer(h, layer, w_in, w_out, lower_bounds, c_norm_w):
    bsz, t = h.shape[:2]
    proj = h @ w_in
    q, f, i, g = _split(proj, [C_HEADS * C_KEY_DIM, C_HEADS * C_KEY_DIM, C_WIDTH, C_WIDTH])
    lb_soft = jax.nn.softmax(lower_bounds.astype(jnp.float32), axis=0)
    lb = (jnp.cumsum(lb_soft, axis=0) - lb_soft[0])[layer]
    forget = lb + (1.0 - lb) * jax.nn.sigmoid(f)

    def hk(z):
        return z.reshape(bsz, t, C_HEADS, C_KEY_DIM)

    def hv(z):
        return z.reshape(bsz, t, C_HEADS, C_VAL_DIM)

    o = hgrn2_chunkwise(hk(jax.nn.silu(q)), hk(1.0 - forget), hv(i), hk(jnp.log(forget)))
    o = o * lax.rsqrt(jnp.mean(o * o, axis=-1, keepdims=True) + NORM_EPS) * c_norm_w
    o = o * jax.nn.silu(hv(g))
    return o.reshape(bsz, t, C_WIDTH) @ w_out

def setup_inputs(seed: int = 0) -> dict:
    key = jax.random.key(seed)
    ks = jax.random.split(key, 23)

    def nrm(k, shape, scale):
        return jax.random.normal(k, shape, jnp.float32) * scale

    def gain(k, n):
        return 1.0 + nrm(k, (n,), 0.05)

    return {
        'x': nrm(ks[0], (BATCH, SEQ, D_MODEL), 1.0),
        'rel_bias_table': nrm(ks[1], (REL_BUCKETS, B_HEADS), 0.5),
        'lower_bounds': nrm(ks[2], (DEPTH, C_HEADS * C_KEY_DIM), 0.1),
        'l0_pre_norm': gain(ks[3], D_MODEL),
        'l0_post_norm': gain(ks[4], D_MODEL),
        'l0_w_in': nrm(ks[5], (D_MODEL, A_COLS + B_COLS), D_MODEL ** -0.5),
        'l0_w_out': nrm(ks[6], (A_WIDTH + B_WIDTH, D_MODEL), (A_WIDTH + B_WIDTH) ** -0.5),
        'a_mu': jax.random.uniform(ks[7], (A_COLS,), jnp.float32),
        'a_w0': jax.random.uniform(ks[8], (A_WIDTH,), jnp.float32, minval=-6.0, maxval=1.0),
        'a_w2': nrm(ks[9], (A_DECAY_LORA, A_WIDTH), 0.1),
        'a_a0': nrm(ks[10], (A_WIDTH,), 0.5),
        'a_a2': nrm(ks[11], (A_ICLR_LORA, A_WIDTH), A_ICLR_LORA ** -0.5),
        'a_k_k': 0.85 + nrm(ks[12], (A_WIDTH,), 0.05),
        'a_k_a': gain(ks[13], A_WIDTH),
        'a_r_k': nrm(ks[14], (A_HEADS, A_HEAD_DIM), 0.1),
        'a_ln_w': gain(ks[15], A_WIDTH),
        'a_ln_b': nrm(ks[16], (A_WIDTH,), 0.01),
        'b_sinks': nrm(ks[17], (B_HEADS,), 1.0),
        'l1_pre_norm': gain(ks[18], D_MODEL),
        'l1_post_norm': gain(ks[19], D_MODEL),
        'l1_w_in': nrm(ks[20], (D_MODEL, C_COLS), D_MODEL ** -0.5),
        'l1_w_out': nrm(ks[21], (C_WIDTH, D_MODEL), C_WIDTH ** -0.5),
        'c_norm_w': gain(ks[22], C_VAL_DIM),
    }

def reference(x, rel_bias_table, lower_bounds, l0_pre_norm, l0_post_norm, l0_w_in, l0_w_out,
              a_mu, a_w0, a_w2, a_a0, a_a2, a_k_k, a_k_a, a_r_k, a_ln_w, a_ln_b, b_sinks,
              l1_pre_norm, l1_post_norm, l1_w_in, l1_w_out, c_norm_w):
    for layer in range(DEPTH):
        if layer % 2 == 0:
            h = rms_norm(x, l0_pre_norm)
            y = rwkv_swa_layer(h, l0_w_in, l0_w_out, a_mu, a_w0, a_w2, a_a0, a_a2, a_k_k, a_k_a,
                               a_r_k, a_ln_w, a_ln_b, b_sinks, rel_bias_table)
            x = x + rms_norm(y, l0_post_norm).astype(x.dtype)
        else:
            h = rms_norm(x, l1_pre_norm)
            y = hgrn2_layer(h, layer, l1_w_in, l1_w_out, lower_bounds, c_norm_w)
            x = x + rms_norm(y, l1_post_norm).astype(x.dtype)
    return x


_drawn_inputs = setup_inputs


def setup_inputs(seed=0):
    import zlib

    import numpy as np

    out = dict(_drawn_inputs(seed))
    spreads = {}
    factors = {'lower_bounds': 7.187, 'a_ln_b': 6.51, 'b_sinks': 8.0}
    for name, (base, spread) in spreads.items():
        noise = np.random.default_rng([zlib.crc32(name.encode()), seed]).standard_normal(out[name].shape)
        drawn = base * np.exp(spread * noise) if base else spread * noise
        out[name] = __import__('jax').numpy.asarray(drawn.astype(out[name].dtype))
    for name, factor in factors.items():
        out[name] = (out[name] * factor).astype(out[name].dtype)
    return out
```

```python
from contextlib import ExitStack

import numpy as np

import concourse.bass as bass
from concourse import mybir

ALU = mybir.AluOpType
ACT = mybir.ActivationFunctionType
AX = mybir.AxisListType
F32 = mybir.dt.float32
F32R = mybir.dt.float32r

P = 128
D = 1024
T = 1024
KT = D // P
HALF = 512
C = 128
NC = T // C
HD = 64
PAIRS = 4
LEVELS = 7
LORA = 64
NORM_EPS = 1e-6
GN_EPS = 64e-5
DECAY = float(np.exp(-0.5))
BUCKETS = 32
A_COLS = 2112
COL_R, COL_K, COL_V, COL_LORA, COL_AG = 0, 512, 1024, 1536, 1600
COL_Q, COL_BK, COL_BV, COL_BG = A_COLS, A_COLS + 512, A_COLS + 640, A_COLS + 768
KV = 2
HEADS_C = 8
NEG = -1e30

SLAB_LORA = 0
SLAB_A = 1
SLAB_V = SLAB_A + 4 * PAIRS
SLAB_B = SLAB_V + 1
SLAB_O0 = SLAB_B + 5 * KV
SLAB_C = SLAB_O0 + 8
SLAB_O1 = SLAB_C + 4 * HEADS_C
SLABS = SLAB_O1 + 8

RAW_KINDS = 11
MU, W0, A0, KK, KA, RK, LNW, LNB = 0, 4, 5, 6, 7, 8, 9, 10
OMU, W0H, A0H, KAH, OKAH = 11, 15, 16, 17, 18
KINDS = 19
PRE0, POST0, PRE1, POST1, LB0, LB1, CN, MUL = 44, 52, 60, 68, 76, 84, 92, 93
ROWS = 94

CI, CO64, CM, CL, CN7 = 0, 128, 256, 768, 896
CONSTS = CN7 + 128 * LEVELS


def constants():
    s = np.arange(P)[:, None]
    t = np.arange(P)[None, :]
    c = np.zeros((P, CONSTS), np.float32)
    c[:, CI:CI + P] = s == t
    c[:, CO64:CO64 + P] = s // HD == t // HD
    for q in range(4):
        c[:, CM + P * q:CM + P * (q + 1)] = (s < t) if q % 2 == 0 else (s <= t)
    c[:, CL:CL + P] = s > t
    for k in range(LEVELS):
        b = 1 << k
        m = (s // (2 * b) == t // (2 * b)) & ((s // b) % 2 == 0) & ((t // b) % 2 == 1)
        c[:, CN7 + P * k:CN7 + P * (k + 1)] = -1.0 * m
    return c


def bucket_table():
    c = np.zeros((BUCKETS, 768), np.float32)
    half = BUCKETS // 2
    c[:, 384:768] = NEG
    for m in range(128, 256):
        dist = 255 - m
        far = half + int(np.log(np.float32(max(dist, 1)) / half) / np.log(128 / half) * half)
        c[dist if dist < half else min(far, BUCKETS - 1), m] = 1.0
        c[:, 384 + m] = 0.0
    return c


class Steps:

    def __init__(self, eng, sem):
        self.eng, self.sem, self.n, self.i, self.per, self.start = eng, sem, 0, None, 0, 0

    def on(self, ins):
        ins.then_inc(self.sem, 1)
        self.n += 1

    def wait(self):
        self.eng.wait_ge(self.sem, self.n if self.i is None else self.i * self.per + self.n)

    def enter(self, i, per):
        self.i, self.per, self.start = i, per, self.n

    def leave(self, times):
        assert self.n - self.start == self.per, (self.n - self.start, self.per)
        self.n, self.i = self.start + self.per * times, None


def trunk(nc, x, table, lbs, pre0, post0, w_in0, w_out0, mu, w0, w2, a0, a2, k_k, k_a, r_k, ln_w,
          ln_b, sinks, pre1, post1, w_in1, w_out1, c_norm, cst_in, buckets, scratch, out):
    with ExitStack() as ctx:
        def sb(name, shape, dt=F32):
            return ctx.enter_context(nc.sbuf_tensor(name, shape, dt))

        def sem(name):
            return ctx.enter_context(nc.semaphore(name))

        bank = [ctx.enter_context(nc.psum_tensor(f"bank{i}", [P, HALF], F32)) for i in range(8)]
        PJ, SC, ZB, DP, SQ = bank[0:2], bank[2:4], bank[4], bank[5:7], bank[7]

        h_hi = sb("h_hi", [P, KT, T], F32R)
        h_lo = sb("h_lo", [P, KT, T], F32R)
        yT = sb("yT", [P, KT, T])
        zT = sb("zT", [P, KT, T])
        w_raw = sb("w_raw", [P, 2, KT, P])
        w_hi = sb("w_hi", [P, 2, KT, P], F32R)
        w_lo = sb("w_lo", [P, 2, KT, P], F32R)
        cst = sb("cst", [P, CONSTS])
        work = sb("work", [P, 9 * T + 64])
        par_raw = sb("par_raw", [ROWS, P])
        par = sb("par", [P, KINDS, 4])
        oth = sb("oth", [P, ROWS - 44])
        lbp = sb("lbp", [P, 6, 8])
        pp = sb("pp", [P, KINDS])
        rms = sb("rms", [P, 16])
        lw = sb("lw", [LORA, HALF])
        lwp = sb("lwp", [LORA, P])
        rkm = sb("rkm", [P, P])
        eps = sb("eps", [P, 4])
        fac = sb("fac", [P, 2, 8])
        sinkb = sb("sinkb", [P, 8])
        tb = sb("tb", [BUCKETS, 8])
        soft = sb("soft", [P, 2, 24])
        lbc = sb("lbc", [P, 2])
        ones_all = sb("ones_all", [P, P])
        reset_c = sb("reset_c", [P, HALF])
        ident = cst[:, CI:CI + P]
        ones64 = cst[:, CO64:CO64 + P]

        own_act, own_dve, own_pool = (sem(f"own_{e}") for e in ("act", "dve", "pool"))
        phase_done = sem("phase_done")
        par_zeroed, const_in, par_in, small_in = (sem(n) for n in ("par_zeroed", "const_in", "par_in", "small_in"))
        x_in = [sem(f"x_in{i}") for i in range(2)]
        w_in = [sem(f"weights_in{i}") for i in range(2)]
        w_split = sem("weights_split")
        proj_full = [sem(f"proj_full{i}") for i in range(2)]
        proj_free = [sem(f"proj_free{i}") for i in range(2)]
        sc_full = [sem(f"sc_full{i}") for i in range(2)]
        sc_free = [sem(f"sc_free{i}") for i in range(2)]
        par_full, bias_full, bias_row, scr_in, scr_out = (
            sem(n) for n in ("par_full", "bias_full", "bias_row", "scr_in", "scr_out"))
        par_ready, eps_ready = sem("par_ready"), sem("eps_ready")
        rstd_ready, xn_ready, hi_ready, lo_ready = (sem(n) for n in ("rstd_ready", "xn_ready", "hi_ready", "lo_ready"))
        pp_ready, lwp_ready, rkm_ready, mix_scaled, lora_ready, gate_ready = (
            sem(n) for n in ("pp_ready", "lwp_ready", "rkm_ready", "mix_scaled", "lora_ready", "gate_ready"))
        ksq_ready, gc_ready, exp_ready, rn_ready, kk_ready, t_ready, kp_ready, kq_ready, rk_ready, ab_ready = (
            sem(n) for n in ("ksq_ready", "gc_ready", "exp_ready", "rn_ready", "kk_ready", "t_ready",
                             "kp_ready", "kq_ready", "rk_ready", "ab_ready"))
        z_full, lm_ready, xt_ready = sem("z_full"), sem("lm_ready"), sem("xt_ready")
        dp_full = [sem(f"dp_full{i}") for i in range(2)]
        dp_copied = sem("dp_copied")
        rhs_full, nr_ready, sa_full, sa_ready, sy_full, state_ready, y_copied = (
            sem(n) for n in ("rhs_full", "nr_ready", "sa_full", "sa_ready", "sy_full", "state_ready", "y_copied"))
        vt_full, vt_ready, m_ready, p_ready, es_ready, o_full, o_ready, ot_full, y_out = (
            sem(n) for n in ("vt_full", "vt_ready", "m_ready", "p_ready", "es_ready", "o_full", "o_ready", "ot_full", "y_out"))
        pt_full = [sem(f"pt_full{i}") for i in range(2)]
        pt_copied = [sem(f"pt_copied{i}") for i in range(2)]
        y_hi, y_split, x_again, h_ready, h_hi_ready, h_lo_ready, sq_ready, sq_used, norm_ready, final_ready = (
            sem(n) for n in ("y_hi", "y_split", "x_again", "h_ready", "h_hi_ready", "h_lo_ready", "sq_ready",
                             "sq_used", "norm_ready", "final_ready"))
        xt_full, xt_added, out_full, out_copied, out_done = (
            [sem(f"{n}{i}") for i in range(2)] for n in ("xt_full", "xt_added", "out_full", "out_copied", "out_done"))
        lb_step, lb_exp, lb_ready, ln_ready, gcc_ready, expc_ready, kc_ready, qc_ready = (
            sem(n) for n in ("lb_step", "lb_exp", "lb_ready", "ln_ready", "gcc_ready", "expc_ready", "kc_ready", "qc_ready"))
        tc_ready, inc_full, oc_full, oc_copied, sc_state, osq_ready, orn_ready = (
            sem(n) for n in ("tc_ready", "inc_full", "oc_full", "oc_copied", "sc_state", "osq_ready", "orn_ready"))
        head_done = sem("head_done")
        ysq_ready, ynorm_ready = sem("ysq_ready"), sem("ynorm_ready")

        def phase_end(eng, k):
            eng.drain().then_inc(phase_done, 1)
            eng.wait_ge(phase_done, 5 * (k + 1))

        def buf(n):
            return work[:, 4 * 1032 + n * T:4 * 1032 + (n + 1) * T]

        xt = [zT[:, j, :] for j in range(2)]
        xn = [zT[:, 2 + j, :] for j in range(2)]
        hf = [zT[:, 4 + j, :].rearrange("p (k t) -> p k t", k=KT) for j in range(2)]
        bk = zT[0:BUCKETS, 6, 0:768]
        brow = zT[0:8, 7, 0:384]
        u = [work[:, j * 1032:j * 1032 + T + 1] for j in range(2)]
        gc = work[:, 2 * 1032:3 * 1032].rearrange("p (c t) -> p c t", c=NC)
        ee = work[:, 3 * 1032:4 * 1032].rearrange("p (c t) -> p c t", c=NC)
        ysb = work[:, 3 * 1032:3 * 1032 + T]
        ysq = work[:, 2 * 1032:2 * 1032 + T]
        rb, kb, vb, gb, bb, kt = (zT[:, n, :] for n in (0, 1, 2, 3, 4, 7))
        ar = zT[:, 5:7, :]
        ldb, gcum, em, kkb = (buf(n) for n in range(4))
        scm = zT[:, 0:2, :].rearrange("p a (b t) -> p (a b) t", b=2)
        tm = ldb[:, 0:768].rearrange("p (j n) -> p j n", j=2)
        nr = ldb[:, 768:1024].rearrange("p (j n) -> p j n", j=2)
        lm = gcum[:, 0:512]
        xtm = gcum[:, 512:1024]
        dps = kkb
        sa = buf(4)[:, 0:256].rearrange("p (j n) -> p j n", j=2)
        st = buf(4)[:, 256:384]
        st2 = buf(4)[:, 384:512]
        reset = buf(4)[:, 512:1024]
        lora = yT[0:LORA, 4, :]

        def load_slab(sp, s, slot, uses, src):
            if not (isinstance(s, int) and s < 2):
                sp.wait_ge(w_split, s - 1)
            sp.dma_start(w_raw[:, slot, :, 0:src.shape[-1]], src).then_inc(w_in[slot], 16)

        def split_slab(pool, own, s, slot, uses, n=P):
            pool.wait_ge(w_in[slot], uses * 16 + 16)
            if not (isinstance(s, int) and s < 2):
                pool.wait_ge(proj_full[1], s - 1)
            own.on(nc.gpsimd.tensor_tensor(w_hi[:, slot, :, 0:n], w_raw[:, slot, :, 0:n],
                                           wide(zeros[:, 0:n], KT), ALU.add))
            own.wait()
            nc.gpsimd.tensor_tensor(w_lo[:, slot, :, 0:n], w_raw[:, slot, :, 0:n],
                                    w_hi[:, slot, :, 0:n], ALU.subtract).then_inc(w_split, 1)

        def project(pe, s, slot, m=P):
            pe.wait_ge(w_split, s + 1)
            for h in range(2):
                if not (isinstance(s, int) and s == 0):
                    pe.wait_ge(proj_free[h], s)
                n = 0
                for k in range(KT):
                    for a, b in ((w_hi, h_hi), (w_lo, h_hi), (w_hi, h_lo)):
                        mm = nc.tensor.matmul(PJ[h][0:m, :], a[:, slot, k, 0:m],
                                              b[:, k, h * HALF:(h + 1) * HALF],
                                              start=n == 0, stop=n == 3 * KT - 1)
                        n += 1
                mm.then_inc(proj_full[h], 1)

        def columns(w, c0, n=P):
            return w.rearrange("(k p) c -> p k c", p=P)[:, :, c0:c0 + n]

        def columns_at(w, c0, i, step):
            return w.rearrange("(k p) c -> p k c", p=P)[:, :, bass.ds(i * step + c0, P)]

        def at(i, per, n):
            return i * per + n

        zeros = sb("zeros", [P, P])

        def wide(ap, n):
            return ap.rearrange("p (o m) -> p o m", o=1).broadcast_to([ap.shape[0], n, ap.shape[1]])

        def each(ap, n):
            return ap.rearrange("p (m o) -> p m o", o=1).broadcast_to([ap.shape[0], ap.shape[1], n])

        X0 = 8

        def sync_0(sp):
            sp.dma_start(cst[:], cst_in).then_inc(const_in, 16)
            sp.wait_ge(par_zeroed, 1)
            rows = [(0, 12, mu[0:1536]), (12, 4, mu[1600:2112]), (16, 4, w0), (20, 4, a0), (24, 4, k_k),
                    (28, 4, k_a), (36, 4, ln_w), (40, 4, ln_b), (PRE0, 8, pre0),
                    (POST0, 8, post0), (PRE1, 8, pre1), (POST1, 8, post1), (CN, 1, c_norm)]
            for r0, n, src in rows:
                sp.dma_start(par_raw[r0:r0 + n, :], src.rearrange("(r c) -> r c", c=P)).then_inc(par_in, 16)
            sp.dma_start(par_raw[32:36, :], r_k.rearrange("(g h) c -> g (h c)", h=2)).then_inc(par_in, 16)
            sp.dma_start(par_raw[LB0:LB0 + 16, :], lbs.rearrange("l (r c) -> (l r) c", c=P)).then_inc(par_in, 16)
            sp.dma_start(par_raw[MUL:MUL + 1, 0:LORA],
                         mu[1536:1600].rearrange("(r c) -> r c", r=1)).then_inc(par_in, 16)
            for tile in range(NC):
                j = tile % 2
                if tile >= 2:
                    sp.wait_ge(xn_ready, tile - 1)
                sp.dma_start(xt[j], x[tile * P:(tile + 1) * P, :]).then_inc(x_in[j], 16)
                if tile == 1:
                    sp.dma_start(lw[0:32, :], w2).then_inc(small_in, 16)
                    sp.dma_start(lw[32:64, :], a2).then_inc(small_in, 16)
                    sp.dma_start(tb[:], table).then_inc(small_in, 16)
                    sp.dma_start(bk, buckets).then_inc(small_in, 16)
                    sp.dma_start(sinkb[:], sinks.rearrange("(o h) -> o h", o=1).broadcast_to([P, 8])).then_inc(small_in, 16)
            sp.wait_ge(bias_row, 1)
            sp.dma_start(scratch.rearrange("q h m -> h q m"),
                         brow.rearrange("h (o m) -> h o m", o=1).broadcast_to([8, P, 384])).then_inc(scr_out, 16)
            sp.wait_ge(scr_out, 16)

        def pool_0(pool, own):
            nc.gpsimd.memset(par_raw[:], 0.0).then_inc(par_zeroed, 1)
            own.on(nc.gpsimd.memset(zeros[:], 0.0))
            nc.gpsimd.memset(ones_all[:], 1.0)
            for n, v in enumerate((NORM_EPS, GN_EPS, 20 * float(np.log(2.0)), 1.0)):
                ins = nc.gpsimd.memset(eps[:, n:n + 1], v)
            ins.then_inc(eps_ready, 1)
            for tile in range(NC):
                j = tile % 2
                pool.wait_ge(hi_ready, tile + 1)
                nc.gpsimd.tensor_tensor(h_lo[:, :, tile * P:(tile + 1) * P], hf[j],
                                        h_hi[:, :, tile * P:(tile + 1) * P], ALU.subtract).then_inc(lo_ready, 1)

        def tensor_0(pe):
            pe.wait_ge(const_in, 16)
            pe.wait_ge(par_in, 16 * 16)
            nc.tensor.transpose(ZB[:, 0:ROWS], par_raw[:], cst[0:ROWS, CI:CI + ROWS]).then_inc(par_full, 1)
            for tile in range(NC):
                j = tile % 2
                pe.wait_ge(xn_ready, tile + 1)
                for b in range(2):
                    if tile:
                        pe.wait_ge(sc_free[b], tile)
                    for k in range(4):
                        kk = 4 * b + k
                        mm = nc.tensor.transpose(SC[b][:, k * P:(k + 1) * P], xn[j][:, kk * P:(kk + 1) * P], ident)
                    mm.then_inc(sc_full[b], 1)
            pe.wait_ge(small_in, 16 * 5)
            nc.tensor.matmul(DP[0][0:8, 0:384], tb[:], bk[:, 0:384], start=True, stop=True).then_inc(bias_full, 1)

        def scalar_0(act, own):
            act.wait_ge(eps_ready, 1)
            for tile in range(NC):
                j = tile % 2
                act.wait_ge(x_in[j], 16 * (tile // 2 + 1))
                if tile >= 2:
                    act.wait_ge(sc_full[1], tile - 1)
                own.on(nc.scalar.activation(xn[j], xt[j], ACT.Square, accum_out=rms[:, j:j + 1]))
                own.wait()
                own.on(nc.scalar.activation(rms[:, 2 + j:3 + j], rms[:, j:j + 1], ACT.Ln, scale=1.0 / D, bias=eps[:, 0:1]))
                own.wait()
                nc.scalar.activation(rms[:, 4 + j:5 + j], rms[:, 2 + j:3 + j], ACT.Exp, scale=-0.5).then_inc(rstd_ready, 1)
                act.wait_ge(sc_free[1], tile + 1)
                act.wait_ge(sc_free[0], tile + 1)
                nc.scalar.activation(h_hi[:, :, tile * P:(tile + 1) * P], hf[j], ACT.Copy).then_inc(hi_ready, 1)

        def vector_0(dve, own):
            dve.wait_ge(par_full, 1)
            own.on(nc.vector.tensor_copy(par[:, 0:RAW_KINDS, :].rearrange("p k f -> p (k f)"), ZB[:, 0:44]))
            own.on(nc.vector.tensor_copy(oth[:], ZB[:, 44:ROWS]))
            own.wait()
            nc.vector.tensor_scalar(par[:, OMU:OMU + 4, :], par[:, 0:4, :], -1.0, 1.0, ALU.mult, ALU.add)
            nc.vector.tensor_scalar(par[:, W0H:W0H + 2, :], par[:, W0:W0 + 2, :], 0.5, None, ALU.mult)
            nc.vector.tensor_scalar(par[:, KAH:KAH + 1, :], par[:, KA:KA + 1, :], 0.5, None, ALU.mult)
            nc.vector.tensor_scalar(par[:, OKAH:OKAH + 1, :], par[:, KA:KA + 1, :], -0.5, 1.0, ALU.mult, ALU.add)
            own.on(nc.vector.tensor_scalar(lbp[:, 0, 0:1], oth[:, MUL - 44:MUL - 43], -1.0, 1.0, ALU.mult, ALU.add))
            for j in range(2):
                own.on(nc.vector.memset(u[j][:, 0:1], 0.0))
            own.on(nc.vector.memset(reset[:], 1.0))
            own.wait()
            nc.vector.memset(reset[:].rearrange("p (c t) -> p c t", t=C)[:, :, 0:1], 0.0).then_inc(par_ready, 1)
            for tile in range(NC):
                j = tile % 2
                dve.wait_ge(rstd_ready, tile + 1)
                nc.vector.tensor_scalar(xn[j], xt[j], rms[:, 4 + j:5 + j], None, ALU.mult).then_inc(xn_ready, 1)
                if tile >= 2:
                    dve.wait_ge(lo_ready, tile - 1)
                for b in range(2):
                    dve.wait_ge(sc_full[b], tile + 1)
                    nc.vector.tensor_tensor(hf[j][:, 4 * b:4 * b + 4, :], SC[b][:].rearrange("p (k t) -> p k t", k=4),
                                            each(oth[:, PRE0 - 44 + 4 * b:PRE0 - 44 + 4 * b + 4], P),
                                            ALU.mult).then_inc(sc_free[b], 1)
            dve.wait_ge(bias_full, 1)
            nc.vector.tensor_tensor(brow, DP[0][0:8, 0:384], bk[0:8, 384:768], ALU.add).then_inc(bias_row, 1)

        def sync_a(sp):
            load_slab(sp, SLAB_LORA, 0, 0, columns(w_in0, COL_LORA, LORA))
            with sp.Fori(0, PAIRS) as i:
                for q, col in enumerate((COL_R, COL_K, COL_V, COL_AG)):
                    load_slab(sp, at(i, 4, SLAB_A + q), (SLAB_A + q) % 2, at(i, 2, (SLAB_A + q) // 2),
                              columns_at(w_in0, col, i, P))

        def pool_a(pool, own):
            split_slab(pool, own, SLAB_LORA, 0, 0, LORA)
            with pool.Fori(0, PAIRS) as i:
                own.enter(i, 4)
                for q in range(4):
                    split_slab(pool, own, at(i, 4, SLAB_A + q), (SLAB_A + q) % 2, at(i, 2, (SLAB_A + q) // 2))
                pool.wait_ge(t_ready, at(i, 1, 1))
                nc.gpsimd.tensor_tensor(gcum[:], gcum[:], kb[:], ALU.mult).then_inc(kp_ready, 1)
                pool.wait_ge(kp_ready, at(i, 1, 1))
                pool.wait_ge(exp_ready, at(i, 3, 3))
                nc.gpsimd.tensor_tensor(kt[:], gcum[:], em[:], ALU.mult).then_inc(kq_ready, 1)
                nc.gpsimd.tensor_tensor(ldb[:], gcum[:], rb[:], ALU.mult).then_inc(rk_ready, 1)
                own.leave(PAIRS)
        GROUPS = NC // 2

        def tensor_a(pe):
            project(pe, SLAB_LORA, 0, LORA)
            with pe.Fori(0, PAIRS) as i:
                for q in range(4):
                    project(pe, at(i, 4, SLAB_A + q), (SLAB_A + q) % 2)
                use = X0
                pe.wait_ge(lora_ready, 2)
                pe.wait_ge(lwp_ready, at(i, 1, 1))
                for r in range(2):
                    for h in range(2):
                        pe.wait_ge(sc_free[h], at(i, 18, use))
                        nc.tensor.matmul(SC[h][:], lwp[32 * r:32 * r + 32, :],
                                         lora[32 * r:32 * r + 32, h * HALF:(h + 1) * HALF],
                                         start=True, stop=True).then_inc(sc_full[h], 1)
                    use += 1
                pe.wait_ge(ksq_ready, at(i, 1, 1))
                for h in range(2):
                    pe.wait_ge(sc_free[h], at(i, 18, use))
                    nc.tensor.matmul(SC[h][:], ones64, kkb[:, h * HALF:(h + 1) * HALF],
                                     start=True, stop=True).then_inc(sc_full[h], 1)
                use += 1
                pe.wait_ge(rkm_ready, at(i, 1, 1))
                pe.wait_ge(rk_ready, at(i, 1, 1))
                for h in range(2):
                    pe.wait_ge(sc_free[h], at(i, 18, use))
                    nc.tensor.matmul(SC[h][:], rkm[:], ldb[:, h * HALF:(h + 1) * HALF],
                                     start=True, stop=True).then_inc(sc_full[h], 1)
                use += 1
                pe.wait_ge(ab_ready, at(i, 3, 3))
                for g in range(GROUPS):
                    for j in range(2):
                        c = slice((2 * g + j) * C, (2 * g + j + 1) * C)
                        pe.wait_ge(sc_free[j], at(i, 18, use))
                        for n, src in enumerate((vb, bb, kt)):
                            mm = nc.tensor.transpose(SC[j][:, n * P:(n + 1) * P], src[:, c], ident)
                        mm.then_inc(sc_full[j], 1)
                    for j in range(2):
                        c = slice((2 * g + j) * C, (2 * g + j + 1) * C)
                        for h in range(2):
                            hp = slice(h * HD, (h + 1) * HD)
                            pe.wait_ge(sc_free[h], at(i, 18, use + 1 + j))
                            for n, src in enumerate((bb, kt)):
                                mm = nc.tensor.matmul(SC[h][:, n * 256:(n + 1) * 256].rearrange("p (a t) -> p a t", a=2),
                                                      src[hp, c], ar[hp, :, c], start=True, stop=True)
                            mm.then_inc(sc_full[h], 1)
                    pe.wait_ge(state_ready, at(i, 9, 2 * g + 1))
                    pe.wait_ge(y_copied, at(i, 8, 2 * g + 1))
                    for j in range(2):
                        c = slice((2 * g + j) * C, (2 * g + j + 1) * C)
                        for h in range(2):
                            hp = slice(h * HD, (h + 1) * HD)
                            dst = SQ if h else ZB
                            mm = nc.tensor.matmul(dst[:, j * P:(j + 1) * P], ar[hp, 0, c], bb[hp, c],
                                                  start=True, stop=True)
                    mm.then_inc(z_full, 1)
                    for k in range(LEVELS):
                        if k:
                            pe.wait_ge(dp_copied, at(i, 56, 14 * g + 2 * k))
                            if k == 1:
                                pe.wait_ge(lm_ready, at(i, 8, 2 * g + 2))
                            for un in range(4):
                                b, v = un // 2, un % 2
                                mm = nc.tensor.matmul(ZB[:, un * P:(un + 1) * P], lm[:, un * P:(un + 1) * P],
                                                      dps[:, b * HALF + v * 256 + P:b * HALF + v * 256 + 256],
                                                      start=True, stop=True)
                            mm.then_inc(z_full, 1)
                        else:
                            if g:
                                pe.wait_ge(dp_copied, at(i, 56, 14 * g))
                            for b in range(2):
                                nc.tensor.matmul(DP[b][:].rearrange("p (n t) -> p n t", n=4), ident, wide(ident, 4),
                                                 start=True, stop=True, skip_group_check=True)
                        pe.wait_ge(xt_ready, at(i, 28, 7 * g + k + 1))
                        for un in range(4):
                            b, v = un // 2, un % 2
                            xs = xtm[:, un * P:(un + 1) * P]
                            d0, p0 = v * 256, v * 256 + P
                            dk = ident if k == 0 else dps[:, b * HALF + d0:b * HALF + d0 + P]
                            nc.tensor.matmul(DP[b][:, d0:d0 + P], xs, dk, start=False, stop=True, skip_group_check=True)
                            mm = nc.tensor.matmul(DP[b][:, p0:p0 + P], dk, xs, start=False, stop=True,
                                                  skip_group_check=True)
                            if v:
                                mm.then_inc(dp_full[b], 1)
                    pe.wait_ge(dp_copied, at(i, 56, 14 * g + 14))
                    for j in range(2):
                        cn = 2 * g + j
                        c = slice(cn * C, (cn + 1) * C)
                        pe.wait_ge(state_ready, at(i, 9, cn + 1))
                        if j == 0:
                            pe.wait_ge(sc_free[0], at(i, 18, use + 3))
                            pe.wait_ge(sc_free[1], at(i, 18, use + 3))
                        nc.tensor.matmul(SQ[:, 0:P], ar[:, 0, c], st[:], start=True, stop=True)
                        for h in range(2):
                            un = 2 * j + h
                            mm = nc.tensor.matmul(SQ[:, h * HD:(h + 1) * HD], scm[:, un, 256:384],
                                                  tm[:, j, h * HD:(h + 1) * HD], start=False, stop=True,
                                                  skip_group_check=True)
                        mm.then_inc(rhs_full, 1)
                        pe.wait_ge(nr_ready, at(i, 8, cn + 1))
                        for h in range(2):
                            un = 2 * j + h
                            b, v = un // 2, un % 2
                            mm = nc.tensor.matmul(SQ[:, P + h * HD:P + (h + 1) * HD],
                                                  dps[:, b * HALF + v * 256 + P:b * HALF + v * 256 + 256],
                                                  nr[:, j, h * HD:(h + 1) * HD], start=True, stop=True)
                        mm.then_inc(sa_full, 1)
                        pe.wait_ge(sa_ready, at(i, 8, cn + 1))
                        pe.wait_ge(y_copied, at(i, 8, cn + 1))
                        nc.tensor.matmul(SQ[:, 256:384], tm[:, j, P:2 * P], sa[:, j, :], start=True, stop=False)
                        nc.tensor.matmul(SQ[:, 256:384], tm[:, j, 2 * P:3 * P], tm[:, j, 0:P], start=False, stop=True)
                        nc.tensor.matmul(ZB[:, 384:512], st[:], ar[:, 1, c], start=True, stop=True)
                        for h in range(2):
                            hp = slice(h * HD, (h + 1) * HD)
                            un = 2 * j + h
                            nc.tensor.matmul(ZB[hp, 384:512], sa[:, j, hp], scm[:, un, P:2 * P], start=False, stop=True,
                                             skip_group_check=True)
                            mm = nc.tensor.matmul(ZB[hp, 384:512], tm[:, j, hp], scm[:, un, 3 * P:4 * P], start=False,
                                                  stop=True, skip_group_check=True)
                        mm.then_inc(sy_full, 1)
                    use += 3
                pe.wait_ge(y_copied, at(i, 8, 9))
                for h in range(2):
                    pe.wait_ge(sc_free[h], at(i, 18, use))
                    nc.tensor.matmul(SC[h][:], ones64, ysb[:, h * HALF:(h + 1) * HALF],
                                     start=True, stop=True).then_inc(sc_full[h], 1)
                use += 1
                pe.wait_ge(ysq_ready, at(i, 1, 1))
                for h in range(2):
                    pe.wait_ge(sc_free[h], at(i, 18, use))
                    nc.tensor.matmul(SC[h][:], ones64, ysq[:, h * HALF:(h + 1) * HALF],
                                     start=True, stop=True).then_inc(sc_full[h], 1)

        def scalar_a(act, own):
            act.wait_ge(par_ready, 1)
            for h in range(2):
                act.wait_ge(proj_full[h], 1)
                nc.scalar.activation(u[0][0:LORA, 1 + h * HALF:1 + (h + 1) * HALF], PJ[h][0:LORA, :], ACT.Copy,
                                     scale=oth[0:LORA, MUL - 44:MUL - 43]).then_inc(mix_scaled, 1)
            act.wait_ge(proj_free[1], 1)
            nc.scalar.activation(lora[0:32, :], lora[0:32, :], ACT.Tanh).then_inc(lora_ready, 1)
            nc.scalar.activation(lora[32:64, 0:1], lora[32:64, 0:1], ACT.Copy).then_inc(lora_ready, 1)
            nc.scalar.activation(eps[:, 3:4], eps[:, 3:4], ACT.Copy).then_inc(y_copied, 1)
            with act.Fori(0, PAIRS) as i:
                own.enter(i, 1)
                act.wait_ge(pp_ready, at(i, 1, 1))
                for q in range(4):
                    for h in range(2):
                        act.wait_ge(proj_full[h], at(i, 4, SLAB_A + q + 1))
                        nc.scalar.activation(u[q % 2][:, 1 + h * HALF:1 + (h + 1) * HALF], PJ[h][:], ACT.Copy,
                                             scale=pp[:, MU + q:MU + q + 1]).then_inc(mix_scaled, 1)
                act.wait_ge(proj_free[1], at(i, 4, SLAB_A + 4))
                nc.scalar.activation(gb[:], gb[:], ACT.Silu).then_inc(gate_ready, 1)
                for r, (dst, kind) in enumerate(((ldb, W0H), (bb, A0H))):
                    for h in range(2):
                        act.wait_ge(sc_full[h], at(i, 18, X0 + r + 1))
                        nc.scalar.activation(dst[:, h * HALF:(h + 1) * HALF], SC[h][:], ACT.Tanh, scale=0.5,
                                             bias=pp[:, kind:kind + 1]).then_inc(sc_free[h], 1)
                nc.scalar.activation(kkb[:], kb[:], ACT.Square, scale=pp[:, KK:KK + 1]).then_inc(ksq_ready, 1)
                act.wait_ge(gc_ready, at(i, 1, 1))
                nc.scalar.activation(ee[:, :, 0:C + 1], gc[:, :, 0:C + 1], ACT.Exp).then_inc(exp_ready, 1)
                nc.scalar.activation(fac[:, 1, 0:7], fac[:, 0, 0:7], ACT.Exp).then_inc(exp_ready, 1)
                nc.scalar.activation(em[:].rearrange("p (c t) -> p c t", c=NC), gc[:, :, 1:C + 1], ACT.Exp,
                                     scale=-1.0).then_inc(exp_ready, 1)
                act.wait_ge(sc_free[0], at(i, 18, X0 + 3))
                act.wait_ge(sc_free[1], at(i, 18, X0 + 3))
                own.on(nc.scalar.activation(kkb[:], kkb[:], ACT.Ln, scale=2.0 ** 40))
                own.wait()
                nc.scalar.activation(kkb[:], kkb[:], ACT.Exp, scale=-0.5, bias=eps[:, 2:3]).then_inc(rn_ready, 1)
                use = X0 + 4
                for g in range(GROUPS):
                    for j in range(2):
                        act.wait_ge(sc_full[j], at(i, 18, use + 1))
                        nc.scalar.activation(tm[:, j, :], SC[j][:, 0:384], ACT.Copy).then_inc(sc_free[j], 1)
                    for k in range(LEVELS):
                        for b in range(2):
                            act.wait_ge(dp_full[b], at(i, 28, 7 * g + k + 1))
                            nc.scalar.activation(dps[:, b * HALF:(b + 1) * HALF], DP[b][:], ACT.Copy).then_inc(dp_copied, 1)
                    for j in range(2):
                        cn = 2 * g + j
                        act.wait_ge(rhs_full, at(i, 8, cn + 1))
                        nc.scalar.activation(nr[:, j, :], SQ[:, 0:P], ACT.Copy, scale=-1.0).then_inc(nr_ready, 1)
                        act.wait_ge(sa_full, at(i, 8, cn + 1))
                        nc.scalar.activation(sa[:, j, :], SQ[:, P:2 * P], ACT.Copy).then_inc(sa_ready, 1)
                        act.wait_ge(sy_full, at(i, 8, cn + 1))
                        nc.scalar.activation(ysb[:, cn * C:(cn + 1) * C], ZB[:, 384:512], ACT.Copy).then_inc(y_copied, 1)
                    use += 3
                act.wait_ge(sc_free[0], at(i, 18, use + 1))
                act.wait_ge(sc_free[1], at(i, 18, use + 1))
                nc.scalar.activation(ysq[:], ysb[:], ACT.Square).then_inc(ysq_ready, 1)
                for h in range(2):
                    act.wait_ge(sc_full[h], at(i, 18, use + 2))
                    nc.scalar.activation(kkb[:, h * HALF:(h + 1) * HALF], SC[h][:], ACT.Ln, scale=1.0 / HD,
                                         bias=eps[:, 1:2]).then_inc(sc_free[h], 1)
                act.wait_ge(sc_free[0], at(i, 18, use + 2))
                act.wait_ge(sc_free[1], at(i, 18, use + 2))
                nc.scalar.activation(kkb[:], kkb[:], ACT.Exp, scale=-0.5).then_inc(ynorm_ready, 1)
                own.leave(PAIRS)

        def vector_a(dve, own):
            for h in range(2):
                dve.wait_ge(proj_full[h], 1)
                dve.wait_ge(mix_scaled, h + 1)
                nc.vector.scalar_tensor_tensor(lora[:, h * HALF:(h + 1) * HALF], PJ[h][0:LORA, :], lbp[0:LORA, 0, 0:1],
                                               u[0][0:LORA, h * HALF:(h + 1) * HALF], ALU.mult,
                                               ALU.add).then_inc(proj_free[h], 1)
            with dve.Fori(0, PAIRS) as i:
                own.enter(i, 1 + 2 + 2 + 1 + 7 + 4)
                nc.vector.tensor_scalar(pp[:].rearrange("p (k o) -> p k o", o=1), par[:, :, bass.ds(i, 1)], 1.0, None,
                                        ALU.mult).then_inc(pp_ready, 1)
                dve.wait_ge(small_in, 16 * 5)
                nc.vector.tensor_scalar(lwp[:], lw[:, bass.ds(i * P, P)], 1.0, None, ALU.mult).then_inc(lwp_ready, 1)
                dve.wait_ge(pp_ready, at(i, 1, 1))
                nc.vector.tensor_scalar(rkm[:], ones64, pp[:, RK:RK + 1], None, ALU.mult).then_inc(rkm_ready, 1)
                for q, dst in enumerate((rb, kb, vb, gb)):
                    for h in range(2):
                        dve.wait_ge(proj_full[h], at(i, 4, SLAB_A + q + 1))
                        dve.wait_ge(mix_scaled, at(i, 8, 2 + 2 * q + h + 1))
                        nc.vector.scalar_tensor_tensor(dst[:, h * HALF:(h + 1) * HALF], PJ[h][:],
                                                       pp[:, OMU + q:OMU + q + 1],
                                                       u[q % 2][:, h * HALF:(h + 1) * HALF], ALU.mult,
                                                       ALU.add).then_inc(proj_free[h], 1)
                dve.wait_ge(sc_free[0], at(i, 18, X0 + 2))
                dve.wait_ge(sc_free[1], at(i, 18, X0 + 2))
                own.on(nc.vector.tensor_scalar(ldb[:], ldb[:], -0.5 * DECAY, -0.5 * DECAY, ALU.mult, ALU.add))
                own.wait()
                for h in range(2):
                    own.on(nc.vector.tensor_tensor_scan(gcum[:, h * HALF:(h + 1) * HALF], reset[:],
                                                        ldb[:, h * HALF:(h + 1) * HALF], 0.0, ALU.mult, ALU.add))
                own.wait()
                g3 = gcum[:].rearrange("p (c t) -> p c t", c=NC)
                own.on(nc.vector.tensor_tensor(gc[:, :, 1:C + 1], g3, g3[:, :, 63:64].broadcast_to([P, NC, C]),
                                               ALU.subtract))
                own.on(nc.vector.tensor_scalar(gc[:, :, 0:1], g3[:, :, 63:64], -1.0, None, ALU.mult))
                own.wait()
                nc.vector.tensor_tensor(fac[:, 0, 0:7], gc[:, 0:7, C:C + 1].rearrange("p c o -> p (c o)"),
                                        g3[:, 1:8, 63:64].rearrange("p c o -> p (c o)"), ALU.add).then_inc(gc_ready, 1)
                dve.wait_ge(gc_ready, at(i, 1, 1))
                nc.vector.tensor_scalar(gcum[:], bb[:], pp[:, KAH:KAH + 1], pp[:, OKAH:OKAH + 1], ALU.mult,
                                        ALU.add).then_inc(t_ready, 1)
                for h in range(2):
                    dve.wait_ge(sc_full[h], at(i, 18, X0 + 3))
                    nc.vector.tensor_scalar(kkb[:, h * HALF:(h + 1) * HALF], SC[h][:], 1e-24, None,
                                            ALU.max).then_inc(sc_free[h], 1)
                dve.wait_ge(rn_ready, at(i, 1, 1))
                nc.vector.scalar_tensor_tensor(kkb[:], kb[:], pp[:, KK:KK + 1], kkb[:], ALU.mult,
                                               ALU.mult).then_inc(kk_ready, 1)
                dve.wait_ge(exp_ready, at(i, 3, 3))
                dve.wait_ge(kk_ready, at(i, 1, 1))
                nc.vector.tensor_tensor(ar[:, 0, :].rearrange("p (c t) -> p c t", c=NC),
                                        kkb[:].rearrange("p (c t) -> p c t", c=NC), ee[:, :, 0:C],
                                        ALU.mult).then_inc(ab_ready, 1)
                nc.vector.tensor_tensor(ar[:, 1, :].rearrange("p (c t) -> p c t", c=NC),
                                        rb[:].rearrange("p (c t) -> p c t", c=NC), ee[:, :, 1:C + 1],
                                        ALU.mult).then_inc(ab_ready, 1)
                own.on(nc.vector.scalar_tensor_tensor(bb[:], bb[:], 1.0, kkb[:], ALU.add, ALU.mult))
                own.wait()
                nc.vector.scalar_tensor_tensor(bb[:], bb[:], 0.5, em[:], ALU.mult, ALU.mult).then_inc(ab_ready, 1)
                dve.wait_ge(ab_ready, at(i, 3, 3))
                dve.wait_ge(kq_ready, at(i, 1, 1))
                for h in range(2):
                    dve.wait_ge(sc_full[h], at(i, 18, X0 + 4))
                    nc.vector.tensor_tensor(em[:, h * HALF:(h + 1) * HALF], SC[h][:], vb[:, h * HALF:(h + 1) * HALF],
                                            ALU.mult).then_inc(sc_free[h], 1)
                use = X0 + 4
                nc.vector.memset(st[:], 0.0).then_inc(state_ready, 1)
                for g in range(GROUPS):
                    for un in range(4):
                        h, j = un % 2, un // 2
                        dve.wait_ge(sc_full[h], at(i, 18, use + 2 + j))
                        nc.vector.tensor_tensor(scm[:, un, :], SC[h][:], cst[:, CM:CM + 512], ALU.mult).then_inc(sc_free[h], 1)
                    dve.wait_ge(z_full, at(i, 28, 7 * g + 1))
                    for h, src in enumerate((ZB, SQ)):
                        nc.vector.tensor_tensor(lm[:].rearrange("p (j h t) -> p j h t", j=2, h=2)[:, :, h, :],
                                                src[:, 0:256].rearrange("p (j t) -> p j t", j=2),
                                                wide(cst[:, CL:CL + P], 2), ALU.mult).then_inc(lm_ready, 1)
                    for k in range(LEVELS):
                        if k:
                            dve.wait_ge(z_full, at(i, 28, 7 * g + k + 1))
                            src = ZB[:].rearrange("p (u t) -> p u t", u=4)
                        else:
                            dve.wait_ge(sc_free[0], at(i, 18, use + 3))
                            dve.wait_ge(sc_free[1], at(i, 18, use + 3))
                            src = scm[:, :, 0:P]
                        nc.vector.tensor_tensor(xtm[:].rearrange("p (u t) -> p u t", u=4), src,
                                                wide(cst[:, CN7 + k * P:CN7 + (k + 1) * P], 4),
                                                ALU.mult).then_inc(xt_ready, 1)
                    for j in range(2):
                        cn = 2 * g + j
                        dve.wait_ge(sy_full, at(i, 8, cn + 1))
                        if cn < NC - 1:
                            own.on(nc.vector.scalar_tensor_tensor(st2[:], SQ[:, 256:384], fac[:, 1, cn:cn + 1], ones64,
                                                                  ALU.mult, ALU.mult))
                            own.wait()
                            nc.vector.scalar_tensor_tensor(st[:], st[:], fac[:, 1, cn:cn + 1], st2[:], ALU.mult,
                                                           ALU.add).then_inc(state_ready, 1)
                        else:
                            nc.vector.memset(st2[:], 0.0).then_inc(state_ready, 1)
                    use += 3
                dve.wait_ge(y_copied, at(i, 8, 9))
                for h in range(2):
                    dve.wait_ge(sc_full[h], at(i, 18, use + 1))
                    nc.vector.scalar_tensor_tensor(ysb[:, h * HALF:(h + 1) * HALF], SC[h][:], -1.0 / HD,
                                                   ysb[:, h * HALF:(h + 1) * HALF], ALU.mult,
                                                   ALU.add).then_inc(sc_free[h], 1)
                dve.wait_ge(ynorm_ready, at(i, 1, 1))
                own.on(nc.vector.tensor_tensor(ysb[:], ysb[:], kkb[:], ALU.mult))
                own.wait()
                own.on(nc.vector.tensor_scalar(ysb[:], ysb[:], pp[:, LNW:LNW + 1], pp[:, LNB:LNB + 1], ALU.mult, ALU.add))
                own.wait()
                own.on(nc.vector.tensor_tensor(ysb[:], ysb[:], em[:], ALU.add))
                dve.wait_ge(gate_ready, at(i, 1, 1))
                own.wait()
                own.on(nc.vector.tensor_tensor(yT[:, bass.ds(i, 1), :], ysb[:].rearrange("p (o t) -> p o t", o=1),
                                               gb[:].rearrange("p (o t) -> p o t", o=1), ALU.mult))
                own.leave(PAIRS)

        SB = X0 + 18 * PAIRS
        bias = zT[:, 0:2, :].rearrange("p a (b k) -> p (a b) k", b=4)
        kd = [zT[:, 2 + j, :] for j in range(KV)]
        qb = [zT[:, 4 + n, :] for n in range(4)]
        vch = work[:, 0:T]
        vtm = work[:, T:2 * T].rearrange("p (n c) -> p n c", n=NC)
        ps = work[:, 2 * T:4 * T].rearrange("p (g h k) -> p g h k", g=2, h=4)
        pt = work[:, 4 * T:6 * T].rearrange("p (g h a q) -> p g h a q", g=2, h=4, a=2)
        ob = work[:, 6 * T:6 * T + 512].rearrange("p (g c) -> p g c", g=2)
        GROUPS_B = KV * NC
        sm = soft[:]

        B_SLABS = [("v", 0), ("k", 0), ("q", 0), ("q", 1), ("g", 0), ("g", 1),
                   ("k", 1), ("q", 2), ("q", 3), ("g", 2), ("g", 3)]
        B_FIRST = 6

        def sync_b(sp):
            sp.dma_start(bias[:], bass.AP(scratch.tensor, 127, [[8 * 384 - 1, P], [384, 8], [1, 256]])).then_inc(scr_in, 16)
            for n, (kind, a) in enumerate(B_SLABS):
                s = SLAB_V + n
                if kind == "k":
                    load_slab(sp, s, s % 2, s // 2, columns(w_in0, COL_BK + a * HD, HD))
                    sp.dma_start(w_raw[:, s % 2, :, HD:P], columns(w_in0, COL_BK + a * HD, HD)).then_inc(w_in[s % 2], 16)
                else:
                    load_slab(sp, s, s % 2, s // 2,
                              columns(w_in0, {"v": COL_BV, "q": COL_Q, "g": COL_BG}[kind] + a * P))

        def pool_b(pool, own):
            extra = [0, 0]
            for n, (kind, a) in enumerate(B_SLABS):
                s = SLAB_V + n
                extra[s % 2] += kind == "k"
                split_slab(pool, own, s, s % 2, s // 2 + extra[s % 2])

        def tensor_b(pe):
            for n in range(B_FIRST):
                project(pe, SLAB_V + n, (SLAB_V + n) % 2)
                if n == 0:
                    pe.wait_ge(proj_free[0], SLAB_V + 1)
                    pe.wait_ge(proj_free[1], SLAB_V + 1)
                    for b in range(2):
                        for m in range(4):
                            mm = nc.tensor.transpose(DP[b][:, m * P:(m + 1) * P],
                                                     vch[:, (4 * b + m) * P:(4 * b + m + 1) * P], ident)
                        mm.then_inc(vt_full, 1)

            def scores(grp):
                j, n = grp // NC, grp % NC
                if n == 0:
                    for h in range(2):
                        pe.wait_ge(proj_free[h], SLAB_V + (4 if j == 0 else 9))
                for part in range(2):
                    hp = slice(part * HD, (part + 1) * HD)
                    pe.wait_ge(sc_free[part], SB + grp)
                    for qi in range(2):
                        w = P if n == 0 else 2 * P
                        mm = nc.tensor.matmul(SC[part][:, qi * 256 + 256 - w:qi * 256 + 256],
                                              qb[2 * j + qi][hp, n * P:(n + 1) * P],
                                              kd[j][hp, (n + 1) * P - w:(n + 1) * P], start=True, stop=True)
                    mm.then_inc(sc_full[part], 1)

            def attend(grp):
                j, n = grp // NC, grp % NC
                halves = (1,) if n == 0 else (0, 1)
                pe.wait_ge(p_ready, 4 * (grp + 1))
                if grp == 0:
                    pe.wait_ge(vt_ready, 2)
                for qi in range(2):
                    if grp:
                        pe.wait_ge(pt_copied[qi], grp)
                    for part in range(2):
                        for a in halves:
                            mm = nc.tensor.transpose(DP[qi][:, (2 * part + a) * P:(2 * part + a + 1) * P],
                                                     ps[:, grp % 2, 2 * qi + part, a * P:(a + 1) * P], ident)
                    mm.then_inc(pt_full[qi], 1)
                for qi in range(2):
                    pe.wait_ge(pt_copied[qi], grp + 1)
                    if qi == 0 and grp:
                        pe.wait_ge(o_ready, grp)
                    for part in range(2):
                        h = 2 * qi + part
                        for a in halves:
                            mm = nc.tensor.matmul(SQ[:, h * HD:(h + 1) * HD], pt[:, grp % 2, h, a, :],
                                                  vtm[:, n - 1 + a, j * HD:(j + 1) * HD],
                                                  start=a == halves[0], stop=a == 1)
                mm.then_inc(o_full, 1)

            def turn(grp):
                pe.wait_ge(o_ready, grp + 1)
                if grp:
                    pe.wait_ge(y_out, grp)
                for qi in range(2):
                    mm = nc.tensor.transpose(ZB[:, qi * P:(qi + 1) * P], ob[:, grp % 2, qi * P:(qi + 1) * P], ident)
                mm.then_inc(ot_full, 1)

            for grp in range(GROUPS_B + 2):
                if grp < GROUPS_B:
                    scores(grp)
                if 1 <= grp <= GROUPS_B:
                    attend(grp - 1)
                if grp >= 2:
                    turn(grp - 2)
                if grp < len(B_SLABS) - B_FIRST:
                    s = SLAB_V + B_FIRST + grp
                    project(pe, s, s % 2)

        def scalar_b(act, own):
            def evacuate(n):
                kind, a = B_SLABS[n]
                dst = {"v": [vch], "k": kd, "q": qb, "g": [yT[:, 4 + m, :] for m in range(4)]}[kind][a]
                for h in range(2):
                    act.wait_ge(proj_full[h], SLAB_V + n + 1)
                    nc.scalar.activation(dst[:, h * HALF:(h + 1) * HALF], PJ[h][:],
                                         ACT.Silu if kind == "g" else ACT.Copy,
                                         scale=HD ** -0.5 if kind == "q" else 1.0).then_inc(proj_free[h], 1)

            for n in range(B_FIRST):
                evacuate(n)
                if n == 0:
                    for b in range(2):
                        act.wait_ge(vt_full, b + 1)
                        nc.scalar.activation(vtm[:, 4 * b:4 * b + 4, :], DP[b][:].rearrange("p (n c) -> p n c", n=4),
                                             ACT.Copy).then_inc(vt_ready, 1)

            def probs(grp):
                n = grp % NC
                lo = P if n == 0 else 0
                v = grp % 2
                act.wait_ge(m_ready, 2 * grp + 2)
                if grp >= 2:
                    act.wait_ge(pt_full[1], grp - 1)
                for h in range(4):
                    nc.scalar.activation(ps[:, v, h, lo:], ps[:, v, h, lo:], ACT.Exp, bias=sm[:, v, 4 + h:5 + h],
                                         accum_out=sm[:, v, 12 + h:13 + h]).then_inc(p_ready, 1)
                nc.scalar.activation(sm[:, v, 16:20], sm[:, v, 8:12], ACT.Exp).then_inc(es_ready, 1)

            def copy_p(grp):
                act.wait_ge(pt_full[1], grp + 1)
                if grp >= 2:
                    act.wait_ge(o_full, grp - 1)
                a = 1 if grp % NC == 0 else 0
                nc.scalar.activation(pt[:, grp % 2, 2:4, a:2, :],
                                     DP[1][:].rearrange("p (h a q) -> p h a q", h=2, a=2)[:, :, a:2, :],
                                     ACT.Copy).then_inc(pt_copied[1], 1)

            for grp in range(GROUPS_B + 1):
                if grp < GROUPS_B:
                    probs(grp)
                if grp:
                    copy_p(grp - 1)
                if grp < len(B_SLABS) - B_FIRST:
                    evacuate(B_FIRST + grp)

        def vector_b(dve, own):
            def row_max(grp):
                j, n = grp // NC, grp % NC
                v = grp % 2
                lo = P if n == 0 else 0
                if grp == 0:
                    dve.wait_ge(scr_in, 16)
                    dve.wait_ge(small_in, 16 * 5)
                if grp >= 2:
                    dve.wait_ge(pt_full[1], grp - 1)
                for part in range(2):
                    dve.wait_ge(sc_full[part], SB + grp + 1)
                    for qi in range(2):
                        h = 2 * qi + part
                        ins = nc.vector.tensor_tensor_reduce(
                            ps[:, v, h, lo:], SC[part][:, qi * 256 + lo:qi * 256 + 256], bias[:, 4 * j + h, lo:], 1.0,
                            sinkb[:, 4 * j + h:4 * j + h + 1], ALU.add, ALU.max, sm[:, v, h:h + 1])
                        if qi:
                            ins.then_inc(sc_free[part], 1)
                        else:
                            own.on(ins)
                dve.wait_ge(sc_free[0], SB + grp + 1)
                dve.wait_ge(sc_free[1], SB + grp + 1)
                own.wait()
                nc.vector.tensor_scalar(sm[:, v, 4:8], sm[:, v, 0:4], -1.0, None, ALU.mult).then_inc(m_ready, 1)
                nc.vector.tensor_tensor(sm[:, v, 8:12], sinkb[:, 4 * j:4 * j + 4], sm[:, v, 0:4],
                                        ALU.subtract).then_inc(m_ready, 1)

            def copy_p(grp):
                dve.wait_ge(pt_full[0], grp + 1)
                if grp >= 2:
                    dve.wait_ge(o_full, grp - 1)
                a = 1 if grp % NC == 0 else 0
                nc.vector.tensor_copy(pt[:, grp % 2, 0:2, a:2, :],
                                      DP[0][:].rearrange("p (h a q) -> p h a q", h=2, a=2)[:, :, a:2, :]
                                      ).then_inc(pt_copied[0], 1)
                v = grp % 2
                dve.wait_ge(es_ready, grp + 1)
                dve.wait_ge(p_ready, 4 * grp + 4)
                own.on(nc.vector.tensor_tensor(sm[:, v, 20:24], sm[:, v, 12:16], sm[:, v, 16:20], ALU.add))
                own.wait()
                own.on(nc.vector.reciprocal(sm[:, v, 20:24], sm[:, v, 20:24]))
                own.wait()
                dve.wait_ge(o_full, grp + 1)
                if grp >= 2:
                    dve.wait_ge(ot_full, grp - 1)
                nc.vector.tensor_tensor(ob[:, v, :].rearrange("p (h c) -> p h c", h=4),
                                        SQ[:, 0:256].rearrange("p (h c) -> p h c", h=4),
                                        each(sm[:, v, 20:24], HD), ALU.mult).then_inc(o_ready, 1)

            def gate(grp):
                j, n = grp // NC, grp % NC
                if n == 0:
                    dve.wait_ge(proj_free[1], SLAB_V + (6 if j == 0 else 11))
                    dve.wait_ge(proj_free[0], SLAB_V + (6 if j == 0 else 11))
                dve.wait_ge(ot_full, grp + 1)
                y = yT[:, 4 + 2 * j:6 + 2 * j, n * P:(n + 1) * P]
                nc.vector.tensor_tensor(y, ZB[:, 0:256].rearrange("p (a t) -> p a t", a=2), y, ALU.mult).then_inc(y_out, 1)

            for grp in range(GROUPS_B + 2):
                if grp < GROUPS_B:
                    row_max(grp)
                if 1 <= grp <= GROUPS_B:
                    copy_p(grp - 1)
                if grp >= 2:
                    gate(grp - 2)

        sqb = [work[:, j * T:(j + 1) * T] for j in range(2)]
        rstd = work[:, 8 * T:9 * T]
        SO = [SB + GROUPS_B, SB + GROUPS_B + 2 + 5 * HEADS_C]
        xin = yT

        def sync_o(sp, layer, w_out):
            base = (SLAB_O0, SLAB_O1)[layer]
            with sp.Fori(0, 4) as i:
                for q in range(2):
                    s = base + q
                    load_slab(sp, at(i, 2, s), s % 2, None, columns_at(w_out, q * P, i, 2 * P))
            if layer == 0:
                sp.wait_ge(y_split, 8)
                for t in range(NC):
                    sp.dma_start(xin[:, t, :], x[t * P:(t + 1) * P, :]).then_inc(x_again, 16)

        def pool_o(pool, own, layer):
            base = (SLAB_O0, SLAB_O1)[layer]
            for k in range(KT):
                pool.wait_ge(y_hi, 8 * layer + k + 1)
                nc.gpsimd.tensor_tensor(h_lo[:, k, :], yT[:, k, :], h_hi[:, k, :], ALU.subtract).then_inc(y_split, 1)
            with pool.Fori(0, 4) as i:
                own.enter(i, 2)
                for q in range(2):
                    s = base + q
                    split_slab(pool, own, at(i, 2, s), s % 2, at(i, 1, s // 2 + 1))
                own.leave(4)
            if layer == 0:
                for k in range(KT):
                    pool.wait_ge(h_hi_ready, k + 1)
                    nc.gpsimd.tensor_tensor(h_lo[:, k, :], h_stage[k % 2], h_hi[:, k, :],
                                            ALU.subtract).then_inc(h_lo_ready, 1)

        h_stage = [work[:, (2 + j) * T:(3 + j) * T] for j in range(2)]

        def tensor_norm(pe, n, first):
            for k in range(KT):
                pe.wait_ge(sq_ready, 8 * n + k + 1)
                for h in range(2):
                    if k == 0:
                        pe.wait_ge(sc_free[h], first)
                    mm = nc.tensor.matmul(SC[h][:], ones_all[:], sqb[k % 2][:, h * HALF:(h + 1) * HALF],
                                          start=k == 0, stop=k == KT - 1)
                    if k == KT - 1:
                        mm.then_inc(sc_full[h], 1)
                    elif h:
                        mm.then_inc(sq_used, 1)

        def scalar_norm(act, own, n, first, src, ready):
            for k in range(KT):
                for s in ready:
                    act.wait_ge(s, k + 1)
                if k >= 2:
                    act.wait_ge(sq_used, 7 * n + k - 1)
                nc.scalar.activation(sqb[k % 2], src(k), ACT.Square).then_inc(sq_ready, 1)
            for h in range(2):
                act.wait_ge(sc_full[h], first + 1)
                nc.scalar.activation(rstd[:, h * HALF:(h + 1) * HALF], SC[h][:], ACT.Ln, scale=1.0 / D,
                                     bias=eps[:, 0:1]).then_inc(sc_free[h], 1)
            act.wait_ge(sc_free[0], first + 1)
            act.wait_ge(sc_free[1], first + 1)
            nc.scalar.activation(rstd[:], rstd[:], ACT.Exp, scale=-0.5).then_inc(norm_ready, 1)

        def tensor_o(pe, layer):
            base = (SLAB_O0, SLAB_O1)[layer]
            pe.wait_ge(y_split, 8 * layer + 8)
            with pe.Fori(0, 4) as i:
                for q in range(2):
                    project(pe, at(i, 2, base + q), (base + q) % 2)
            tensor_norm(pe, 2 * layer, SO[layer])
            if layer == 0:
                for t in range(NC):
                    if t == 0:
                        pe.wait_ge(x_again, 16 * NC)
                for k in range(KT):
                    for h in range(2):
                        if k:
                            pe.wait_ge(xt_added[h], k)
                        for m in range(4):
                            mm = nc.tensor.transpose(DP[h][:, m * P:(m + 1) * P],
                                                     xin[:, 4 * h + m, k * P:(k + 1) * P], ident)
                        mm.then_inc(xt_full[h], 1)
                tensor_norm(pe, 1, SO[0] + 1)
            else:
                for t in range(NC):
                    for h in range(2):
                        if t:
                            pe.wait_ge(out_copied[h], t)
                        for m in range(4):
                            k = 4 * h + m
                            if t == 0:
                                pe.wait_ge(final_ready, k + 1)
                            mm = nc.tensor.transpose(DP[h][:, m * P:(m + 1) * P], yT[:, k, t * P:(t + 1) * P], ident)
                        mm.then_inc(out_full[h], 1)

        def scalar_o(act, own, layer):
            for k in range(KT):
                nc.scalar.activation(h_hi[:, k, :], yT[:, k, :], ACT.Copy).then_inc(y_hi, 1)
            base = (SLAB_O0, SLAB_O1)[layer]
            z = (zT, yT)[layer]
            act.wait_ge(proj_free[0], base + 8)
            act.wait_ge(proj_free[1], base + 8)
            scalar_norm(act, own, 2 * layer, SO[layer], lambda k: z[:, k, :], ())
            if layer == 0:
                scalar_norm(act, own, 1, SO[0] + 1, lambda k: zT[:, k, :], xt_added)
                for k in range(KT):
                    act.wait_ge(h_ready, k + 1)
                    nc.scalar.activation(h_hi[:, k, :], h_stage[k % 2], ACT.Copy).then_inc(h_hi_ready, 1)
            else:
                for t in range(NC):
                    act.wait_ge(out_full[1], t + 1)
                    if t >= 2:
                        act.wait_ge(out_done[t % 2], 16 * (t // 2))
                    nc.scalar.activation(out_stage[t % 2][:, HALF:T], DP[1][:], ACT.Copy).then_inc(out_copied[1], 1)

        def vector_o(dve, own, layer):
            base = (SLAB_O0, SLAB_O1)[layer]
            z = (zT, yT)[layer]
            if layer == 1:
                dve.wait_ge(y_split, 16)
            with dve.Fori(0, 4) as i:
                for q in range(2):
                    for h in range(2):
                        dve.wait_ge(proj_full[h], at(i, 2, base + q + 1))
                        nc.vector.tensor_scalar(z[:, bass.ds(i * 2 + q, 1), h * HALF:(h + 1) * HALF],
                                                PJ[h][:].rearrange("p (o t) -> p o t", o=1), 1.0, None,
                                                ALU.mult).then_inc(proj_free[h], 1)
            post = (POST0, POST1)[layer] - 44
            dve.wait_ge(norm_ready, 2 * layer + 1)
            for k in range(KT):
                own.on(nc.vector.scalar_tensor_tensor(z[:, k, :], z[:, k, :], oth[:, post + k:post + k + 1], rstd,
                                                      ALU.mult, ALU.mult))
                own.wait()
                if layer == 0:
                    for h in range(2):
                        dve.wait_ge(xt_full[h], k + 1)
                        nc.vector.tensor_tensor(z[:, k, h * HALF:(h + 1) * HALF], z[:, k, h * HALF:(h + 1) * HALF],
                                                DP[h][:], ALU.add).then_inc(xt_added[h], 1)
                else:
                    nc.vector.tensor_tensor(z[:, k, :], z[:, k, :], zT[:, k, :], ALU.add).then_inc(final_ready, 1)
            if layer == 0:
                dve.wait_ge(norm_ready, 2)
                for k in range(KT):
                    if k >= 2:
                        dve.wait_ge(h_lo_ready, k - 1)
                    nc.vector.scalar_tensor_tensor(h_stage[k % 2], zT[:, k, :], oth[:, PRE1 - 44 + k:PRE1 - 43 + k], rstd,
                                                   ALU.mult, ALU.mult).then_inc(h_ready, 1)
            else:
                for t in range(NC):
                    dve.wait_ge(out_full[0], t + 1)
                    if t >= 2:
                        dve.wait_ge(out_done[t % 2], 16 * (t // 2))
                    nc.vector.tensor_copy(out_stage[t % 2][:, 0:HALF], DP[0][:]).then_inc(out_copied[0], 1)

        out_stage = [work[:, (4 + j) * T:(5 + j) * T] for j in range(2)]

        def sync_out(sp):
            for t in range(NC):
                sp.wait_ge(out_copied[0], t + 1)
                sp.wait_ge(out_copied[1], t + 1)
                sp.dma_start(out[t * P:(t + 1) * P, :], out_stage[t % 2]).then_inc(out_done[t % 2], 16)
            sp.wait_ge(out_done[0], 16 * NC // 2)
            sp.wait_ge(out_done[1], 16 * NC // 2)

        def cb(n):
            return work[:, n * T:(n + 1) * T]
        qs, vc, og, fc, ec, sp_, gcm, oc = (cb(n) for n in range(8))
        tail = work[:, 8 * T:9 * T]
        tmc = tail[:, 0:512].rearrange("p (j n) -> p j n", j=2)
        stc = tail[:, 512:768].rearrange("p (j n) -> p j n", j=2)
        sc1, sc2 = tail[:, 768:896], tail[:, 896:1024]
        CQ, CG, CF, CV = 0, 3 * D, D, 2 * D
        INC = [SQ, DP[0]]
        SCC = SO[0] + 2

        def sync_c(sp):
            with sp.Fori(0, HEADS_C) as i:
                for q, col in enumerate((CQ, CG, CF, CV)):
                    load_slab(sp, at(i, 4, SLAB_C + q), q % 2, None, columns_at(w_in1, col, i, P))

        def pool_c(pool, own):
            with pool.Fori(0, HEADS_C) as i:
                own.enter(i, 4)
                for q in range(4):
                    split_slab(pool, own, at(i, 4, SLAB_C + q), q % 2, at(i, 2, (SLAB_C + q) // 2 + 1))
                own.leave(HEADS_C)

        def tensor_c(pe):
            with pe.Fori(0, HEADS_C) as i:
                for q in range(4):
                    project(pe, at(i, 4, SLAB_C + q), q % 2)
                pe.wait_ge(kc_ready, at(i, 1, 1))
                pe.wait_ge(qc_ready, at(i, 1, 1))
                pe.wait_ge(proj_free[0], at(i, 4, SLAB_C + 4))
                pe.wait_ge(proj_free[1], at(i, 4, SLAB_C + 4))

                def turn(c):
                    cs = slice(c * C, (c + 1) * C)
                    j = c % 2
                    pe.wait_ge(sc_free[j], at(i, 5, SCC + c // 2))
                    nc.tensor.transpose(SC[j][:, 0:P], vc[:, cs], ident)
                    nc.tensor.transpose(SC[j][:, P:2 * P], fc[:, cs], ident)
                    nc.tensor.matmul(SC[j][0:64, 256:384], fc[:, c * C:c * C + 64], qs[:, cs], start=True, stop=True)
                    nc.tensor.matmul(SC[j][64:128, 320:384], fc[:, c * C + 64:(c + 1) * C],
                                     qs[:, c * C + 64:(c + 1) * C], start=True, stop=True).then_inc(sc_full[j], 1)

                turn(0)
                for c in range(NC):
                    cs = slice(c * C, (c + 1) * C)
                    j = c % 2
                    if c + 1 < NC:
                        turn(c + 1)
                    pe.wait_ge(tc_ready, at(i, NC, c + 1))
                    pe.wait_ge(sc_free[j], at(i, 5, SCC + c // 2 + 1))
                    nc.tensor.matmul(INC[j][:, 0:P], tmc[:, j, P:2 * P], tmc[:, j, 0:P], start=True,
                                     stop=True).then_inc(inc_full, 1)
                    pe.wait_ge(oc_copied, at(i, NC, c + 1))
                    pe.wait_ge(sc_state, at(i, NC, c + 1))
                    nc.tensor.matmul(ZB[:, 0:P], tmc[:, j, 0:P], stc[:, j, :], start=True, stop=False)
                    nc.tensor.matmul(ZB[:, 0:P], sc1, qs[:, cs], start=False, stop=True).then_inc(oc_full, 1)
                pe.wait_ge(osq_ready, at(i, 1, 1))
                for h in range(2):
                    pe.wait_ge(sc_free[h], at(i, 5, SCC + 4))
                    nc.tensor.matmul(SC[h][:], ones_all[:], sp_[:, h * HALF:(h + 1) * HALF], start=True,
                                     stop=True).then_inc(sc_full[h], 1)

        def scalar_c(act, own):
            nc.scalar.activation(eps[:, 3:4], eps[:, 3:4], ACT.Copy).then_inc(oc_copied, 1)
            act.wait_ge(lb_step, 2)
            nc.scalar.activation(lbp[:, 2:4, :], lbp[:, 2:4, :], ACT.Exp).then_inc(lb_exp, 1)
            act.wait_ge(lb_step, 3)
            nc.scalar.activation(lbp[:, 5, :], lbp[:, 5, :], ACT.Ln).then_inc(lb_exp, 1)
            with act.Fori(0, HEADS_C) as i:
                own.enter(i, 1)
                act.wait_ge(head_done, at(i, 1, 1))
                for q, dst in enumerate((qs, og)):
                    for h in range(2):
                        act.wait_ge(proj_full[h], at(i, 4, SLAB_C + q + 1))
                        nc.scalar.activation(dst[:, h * HALF:(h + 1) * HALF], PJ[h][:], ACT.Silu).then_inc(proj_free[h], 1)
                act.wait_ge(proj_free[0], at(i, 4, SLAB_C + 3))
                act.wait_ge(proj_free[1], at(i, 4, SLAB_C + 3))
                act.wait_ge(lb_ready, at(i, 1, 1))
                own.on(nc.scalar.activation(ec, fc, ACT.Exp, scale=-1.0))
                own.wait()
                nc.scalar.activation(sp_, ec, ACT.Ln, bias=1.0).then_inc(ln_ready, 1)
                nc.scalar.activation(ec, ec, ACT.Ln, bias=1.0, scale=lbc[:, 0:1]).then_inc(ln_ready, 1)
                act.wait_ge(gcc_ready, at(i, 2, 1))
                nc.scalar.activation(gcm, ec, ACT.Exp).then_inc(expc_ready, 1)
                nc.scalar.activation(fac[:, 1, 0:7], fac[:, 0, 0:7], ACT.Exp).then_inc(expc_ready, 1)
                act.wait_ge(gcc_ready, at(i, 2, 2))
                nc.scalar.activation(fc, fc, ACT.Exp, scale=-1.0, bias=lbc[:, 1:2]).then_inc(kc_ready, 1)
                for c in range(NC):
                    j = c % 2
                    act.wait_ge(sc_full[j], at(i, 5, SCC + c // 2 + 1))
                    nc.scalar.activation(tmc[:, j, :], SC[j][:, 0:256], ACT.Copy).then_inc(tc_ready, 1)
                    act.wait_ge(oc_full, at(i, NC, c + 1))
                    nc.scalar.activation(oc[:, c * C:(c + 1) * C], ZB[:, 0:P], ACT.Copy).then_inc(oc_copied, 1)
                act.wait_ge(oc_copied, at(i, NC, NC + 1))
                nc.scalar.activation(sp_, oc, ACT.Square).then_inc(osq_ready, 1)
                for h in range(2):
                    act.wait_ge(sc_full[h], at(i, 5, SCC + 5))
                    nc.scalar.activation(ec[:, h * HALF:(h + 1) * HALF], SC[h][:], ACT.Ln, scale=1.0 / C,
                                         bias=eps[:, 0:1]).then_inc(sc_free[h], 1)
                act.wait_ge(sc_free[0], at(i, 5, SCC + 5))
                act.wait_ge(sc_free[1], at(i, 5, SCC + 5))
                nc.scalar.activation(ec, ec, ACT.Exp, scale=-0.5).then_inc(orn_ready, 1)
                own.leave(HEADS_C)

        def vector_c(dve, own):
            lb0, lb1 = oth[:, LB0 - 44:LB0 - 36], oth[:, LB1 - 44:LB1 - 36]
            own.on(nc.vector.tensor_tensor(lbp[:, 1, :], lb0, lb1, ALU.max))
            own.wait()
            nc.vector.tensor_tensor(lbp[:, 2, :], lb0, lbp[:, 1, :], ALU.subtract).then_inc(lb_step, 1)
            nc.vector.tensor_tensor(lbp[:, 3, :], lb1, lbp[:, 1, :], ALU.subtract).then_inc(lb_step, 1)
            dve.wait_ge(lb_exp, 1)
            own.on(nc.vector.tensor_tensor(lbp[:, 1, :], lbp[:, 2, :], lbp[:, 3, :], ALU.add))
            own.wait()
            own.on(nc.vector.reciprocal(lbp[:, 1, :], lbp[:, 1, :]))
            own.wait()
            own.on(nc.vector.tensor_tensor(lbp[:, 4, :], lbp[:, 3, :], lbp[:, 1, :], ALU.mult))
            nc.vector.tensor_tensor(lbp[:, 5, :], lbp[:, 2, :], lbp[:, 1, :], ALU.mult).then_inc(lb_step, 1)
            own.on(nc.vector.memset(stc[:], 0.0))
            nc.vector.memset(sc2, 0.0).then_inc(head_done, 1)
            own.on(nc.vector.memset(reset_c[:], 1.0))
            own.wait()
            own.on(nc.vector.memset(reset_c[:].rearrange("p (c t) -> p c t", t=C)[:, :, 0:1], 0.0))
            own.wait()
            dve.wait_ge(lb_exp, 2)
            with dve.Fori(0, HEADS_C) as i:
                own.enter(i, 5 + 15 + 1)
                nc.vector.tensor_scalar(lbc[:, 0:2].rearrange("p (k o) -> p k o", o=1), lbp[:, 4:6, bass.ds(i, 1)], 1.0,
                                        None, ALU.mult).then_inc(lb_ready, 1)
                for h in range(2):
                    dve.wait_ge(proj_full[h], at(i, 4, SLAB_C + 3))
                    nc.vector.tensor_scalar(fc[:, h * HALF:(h + 1) * HALF], PJ[h][:], -43.0, None,
                                            ALU.max).then_inc(proj_free[h], 1)
                for h in range(2):
                    dve.wait_ge(proj_full[h], at(i, 4, SLAB_C + 4))
                    nc.vector.tensor_scalar(vc[:, h * HALF:(h + 1) * HALF], PJ[h][:], 1.0, None,
                                            ALU.mult).then_inc(proj_free[h], 1)
                dve.wait_ge(ln_ready, at(i, 2, 2))
                own.on(nc.vector.tensor_tensor(ec, ec, sp_, ALU.subtract))
                own.on(nc.vector.tensor_tensor(fc, fc, sp_, ALU.add))
                own.wait()
                for h in range(2):
                    own.on(nc.vector.tensor_tensor_scan(gcm[:, h * HALF:(h + 1) * HALF], reset_c[:],
                                                        ec[:, h * HALF:(h + 1) * HALF], 0.0, ALU.mult, ALU.add))
                own.wait()
                g3 = gcm.rearrange("p (c t) -> p c t", c=NC)
                e3 = ec.rearrange("p (c t) -> p c t", c=NC)
                own.on(nc.vector.tensor_tensor(e3, g3, g3[:, :, 63:64].broadcast_to([P, NC, C]), ALU.subtract))
                own.wait()
                nc.vector.tensor_tensor(fac[:, 0, 0:7], e3[:, 0:7, C - 1:C].rearrange("p c o -> p (c o)"),
                                        g3[:, 1:8, 63:64].rearrange("p c o -> p (c o)"), ALU.add).then_inc(gcc_ready, 1)
                nc.vector.tensor_tensor(fc, fc, ec, ALU.add).then_inc(gcc_ready, 1)
                dve.wait_ge(expc_ready, at(i, 2, 1))
                nc.vector.tensor_tensor(qs, qs, gcm, ALU.mult).then_inc(qc_ready, 1)
                nc.vector.memset(sc1, 0.0).then_inc(sc_state, 1)
                for c in range(NC):
                    j = c % 2
                    dve.wait_ge(sc_full[j], at(i, 5, SCC + c // 2 + 1))
                    dve.wait_ge(tc_ready, at(i, NC, c + 1))
                    own.on(nc.vector.tensor_tensor(stc[0:64, j, :], SC[j][0:64, 256:384], cst[0:64, CM + P:CM + 2 * P],
                                                   ALU.mult))
                    nc.vector.tensor_tensor(stc[64:128, j, 64:128], SC[j][64:128, 320:384],
                                            cst[64:128, CM + P + 64:CM + 2 * P], ALU.mult).then_inc(sc_free[j], 1)
                    if c < NC - 1:
                        dve.wait_ge(inc_full, at(i, NC, c + 1))
                        dve.wait_ge(sc_state, at(i, NC, c + 1))
                        own.on(nc.vector.tensor_tensor(sc2, sc1, INC[j][:, 0:P], ALU.add))
                        own.wait()
                        dve.wait_ge(oc_full, at(i, NC, c + 1))
                        nc.vector.tensor_scalar(sc1, sc2, fac[:, 1, c:c + 1], None, ALU.mult).then_inc(sc_state, 1)
                dve.wait_ge(orn_ready, at(i, 1, 1))
                own.on(nc.vector.scalar_tensor_tensor(oc, oc, oth[:, CN - 44:CN - 43], ec, ALU.mult, ALU.mult))
                own.wait()
                nc.vector.tensor_tensor(yT[:, bass.ds(i, 1), :], oc.rearrange("p (o t) -> p o t", o=1),
                                        og.rearrange("p (o t) -> p o t", o=1), ALU.mult).then_inc(head_done, 1)
                own.leave(HEADS_C)

        block = ctx.enter_context(nc.Block())

        @block.sync
        def _(sp):
            sync_0(sp)
            phase_end(sp, 0)
            sync_a(sp)
            phase_end(sp, 1)
            sync_b(sp)
            phase_end(sp, 2)
            sync_o(sp, 0, w_out0)
            phase_end(sp, 3)
            sync_c(sp)
            phase_end(sp, 4)
            sync_o(sp, 1, w_out1)
            sync_out(sp)

        @block.gpsimd
        def _(pool):
            own = Steps(pool, own_pool)
            pool_0(pool, own)
            phase_end(pool, 0)
            pool_a(pool, own)
            phase_end(pool, 1)
            pool_b(pool, own)
            phase_end(pool, 2)
            pool_o(pool, own, 0)
            phase_end(pool, 3)
            pool_c(pool, own)
            phase_end(pool, 4)
            pool_o(pool, own, 1)

        @block.tensor
        def _(pe):
            tensor_0(pe)
            phase_end(pe, 0)
            tensor_a(pe)
            phase_end(pe, 1)
            tensor_b(pe)
            phase_end(pe, 2)
            tensor_o(pe, 0)
            phase_end(pe, 3)
            tensor_c(pe)
            phase_end(pe, 4)
            tensor_o(pe, 1)

        @block.scalar
        def _(act):
            own = Steps(act, own_act)
            scalar_0(act, own)
            phase_end(act, 0)
            scalar_a(act, own)
            phase_end(act, 1)
            scalar_b(act, own)
            phase_end(act, 2)
            scalar_o(act, own, 0)
            phase_end(act, 3)
            scalar_c(act, own)
            phase_end(act, 4)
            scalar_o(act, own, 1)

        @block.vector
        def _(dve):
            own = Steps(dve, own_dve)
            vector_0(dve, own)
            phase_end(dve, 0)
            vector_a(dve, own)
            phase_end(dve, 1)
            vector_b(dve, own)
            phase_end(dve, 2)
            vector_o(dve, own, 0)
            phase_end(dve, 3)
            vector_c(dve, own)
            phase_end(dve, 4)
            vector_o(dve, own, 1)


_INS = ["x", "rel_bias_table", "lower_bounds", "l0_pre_norm", "l0_post_norm", "l0_w_in", "l0_w_out",
        "a_mu", "a_w0", "a_w2", "a_a0", "a_a2", "a_k_k", "a_k_a", "a_r_k", "a_ln_w", "a_ln_b", "b_sinks",
        "l1_pre_norm", "l1_post_norm", "l1_w_in", "l1_w_out", "c_norm_w"]


def kernel(**inputs):
    import concourse.bacc as bacc
    from concourse.bass_utils import run_bass_kernel_spmd

    nc = bacc.Bacc("TRN2", target_bir_lowering=False, num_devices=1)
    arrays = {name: np.ascontiguousarray(inputs[name]) for name in _INS}
    arrays["x"] = arrays["x"].reshape(T, D)
    arrays["constants"] = constants()
    arrays["buckets"] = bucket_table()
    args = [nc.dram_tensor(f"in_{name}", a.shape, F32, kind="ExternalInput").ap() for name, a in arrays.items()]
    args.append(nc.dram_tensor("bias_rows", (P, 8, 384), F32).ap())
    out = nc.dram_tensor("out_0", (T, D), F32, kind="ExternalOutput").ap()
    trunk(nc, *args, out)
    r = run_bass_kernel_spmd(nc, [{f"in_{name}": a for name, a in arrays.items()}], core_ids=[0])
    return r.results[0]["out_0"].reshape(1, T, D)
```

```python
from contextlib import ExitStack

import numpy as np

import concourse.bass as bass
from concourse import mybir

ALU = mybir.AluOpType
ACT = mybir.ActivationFunctionType
AX = mybir.AxisListType
F32 = mybir.dt.float32
F32R = mybir.dt.float32r

P = 128
D = 1024
T = 1024
KT = D // P
HALF = 512
C = 128
NC = T // C
HD = 64
PAIRS = 4
LEVELS = 7
LORA = 64
NORM_EPS = 1e-6
GN_EPS = 64e-5
DECAY = float(np.exp(-0.5))
BUCKETS = 32
A_COLS = 2112
COL_R, COL_K, COL_V, COL_LORA, COL_AG = 0, 512, 1024, 1536, 1600
COL_Q, COL_BK, COL_BV, COL_BG = A_COLS, A_COLS + 512, A_COLS + 640, A_COLS + 768
KV = 2
HEADS_C = 8
NEG = -1e30

SLAB_LORA = 0
SLAB_A = 1
SLAB_V = SLAB_A + 4 * PAIRS
SLAB_B = SLAB_V + 1
SLAB_O0 = SLAB_B + 5 * KV
SLAB_C = SLAB_O0 + 8
SLAB_O1 = SLAB_C + 4 * HEADS_C
SLABS = SLAB_O1 + 8

RAW_KINDS = 11
MU, W0, A0, KK, KA, RK, LNW, LNB = 0, 4, 5, 6, 7, 8, 9, 10
OMU, W0H, A0H, KAH, OKAH = 11, 15, 16, 17, 18
KINDS = 19
PRE0, POST0, PRE1, POST1, LB0, LB1, CN, MUL = 44, 52, 60, 68, 76, 84, 92, 93
ROWS = 94

CI, CO64, CM, CL, CN7 = 0, 128, 256, 768, 896
CONSTS = CN7 + 128 * LEVELS


def constants():
    s = np.arange(P)[:, None]
    t = np.arange(P)[None, :]
    c = np.zeros((P, CONSTS), np.float32)
    c[:, CI:CI + P] = s == t
    c[:, CO64:CO64 + P] = s // HD == t // HD
    for q in range(4):
        c[:, CM + P * q:CM + P * (q + 1)] = (s < t) if q % 2 == 0 else (s <= t)
    c[:, CL:CL + P] = s > t
    for k in range(LEVELS):
        b = 1 << k
        m = (s // (2 * b) == t // (2 * b)) & ((s // b) % 2 == 0) & ((t // b) % 2 == 1)
        c[:, CN7 + P * k:CN7 + P * (k + 1)] = -1.0 * m
    return c


def bucket_table():
    c = np.zeros((BUCKETS, 768), np.float32)
    half = BUCKETS // 2
    c[:, 384:768] = NEG
    for m in range(128, 256):
        dist = 255 - m
        far = half + int(np.log(np.float32(max(dist, 1)) / half) / np.log(128 / half) * half)
        c[dist if dist < half else min(far, BUCKETS - 1), m] = 1.0
        c[:, 384 + m] = 0.0
    return c


class Steps:

    def __init__(self, eng, sem):
        self.eng, self.sem, self.n, self.i, self.per, self.start = eng, sem, 0, None, 0, 0

    def on(self, ins):
        ins.then_inc(self.sem, 1)
        self.n += 1

    def wait(self):
        self.eng.wait_ge(self.sem, self.n if self.i is None else self.i * self.per + self.n)

    def enter(self, i, per):
        self.i, self.per, self.start = i, per, self.n

    def leave(self, times):
        assert self.n - self.start == self.per, (self.n - self.start, self.per)
        self.n, self.i = self.start + self.per * times, None


def trunk(nc, x, table, lbs, pre0, post0, w_in0, w_out0, mu, w0, w2, a0, a2, k_k, k_a, r_k, ln_w,
          ln_b, sinks, pre1, post1, w_in1, w_out1, c_norm, cst_in, buckets, scratch, stream, out):
    with ExitStack() as ctx:
        def sb(name, shape, dt=F32):
            return ctx.enter_context(nc.sbuf_tensor(name, shape, dt))

        def sem(name):
            return ctx.enter_context(nc.semaphore(name))

        bank = [ctx.enter_context(nc.psum_tensor(f"bank{i}", [P, HALF], F32)) for i in range(8)]
        PJ, SC, ZB, DP, SQ = bank[0:2], bank[2:4], bank[4], bank[5:7], bank[7]

        h_hi = sb("h_hi", [P, KT, T], F32R)
        h_lo = sb("h_lo", [P, KT, T], F32R)
        yT = sb("yT", [P, KT, T])
        zT = sb("zT", [P, KT, T])
        w_raw = sb("w_raw", [P, 2, KT, P])
        w_hi = sb("w_hi", [P, 2, KT, P], F32R)
        w_lo = sb("w_lo", [P, 2, KT, P], F32R)
        cst = sb("cst", [P, CONSTS])
        work = sb("work", [P, 8488])
        par_raw = work[0:ROWS, 128:256]
        par = sb("par", [P, KINDS, 4])
        oth = sb("oth", [P, ROWS - 44])
        lbp = sb("lbp", [P, 6, 8])
        pp = sb("pp", [P, KINDS])
        rms = sb("rms", [P, 16])
        lw = sb("lw", [LORA, HALF])
        lwp = sb("lwp", [LORA, P])
        rkm = sb("rkm", [P, P])
        eps = sb("eps", [P, 4])
        fac = sb("fac", [P, 2, 16])
        xr = sb("xr", [P, HALF], F32R)
        dpr = sb("dpr", [P, 2 * HALF], F32R)
        lmr = sb("lmr", [P, HALF], F32R)
        ident_r = sb("ident_r", [P, P], F32R)
        pn = sb("pn", [P, KINDS])
        sinkb = sb("sinkb", [P, 8])
        tb = sb("tb", [BUCKETS, 8])
        soft = sb("soft", [P, 2, 24])
        lbc = sb("lbc", [P, 2])
        ones_all = sb("ones_all", [P, P])
        reset = sb("reset", [P, HALF])
        ident = cst[:, CI:CI + P]
        ones64 = cst[:, CO64:CO64 + P]

        own_act, own_dve, own_pool = (sem(f"own_{e}") for e in ("act", "dve", "pool"))
        phase_done = sem("phase_done")
        par_zeroed, const_in, par_in, small_in = (sem(n) for n in ("par_zeroed", "const_in", "par_in", "small_in"))
        x_in = [sem(f"x_in{i}") for i in range(2)]
        w_in = [sem(f"weights_in{i}") for i in range(2)]
        w_split = sem("weights_split")
        proj_full = [sem(f"proj_full{i}") for i in range(2)]
        proj_free = [sem(f"proj_free{i}") for i in range(2)]
        sc_full = [sem(f"sc_full{i}") for i in range(2)]
        sc_free = [sem(f"sc_free{i}") for i in range(2)]
        par_full, bias_full, bias_row, scr_in, scr_out = (
            sem(n) for n in ("par_full", "bias_full", "bias_row", "scr_in", "scr_out"))
        par_ready, eps_ready = sem("par_ready"), sem("eps_ready")
        rstd_ready, xn_ready, hi_ready, lo_ready = (sem(n) for n in ("rstd_ready", "xn_ready", "hi_ready", "lo_ready"))
        pp_ready, lwp_ready, rkm_ready, mix_scaled, lora_ready, gate_ready = (
            sem(n) for n in ("pp_ready", "lwp_ready", "rkm_ready", "mix_scaled", "lora_ready", "gate_ready"))
        ksq_ready, gc_ready, exp_ready, rn_ready, kk_ready, t_ready, kp_ready, kq_ready, rk_ready, ab_ready = (
            sem(n) for n in ("ksq_ready", "gc_ready", "exp_ready", "rn_ready", "kk_ready", "t_ready",
                             "kp_ready", "kq_ready", "rk_ready", "ab_ready"))
        z_full, lm_ready, xt_ready = sem("z_full"), sem("lm_ready"), sem("xt_ready")
        dp_full = [sem(f"dp_full{i}") for i in range(2)]
        dp_copied = sem("dp_copied")
        rhs_full, nr_ready, sa_full, sa_ready, sy_full, state_ready, y_copied = (
            sem(n) for n in ("rhs_full", "nr_ready", "sa_full", "sa_ready", "sy_full", "state_ready", "y_copied"))
        vt_full, vt_ready, m_ready, p_ready, es_ready, o_full, o_ready, ot_full, y_out = (
            sem(n) for n in ("vt_full", "vt_ready", "m_ready", "p_ready", "es_ready", "o_full", "o_ready", "ot_full", "y_out"))
        pt_full = [sem(f"pt_full{i}") for i in range(2)]
        pt_copied = [sem(f"pt_copied{i}") for i in range(2)]
        y_hi, y_split, x_again, h_ready, h_hi_ready, h_lo_ready, sq_ready, sq_used, norm_ready, final_ready = (
            sem(n) for n in ("y_hi", "y_split", "x_again", "h_ready", "h_hi_ready", "h_lo_ready", "sq_ready",
                             "sq_used", "norm_ready", "final_ready"))
        xt_full, xt_added, out_full, out_copied, out_done = (
            [sem(f"{n}{i}") for i in range(2)] for n in ("xt_full", "xt_added", "out_full", "out_copied", "out_done"))
        lb_step, lb_exp, lb_ready, ln_ready, gcc_ready, expc_ready, kc_ready, qc_ready = (
            sem(n) for n in ("lb_step", "lb_exp", "lb_ready", "ln_ready", "gcc_ready", "expc_ready", "kc_ready", "qc_ready"))
        inc_full = [sem(f"inc_full{i}") for i in range(2)]
        tc_ready, oc_full, oc_copied, sc_state, osq_ready, orn_ready = (
            sem(n) for n in ("tc_ready", "oc_full", "oc_copied", "sc_state", "osq_ready", "orn_ready"))
        head_done = sem("head_done")
        norm_full, norm_free, gate_c_ready, stream_out, stream_in = (
            sem(n) for n in ("norm_full", "norm_free", "gate_c_ready", "stream_out", "stream_in"))
        ysq_ready, ynorm_ready = sem("ysq_ready"), sem("ynorm_ready")
        pn_ready, lmr_ready, corr_full, pf_ready, ident_ready = (
            sem(n) for n in ("pn_ready", "lmr_ready", "corr_full", "pf_ready", "ident_ready"))

        def phase_end(eng, k):
            eng.drain().then_inc(phase_done, 1)
            eng.wait_ge(phase_done, 5 * (k + 1))

        xt = [zT[:, j, :] for j in range(2)]
        xn = [zT[:, 2 + j, :] for j in range(2)]
        hf = [zT[:, 4 + j, :].rearrange("p (k t) -> p k t", k=KT) for j in range(2)]
        bk = zT[0:BUCKETS, 6, 0:768]
        brow = zT[0:8, 7, 0:384]
        stage = yT[:, 4:8, :]
        rs, ks, vs, gs = (yT[:, 4 + n, :] for n in range(4))
        lora = yT[0:LORA, 3, :]
        scm = [zT[:, 0:2, :].rearrange("p a (b t) -> p (a b) t", b=2),
               work[:, 1032:1032 + 4 * HALF].rearrange("p (b t) -> p b t", b=4)]
        vtm_a = zT[:, 2, :].rearrange("p (n c) -> p n c", n=NC)
        gb, bb, kt = (zT[:, n, :] for n in (3, 4, 7))
        ar = zT[:, 5:7, :]
        u = work[:, 0:T + 1]
        gc = work[:, 1032:2064].rearrange("p (c t) -> p c t", c=NC)
        ysq = work[:, 1032:1032 + T]
        kkb = work[:, 2064:2064 + T]
        ee = work[:, 3096:4128].rearrange("p (c t) -> p c t", c=NC)
        ysb = work[:, 3096:3096 + T]
        ldb, gcum, em = (work[:, 4128 + n * T:4128 + (n + 1) * T] for n in range(3))
        tmb = [ldb[:, n * HALF:(n + 1) * HALF].rearrange("p (j t) -> p j t", j=2) for n in range(2)]
        pf = gcum.rearrange("p (g t) -> p g t", g=2)
        rest = work[:, 4128 + 3 * T:]
        nr = rest[:, 0:256].rearrange("p (j n) -> p j n", j=2)
        sa = rest[:, 256:512].rearrange("p (j n) -> p j n", j=2)
        st, st2 = rest[:, 512:640], rest[:, 640:768]
        lm = rest[:, 768:1280]

        def dpt(un):
            d0 = un // 2 * HALF + un % 2 * 256
            return dpr[:, d0:d0 + P], dpr[:, d0 + P:d0 + 2 * P]

        def load_slab(sp, s, slot, src):
            if not (isinstance(s, int) and s < 2):
                sp.wait_ge(w_split, s - 1)
            sp.dma_start(w_raw[:, slot, :, 0:src.shape[-1]], src).then_inc(w_in[slot], 16)

        def split_slab(pool, own, s, slot, uses, n=P):
            pool.wait_ge(w_in[slot], uses * 16 + 16)
            if not (isinstance(s, int) and s < 2):
                pool.wait_ge(proj_full[1], s - 1)
            own.on(nc.gpsimd.tensor_tensor(w_hi[:, slot, :, 0:n], w_raw[:, slot, :, 0:n],
                                           zeros[:].rearrange("p (a b) -> p a b", a=1).broadcast_to([P, KT, n]), ALU.add))
            own.wait()
            nc.gpsimd.tensor_tensor(w_lo[:, slot, :, 0:n], w_raw[:, slot, :, 0:n],
                                    w_hi[:, slot, :, 0:n], ALU.subtract).then_inc(w_split, 1)

        def project(pe, s, slot, m=P):
            pe.wait_ge(w_split, s + 1)
            for h in range(2):
                if not (isinstance(s, int) and s == 0):
                    pe.wait_ge(proj_free[h], s)
                n = 0
                for k in range(KT):
                    for a, b in ((w_hi, h_hi), (w_lo, h_hi), (w_hi, h_lo)):
                        mm = nc.tensor.matmul(PJ[h][0:m, :], a[:, slot, k, 0:m],
                                              b[:, k, h * HALF:(h + 1) * HALF],
                                              start=n == 0, stop=n == 3 * KT - 1)
                        n += 1
                mm.then_inc(proj_full[h], 1)

        def project_part(pe, s, slot, h, n0, count):
            if n0 == 0:
                if h == 0:
                    pe.wait_ge(w_split, s + 1)
                pe.wait_ge(proj_free[h], s)
            for n in range(n0, n0 + count):
                a, b = ((w_hi, h_hi), (w_lo, h_hi), (w_hi, h_lo))[n % 3]
                mm = nc.tensor.matmul(PJ[h][:], a[:, slot, n // 3, :], b[:, n // 3, h * HALF:(h + 1) * HALF],
                                      start=n == 0, stop=n == 3 * KT - 1)
            if n0 + count == 3 * KT:
                mm.then_inc(proj_full[h], 1)

        def columns(w, c0, n=P):
            return w.rearrange("(k p) c -> p k c", p=P)[:, :, c0:c0 + n]

        def columns_at(w, c0, i, step):
            return w.rearrange("(k p) c -> p k c", p=P)[:, :, bass.ds(i * step + c0, P)]

        def at(i, per, n):
            return i * per + n

        zeros = sb("zeros", [P, 1])

        def wide(ap, n):
            return ap.rearrange("p (o m) -> p o m", o=1).broadcast_to([ap.shape[0], n, ap.shape[1]])

        def each(ap, n):
            return ap.rearrange("p (m o) -> p m o", o=1).broadcast_to([ap.shape[0], ap.shape[1], n])

        X0 = 8

        def sync_0(sp):
            sp.dma_start(cst[:], cst_in).then_inc(const_in, 16)
            sp.wait_ge(par_zeroed, 1)
            rows = [(0, 12, mu[0:1536]), (12, 4, mu[1600:2112]), (16, 4, w0), (20, 4, a0), (24, 4, k_k),
                    (28, 4, k_a), (36, 4, ln_w), (40, 4, ln_b), (PRE0, 8, pre0),
                    (POST0, 8, post0), (PRE1, 8, pre1), (POST1, 8, post1), (CN, 1, c_norm)]
            for r0, n, src in rows:
                sp.dma_start(par_raw[r0:r0 + n, :], src.rearrange("(r c) -> r c", c=P)).then_inc(par_in, 16)
            sp.dma_start(par_raw[32:36, :], r_k.rearrange("(g h) c -> g (h c)", h=2)).then_inc(par_in, 16)
            sp.dma_start(par_raw[LB0:LB0 + 16, :], lbs.rearrange("l (r c) -> (l r) c", c=P)).then_inc(par_in, 16)
            sp.dma_start(par_raw[MUL:MUL + 1, 0:LORA],
                         mu[1536:1600].rearrange("(r c) -> r c", r=1)).then_inc(par_in, 16)
            for tile in range(NC):
                j = tile % 2
                if tile >= 2:
                    sp.wait_ge(xn_ready, tile - 1)
                sp.dma_start(xt[j], x[tile * P:(tile + 1) * P, :]).then_inc(x_in[j], 16)
                if tile == 1:
                    sp.dma_start(lw[0:32, :], w2).then_inc(small_in, 16)
                    sp.dma_start(lw[32:64, :], a2).then_inc(small_in, 16)
                    sp.dma_start(tb[:], table).then_inc(small_in, 16)
                    sp.dma_start(bk, buckets).then_inc(small_in, 16)
                    sp.dma_start(sinkb[:], sinks.rearrange("(o h) -> o h", o=1).broadcast_to([P, 8])).then_inc(small_in, 16)
            sp.wait_ge(bias_row, 1)
            sp.dma_start(scratch.rearrange("q h m -> h q m"),
                         brow.rearrange("h (o m) -> h o m", o=1).broadcast_to([8, P, 384])).then_inc(scr_out, 16)
            sp.wait_ge(scr_out, 16)

        def pool_0(pool, own):
            nc.gpsimd.memset(par_raw, 0.0).then_inc(par_zeroed, 1)
            own.on(nc.gpsimd.memset(zeros[:], 0.0))
            nc.gpsimd.memset(ones_all[:], 1.0)
            for n, v in enumerate((NORM_EPS, GN_EPS, 20 * float(np.log(2.0)), 1.0)):
                ins = nc.gpsimd.memset(eps[:, n:n + 1], v)
            ins.then_inc(eps_ready, 1)
            for tile in range(NC):
                j = tile % 2
                pool.wait_ge(hi_ready, tile + 1)
                nc.gpsimd.tensor_tensor(h_lo[:, :, tile * P:(tile + 1) * P], hf[j],
                                        h_hi[:, :, tile * P:(tile + 1) * P], ALU.subtract).then_inc(lo_ready, 1)

        def tensor_0(pe):
            pe.wait_ge(const_in, 16)
            pe.wait_ge(par_in, 16 * 16)
            nc.tensor.transpose(ZB[:, 0:ROWS], par_raw, cst[0:ROWS, CI:CI + ROWS]).then_inc(par_full, 1)
            for tile in range(NC):
                j = tile % 2
                pe.wait_ge(xn_ready, tile + 1)
                for b in range(2):
                    if tile:
                        pe.wait_ge(sc_free[b], tile)
                    for k in range(4):
                        kk = 4 * b + k
                        mm = nc.tensor.transpose(SC[b][:, k * P:(k + 1) * P], xn[j][:, kk * P:(kk + 1) * P], ident)
                    mm.then_inc(sc_full[b], 1)
            pe.wait_ge(small_in, 16 * 5)
            nc.tensor.matmul(DP[0][0:8, 0:384], tb[:], bk[:, 0:384], start=True, stop=True).then_inc(bias_full, 1)

        def scalar_0(act, own):
            act.wait_ge(const_in, 16)
            nc.scalar.activation(ident_r[:], ident, ACT.Copy).then_inc(ident_ready, 1)
            act.wait_ge(eps_ready, 1)
            nc.scalar.preload_act_table_set("natural_log_exp_and_others")
            for tile in range(NC):
                j = tile % 2
                act.wait_ge(x_in[j], 16 * (tile // 2 + 1))
                if tile >= 2:
                    act.wait_ge(sc_full[1], tile - 1)
                own.on(nc.scalar.activation(xn[j], xt[j], ACT.Square, accum_out=rms[:, j:j + 1]))
                own.wait()
                own.on(nc.scalar.activation(rms[:, 2 + j:3 + j], rms[:, j:j + 1], ACT.Ln, scale=1.0 / D, bias=eps[:, 0:1]))
                own.wait()
                nc.scalar.activation(rms[:, 4 + j:5 + j], rms[:, 2 + j:3 + j], ACT.Exp, scale=-0.5).then_inc(rstd_ready, 1)
                act.wait_ge(sc_free[1], tile + 1)
                act.wait_ge(sc_free[0], tile + 1)
                nc.scalar.activation(h_hi[:, :, tile * P:(tile + 1) * P], hf[j], ACT.Copy).then_inc(hi_ready, 1)

        def vector_0(dve, own):
            dve.wait_ge(par_full, 1)
            own.on(nc.vector.tensor_copy(par[:, 0:RAW_KINDS, :].rearrange("p k f -> p (k f)"), ZB[:, 0:44]))
            own.on(nc.vector.tensor_copy(oth[:], ZB[:, 44:ROWS]))
            own.wait()
            nc.vector.tensor_scalar(par[:, OMU:OMU + 4, :], par[:, 0:4, :], -1.0, 1.0, ALU.mult, ALU.add)
            nc.vector.tensor_scalar(par[:, W0H:W0H + 2, :], par[:, W0:W0 + 2, :], 0.5, None, ALU.mult)
            nc.vector.tensor_scalar(par[:, KAH:KAH + 1, :], par[:, KA:KA + 1, :], 0.5, None, ALU.mult)
            nc.vector.tensor_scalar(par[:, OKAH:OKAH + 1, :], par[:, KA:KA + 1, :], -0.5, 1.0, ALU.mult, ALU.add)
            own.on(nc.vector.tensor_scalar(lbp[:, 0, 0:1], oth[:, MUL - 44:MUL - 43], -1.0, 1.0, ALU.mult, ALU.add))
            own.on(nc.vector.memset(u[:, 0:1], 0.0))
            own.on(nc.vector.memset(reset[:], 1.0))
            own.wait()
            nc.vector.memset(reset[:].rearrange("p (c t) -> p c t", t=C)[:, :, 0:1], 0.0).then_inc(par_ready, 1)
            for tile in range(NC):
                j = tile % 2
                dve.wait_ge(rstd_ready, tile + 1)
                nc.vector.tensor_scalar(xn[j], xt[j], rms[:, 4 + j:5 + j], None, ALU.mult).then_inc(xn_ready, 1)
                if tile >= 2:
                    dve.wait_ge(lo_ready, tile - 1)
                for b in range(2):
                    dve.wait_ge(sc_full[b], tile + 1)
                    nc.vector.tensor_tensor(hf[j][:, 4 * b:4 * b + 4, :], SC[b][:].rearrange("p (k t) -> p k t", k=4),
                                            each(oth[:, PRE0 - 44 + 4 * b:PRE0 - 44 + 4 * b + 4], P),
                                            ALU.mult).then_inc(sc_free[b], 1)
            dve.wait_ge(bias_full, 1)
            nc.vector.tensor_tensor(brow, DP[0][0:8, 0:384], bk[0:8, 384:768], ALU.add).then_inc(bias_row, 1)

        GROUPS = NC // 2
        SLOTS = LEVELS + 1
        USES = 23
        U_W, U_A, U_SS, U_BONUS, U_V = range(5)
        U_MEAN, U_VAR = 21, 22

        def front(g):
            return 5 if g == 0 else 4 + 4 * g

        def out_use(g):
            return front(g + 1) + (3 if g + 1 < GROUPS else 0)

        A_SLABS = (COL_R, COL_K, COL_V, COL_AG)

        def slab_a(i, q):
            return at(i, 4, SLAB_A + q)

        def sync_a(sp):
            load_slab(sp, SLAB_LORA, 0, columns(w_in0, COL_LORA, LORA))
            for q, col in enumerate(A_SLABS):
                load_slab(sp, SLAB_A + q, (SLAB_A + q) % 2, columns(w_in0, col))
            with sp.Fori(0, PAIRS - 1) as i:
                for q, col in enumerate(A_SLABS):
                    load_slab(sp, at(i, 4, SLAB_A + 4 + q), (SLAB_A + q) % 2, columns_at(w_in0, col + P, i, P))

        def pool_a(pool, own):
            split_slab(pool, own, SLAB_LORA, 0, 0, LORA)
            for q in range(4):
                split_slab(pool, own, SLAB_A + q, (SLAB_A + q) % 2, (SLAB_A + q) // 2)

            def prepare(i):
                pool.wait_ge(t_ready, at(i, 1, 1))
                nc.gpsimd.tensor_tensor(gcum, gcum, ks, ALU.mult).then_inc(kp_ready, 1)
                pool.wait_ge(kp_ready, at(i, 1, 1))
                nc.gpsimd.tensor_tensor(ldb, gcum, rs, ALU.mult).then_inc(rk_ready, 1)
                pool.wait_ge(exp_ready, at(i, 3, 3))
                nc.gpsimd.tensor_tensor(kt, gcum, em, ALU.mult).then_inc(kq_ready, 1)

            with pool.Fori(0, PAIRS - 1) as i:
                own.enter(i, 4)
                prepare(i)
                for q in range(4):
                    split_slab(pool, own, at(i, 4, SLAB_A + 4 + q), (SLAB_A + q) % 2, at(i, 2, (SLAB_A + 4 + q) // 2))
                own.leave(PAIRS - 1)
            prepare(PAIRS - 1)

        def tensor_a(pe):
            pe.wait_ge(ident_ready, 1)
            project(pe, SLAB_LORA, 0, LORA)
            for q in range(4):
                project(pe, SLAB_A + q, (SLAB_A + q) % 2)

            def sc_use(h, i, use):
                pe.wait_ge(sc_free[h], at(i, USES, X0 + use))

            def channel_sums(i, use, lhs, src):
                for h in range(2):
                    sc_use(h, i, use)
                    nc.tensor.matmul(SC[h][:], lhs, src[:, h * HALF:(h + 1) * HALF],
                                     start=True, stop=True).then_inc(sc_full[h], 1)

            def prepare(i):
                pe.wait_ge(lora_ready, 2)
                pe.wait_ge(lwp_ready, at(i, 1, 1))
                for r in range(2):
                    channel_sums(i, U_W + r, lwp[32 * r:32 * r + 32, :], lora[32 * r:32 * r + 32, :])
                pe.wait_ge(ksq_ready, at(i, 1, 1))
                channel_sums(i, U_SS, ones64, kkb)
                pe.wait_ge(rkm_ready, at(i, 1, 1))
                pe.wait_ge(rk_ready, at(i, 1, 1))
                channel_sums(i, U_BONUS, rkm[:], ldb)
                for j in range(2):
                    sc_use(j, i, U_V)
                    for n in range(4):
                        mm = nc.tensor.transpose(SC[j][:, n * P:(n + 1) * P], vs[:, (4 * j + n) * C:(4 * j + n + 1) * C],
                                                 ident)
                    mm.then_inc(sc_full[j], 1)
                pe.wait_ge(kq_ready, at(i, 1, 1))
                pe.wait_ge(ab_ready, at(i, 3, 3))

            def scores(i, g):
                for j in range(2):
                    c = slice((2 * g + j) * C, (2 * g + j + 1) * C)
                    sc_use(j, i, front(g))
                    for n, src in enumerate((bb, kt)):
                        mm = nc.tensor.transpose(SC[j][:, n * P:(n + 1) * P], src[:, c], ident)
                    mm.then_inc(sc_full[j], 1)
                for j in range(2):
                    c = slice((2 * g + j) * C, (2 * g + j + 1) * C)
                    for h in range(2):
                        hp = slice(h * HD, (h + 1) * HD)
                        sc_use(h, i, front(g) + 1 + j)
                        for n, src in enumerate((bb, kt)):
                            mm = nc.tensor.matmul(SC[h][:, n * 256:(n + 1) * 256].rearrange("p (a t) -> p a t", a=2),
                                                  src[hp, c], ar[hp, :, c], start=True, stop=True)
                        mm.then_inc(sc_full[h], 1)
                if g:
                    pe.wait_ge(pf_ready, at(i, GROUPS, g))
                for j in range(2):
                    c = slice((2 * g + j) * C, (2 * g + j + 1) * C)
                    for h in range(2):
                        hp = slice(h * HD, (h + 1) * HD)
                        dst = DP[0] if h else ZB
                        mm = nc.tensor.matmul(dst[:, j * P:(j + 1) * P], ar[hp, 0, c], bb[hp, c],
                                              start=True, stop=True)
                mm.then_inc(z_full, 1)

            def level(i, g, k, between):
                if k:
                    pe.wait_ge(dp_copied, at(i, 14 * GROUPS, 14 * g + 2 * k))
                    if k == 1:
                        pe.wait_ge(lmr_ready, at(i, GROUPS, g + 1))
                    for un in range(4):
                        mm = nc.tensor.matmul(ZB[:, un * P:(un + 1) * P], lmr[:, un * P:(un + 1) * P], dpt(un)[1],
                                              start=True, stop=True)
                    mm.then_inc(z_full, 1)
                else:
                    pe.wait_ge(lm_ready, at(i, 2 * GROUPS, 2 * g + 2))
                    for b in range(2):
                        nc.tensor.matmul(DP[b][:].rearrange("p (n t) -> p n t", n=4), ident_r[:], wide(ident_r[:], 4),
                                         start=True, stop=True, skip_group_check=True)
                between()
                pe.wait_ge(xt_ready, at(i, 8 * GROUPS, 8 * g + k + 1))
                for un in range(4):
                    b, v = un // 2, un % 2
                    xs = xr[:, un * P:(un + 1) * P]
                    dk = ident_r[:] if k == 0 else dpt(un)[0]
                    nc.tensor.matmul(DP[b][:, v * 256:v * 256 + P], xs, dk, start=False, stop=True, skip_group_check=True)
                    mm = nc.tensor.matmul(DP[b][:, v * 256 + P:v * 256 + 256], dk, xs, start=False, stop=True,
                                          skip_group_check=True)
                    if v:
                        mm.then_inc(dp_full[b], 1)

            def refine(i, g, between):
                pe.wait_ge(dp_copied, at(i, 14 * GROUPS, 14 * g + 14))
                for un in range(4):
                    zs = ZB[:, un * P:(un + 1) * P]
                    nc.tensor.matmul(zs, lm[:, un * P:(un + 1) * P], dpt(un)[1].bitcast(F32), start=True, stop=False)
                    mm = nc.tensor.matmul(zs, ident_r[:], dpt(un)[1], start=False, stop=True)
                mm.then_inc(z_full, 1)
                between()
                pe.wait_ge(xt_ready, at(i, 8 * GROUPS, 8 * g + 8))
                for un in range(4):
                    mm = nc.tensor.matmul(DP[0][:, un * P:(un + 1) * P], dpt(un)[0], xr[:, un * P:(un + 1) * P],
                                          start=True, stop=True)
                mm.then_inc(corr_full, 1)

            def chain(i, g, piece):
                j, stage = piece // 3, piece % 3
                cn = 2 * g + j
                c = slice(cn * C, (cn + 1) * C)
                sp_ = scm[g % 2]
                tb2 = tmb[g % 2]
                if stage == 0:
                    if j == 0:
                        pe.wait_ge(pf_ready, at(i, GROUPS, g + 1))
                        sc_use(0, i, front(g) + 3)
                        sc_use(1, i, front(g) + 3)
                    pe.wait_ge(state_ready, at(i, 9, cn + 1))
                    nc.tensor.matmul(SQ[:, 0:P], ar[:, 0, c], st, start=True, stop=True)
                    for h in range(2):
                        hp = slice(h * HD, (h + 1) * HD)
                        mm = nc.tensor.matmul(SQ[:, hp], sp_[:, 2 * j + h, 256:384], vtm_a[:, cn, hp], start=False, stop=True,
                                              skip_group_check=True)
                    mm.then_inc(rhs_full, 1)
                elif stage == 1:
                    pe.wait_ge(nr_ready, at(i, 8, cn + 1))
                    for h in range(2):
                        mm = nc.tensor.matmul(SQ[:, P + h * HD:P + (h + 1) * HD],
                                              pf[:, g % 2, (2 * j + h) * P:(2 * j + h + 1) * P],
                                              nr[:, j, h * HD:(h + 1) * HD], start=True, stop=True)
                    mm.then_inc(sa_full, 1)
                else:
                    pe.wait_ge(sa_ready, at(i, 8, cn + 1))
                    nc.tensor.matmul(SQ[:, 256:384], tb2[:, j, 0:P], sa[:, j, :], start=True, stop=False)
                    nc.tensor.matmul(SQ[:, 256:384], tb2[:, j, P:2 * P], vtm_a[:, cn, :], start=False,
                                     stop=True)
                    sc_use(j, i, out_use(g))
                    nc.tensor.matmul(SC[j][:, 0:P], st, ar[:, 1, c], start=True, stop=True)
                    for h in range(2):
                        hp = slice(h * HD, (h + 1) * HD)
                        nc.tensor.matmul(SC[j][hp, 0:P], sa[:, j, hp], sp_[:, 2 * j + h, P:2 * P], start=False, stop=True,
                                         skip_group_check=True)
                        mm = nc.tensor.matmul(SC[j][hp, 0:P], vtm_a[:, cn, hp], sp_[:, 2 * j + h, 3 * P:4 * P],
                                              start=False, stop=True, skip_group_check=True)
                    mm.then_inc(sc_full[j], 1)

            def body(i, next_slabs):
                prepare(i)
                for g in range(GROUPS):
                    scores(i, g)
                    for k in range(SLOTS):
                        def between():
                            if g and k < 6:
                                chain(i, g - 1, k)
                        if k < LEVELS:
                            level(i, g, k, between)
                        else:
                            refine(i, g, between)
                        if next_slabs:
                            project_part(pe, at(i, 4, SLAB_A + 4 + g), (SLAB_A + g) % 2, k // 4, k % 4 * 6, 6)
                for piece in range(6):
                    chain(i, GROUPS - 1, piece)
                sc_use(0, i, U_MEAN)
                sc_use(1, i, U_MEAN)
                channel_sums(i, U_MEAN, ones64, ysb)
                pe.wait_ge(ysq_ready, at(i, 1, 1))
                channel_sums(i, U_VAR, ones64, ysq)

            with pe.Fori(0, PAIRS - 1) as i:
                body(i, True)
            body(PAIRS - 1, False)

        def scalar_a(act, own):
            act.wait_ge(par_ready, 1)

            def scale_shifted(s, h, m, col):
                if h == 0 and not (isinstance(s, int) and s == 0):
                    act.wait_ge(proj_free[1], s)
                act.wait_ge(proj_full[h], s + 1)
                nc.scalar.activation(u[0:m, 1 + h * HALF:1 + (h + 1) * HALF], PJ[h][0:m, :], ACT.Copy,
                                     scale=col).then_inc(mix_scaled, 1)

            for h in range(2):
                scale_shifted(SLAB_LORA, h, LORA, oth[0:LORA, MUL - 44:MUL - 43])
            act.wait_ge(proj_free[0], 1)
            act.wait_ge(proj_free[1], 1)
            nc.scalar.activation(lora[0:32, :], lora[0:32, :], ACT.Tanh).then_inc(lora_ready, 1)
            nc.scalar.activation(lora[32:64, 0:1], lora[32:64, 0:1], ACT.Copy).then_inc(lora_ready, 1)
            act.wait_ge(pp_ready, 1)
            for q in range(4):
                for h in range(2):
                    scale_shifted(SLAB_A + q, h, P, pp[:, MU + q:MU + q + 1])

            def prepare(i):
                nc.scalar.preload_act_table(ACT.Silu)
                act.wait_ge(pp_ready, at(i, 1, 1))
                for h in range(2):
                    act.wait_ge(proj_free[h], slab_a(i, 4))
                nc.scalar.activation(kkb, ks, ACT.Square, scale=pp[:, KK:KK + 1]).then_inc(ksq_ready, 1)
                for r, (dst, kind) in enumerate(((ldb, W0H), (bb, A0H))):
                    for h in range(2):
                        act.wait_ge(sc_full[h], at(i, USES, X0 + r + 1))
                        nc.scalar.activation(dst[:, h * HALF:(h + 1) * HALF], SC[h][:], ACT.Tanh, scale=0.5,
                                             bias=pp[:, kind:kind + 1]).then_inc(sc_free[h], 1)
                nc.scalar.activation(gb, gs, ACT.Silu).then_inc(gate_ready, 1)
                nc.scalar.preload_act_table_set("natural_log_exp_and_others")
                act.wait_ge(sc_free[0], at(i, USES, X0 + 3))
                act.wait_ge(sc_free[1], at(i, USES, X0 + 3))
                own.on(nc.scalar.activation(kkb, kkb, ACT.Ln, scale=2.0 ** 40))
                own.wait()
                nc.scalar.activation(kkb, kkb, ACT.Exp, scale=-0.5, bias=eps[:, 2:3]).then_inc(rn_ready, 1)
                act.wait_ge(gc_ready, at(i, 1, 1))
                nc.scalar.activation(em.rearrange("p (c t) -> p c t", c=NC), gc[:, :, 1:C + 1], ACT.Exp,
                                     scale=-1.0).then_inc(exp_ready, 1)
                nc.scalar.activation(ee[:, :, 0:C + 1], gc[:, :, 0:C + 1], ACT.Exp).then_inc(exp_ready, 1)
                nc.scalar.activation(fac[:, 1, 0:7], fac[:, 0, 0:7], ACT.Exp).then_inc(exp_ready, 1)
                for j in range(2):
                    act.wait_ge(sc_full[j], at(i, USES, X0 + U_V + 1))
                    nc.scalar.activation(vtm_a[:, 4 * j:4 * j + 4, :], SC[j][:].rearrange("p (n c) -> p n c", n=4),
                                         ACT.Copy).then_inc(sc_free[j], 1)

            def chain(i, g, piece):
                j, stage = piece // 3, piece % 3
                cn = 2 * g + j
                if stage == 0:
                    act.wait_ge(rhs_full, at(i, 8, cn + 1))
                    nc.scalar.activation(nr[:, j, :], SQ[:, 0:P], ACT.Copy, scale=-1.0).then_inc(nr_ready, 1)
                elif stage == 1:
                    act.wait_ge(sa_full, at(i, 8, cn + 1))
                    nc.scalar.activation(sa[:, j, :], SQ[:, P:2 * P], ACT.Copy).then_inc(sa_ready, 1)
                else:
                    act.wait_ge(sc_full[j], at(i, USES, X0 + out_use(g) + 1))
                    nc.scalar.activation(ysb[:, cn * C:(cn + 1) * C], SC[j][:, 0:P], ACT.Copy).then_inc(sc_free[j], 1)

            def body(i, next_slabs):
                if next_slabs:
                    own.enter(i, 1)
                prepare(i)

                def mix(g, h):
                    if next_slabs:
                        scale_shifted(at(i, 4, SLAB_A + 4 + g), h, P, pn[:, MU + g:MU + g + 1])

                if next_slabs:
                    act.wait_ge(pn_ready, at(i, 1, 1))
                for g in range(GROUPS):
                    for j in range(2):
                        act.wait_ge(sc_full[j], at(i, USES, X0 + front(g) + 1))
                        nc.scalar.activation(tmb[g % 2][:, j, :], SC[j][:, 0:256], ACT.Copy).then_inc(sc_free[j], 1)
                    act.wait_ge(lm_ready, at(i, 2 * GROUPS, 2 * g + 2))
                    nc.scalar.activation(lmr[:], lm, ACT.Copy).then_inc(lmr_ready, 1)
                    for k in range(SLOTS):
                        if g and k < 6:
                            chain(i, g - 1, k)
                        if k < LEVELS:
                            for b in range(2):
                                act.wait_ge(dp_full[b], at(i, LEVELS * GROUPS, LEVELS * g + k + 1))
                                nc.scalar.activation(dpr[:, b * HALF:(b + 1) * HALF], DP[b][:],
                                                     ACT.Copy).then_inc(dp_copied, 1)
                        if k == 0 and g:
                            mix(g - 1, 1)
                        if k == 4:
                            mix(g, 0)
                mix(GROUPS - 1, 1)
                for piece in range(6):
                    chain(i, GROUPS - 1, piece)
                act.wait_ge(sc_free[0], at(i, USES, X0 + U_MEAN + 1))
                act.wait_ge(sc_free[1], at(i, USES, X0 + U_MEAN + 1))
                nc.scalar.activation(ysq, ysb, ACT.Square).then_inc(ysq_ready, 1)
                for h in range(2):
                    act.wait_ge(sc_full[h], at(i, USES, X0 + U_VAR + 1))
                    nc.scalar.activation(kkb[:, h * HALF:(h + 1) * HALF], SC[h][:], ACT.Ln, scale=1.0 / HD,
                                         bias=eps[:, 1:2]).then_inc(sc_free[h], 1)
                act.wait_ge(sc_free[0], at(i, USES, X0 + U_VAR + 1))
                act.wait_ge(sc_free[1], at(i, USES, X0 + U_VAR + 1))
                nc.scalar.activation(kkb, kkb, ACT.Exp, scale=-0.5).then_inc(ynorm_ready, 1)

            with act.Fori(0, PAIRS - 1) as i:
                body(i, True)
                own.leave(PAIRS - 1)
            body(PAIRS - 1, False)

        DVE_STEPS = 17

        def vector_a(dve, own):
            for h in range(2):
                dve.wait_ge(proj_full[h], 1)
                dve.wait_ge(mix_scaled, h + 1)
                nc.vector.scalar_tensor_tensor(lora[:, h * HALF:(h + 1) * HALF], PJ[h][0:LORA, :], lbp[0:LORA, 0, 0:1],
                                               u[0:LORA, h * HALF:(h + 1) * HALF], ALU.mult,
                                               ALU.add).then_inc(proj_free[h], 1)

            def mix(i, q, h, cols):
                dve.wait_ge(proj_full[h], slab_a(i, q + 1))
                dve.wait_ge(mix_scaled, at(i, 8, 2 + 2 * q + h + 1))
                nc.vector.scalar_tensor_tensor(stage[:, q, h * HALF:(h + 1) * HALF], PJ[h][:],
                                               cols[:, OMU + q:OMU + q + 1], u[:, h * HALF:(h + 1) * HALF], ALU.mult,
                                               ALU.add).then_inc(proj_free[h], 1)

            nc.vector.tensor_scalar(pp[:].rearrange("p (k o) -> p k o", o=1), par[:, :, 0:1], 1.0, None,
                                    ALU.mult).then_inc(pp_ready, 1)
            dve.wait_ge(pp_ready, 1)
            for q in range(4):
                for h in range(2):
                    mix(0, q, h, pp)
            dve.wait_ge(small_in, 16 * 5)

            def masks(i, g):
                for un in range(4):
                    h, j = un % 2, un // 2
                    dve.wait_ge(sc_full[h], at(i, USES, X0 + front(g) + 2 + j))
                    nc.vector.tensor_tensor(scm[g % 2][:, un, :], SC[h][:], cst[:, CM:CM + 512],
                                            ALU.mult).then_inc(sc_free[h], 1)
                dve.wait_ge(z_full, at(i, 8 * GROUPS, 8 * g + 1))
                for h, src in enumerate((ZB, DP[0])):
                    nc.vector.tensor_tensor(lm.rearrange("p (j h t) -> p j h t", j=2, h=2)[:, :, h, :],
                                            src[:, 0:256].rearrange("p (j t) -> p j t", j=2),
                                            wide(cst[:, CL:CL + P], 2), ALU.mult).then_inc(lm_ready, 1)

            def state(i, cn):
                j = cn % 2
                dve.wait_ge(sc_full[j], at(i, USES, X0 + out_use(cn // 2) + 1))
                if cn < NC - 1:
                    own.on(nc.vector.scalar_tensor_tensor(st2, SQ[:, 256:384], fac[:, 1, cn:cn + 1], ones64,
                                                          ALU.mult, ALU.mult))
                    own.wait()
                    nc.vector.scalar_tensor_tensor(st, st, fac[:, 1, cn:cn + 1], st2, ALU.mult,
                                                   ALU.add).then_inc(state_ready, 1)
                else:
                    nc.vector.memset(st2, 0.0).then_inc(state_ready, 1)

            def body(i, next_slabs):
                if next_slabs:
                    own.enter(i, DVE_STEPS)
                    nc.vector.tensor_scalar(pn[:].rearrange("p (k o) -> p k o", o=1), par[:, :, bass.ds(i + 1, 1)], 1.0, None,
                                            ALU.mult).then_inc(pn_ready, 1)
                dyn = bass.ds(i * P, P)
                nc.vector.tensor_scalar(lwp[:], lw[:, dyn], 1.0, None, ALU.mult).then_inc(lwp_ready, 1)
                nc.vector.tensor_scalar(rkm[:], ones64, pp[:, RK:RK + 1], None, ALU.mult).then_inc(rkm_ready, 1)
                dve.wait_ge(sc_free[0], at(i, USES, X0 + 2))
                dve.wait_ge(sc_free[1], at(i, USES, X0 + 2))
                own.on(nc.vector.tensor_scalar(ldb, ldb, -0.5 * DECAY, -0.5 * DECAY, ALU.mult, ALU.add))
                own.wait()
                for h in range(2):
                    own.on(nc.vector.tensor_tensor_scan(gcum[:, h * HALF:(h + 1) * HALF], reset[:],
                                                        ldb[:, h * HALF:(h + 1) * HALF], 0.0, ALU.mult, ALU.add))
                for h in range(2):
                    dve.wait_ge(sc_full[h], at(i, USES, X0 + 3))
                    nc.vector.tensor_scalar(kkb[:, h * HALF:(h + 1) * HALF], SC[h][:], 1e-24, None,
                                            ALU.max).then_inc(sc_free[h], 1)
                own.wait()
                g3 = gcum.rearrange("p (c t) -> p c t", c=NC)
                own.on(nc.vector.tensor_tensor(gc[:, :, 1:C + 1], g3, g3[:, :, 63:64].broadcast_to([P, NC, C]),
                                               ALU.subtract))
                own.on(nc.vector.tensor_scalar(gc[:, :, 0:1], g3[:, :, 63:64], -1.0, None, ALU.mult))
                own.wait()
                nc.vector.tensor_tensor(fac[:, 0, 0:7], gc[:, 0:7, C:C + 1].rearrange("p c o -> p (c o)"),
                                        g3[:, 1:8, 63:64].rearrange("p c o -> p (c o)"), ALU.add).then_inc(gc_ready, 1)
                dve.wait_ge(gc_ready, at(i, 1, 1))
                nc.vector.tensor_scalar(gcum, bb, pp[:, KAH:KAH + 1], pp[:, OKAH:OKAH + 1], ALU.mult,
                                        ALU.add).then_inc(t_ready, 1)
                dve.wait_ge(rn_ready, at(i, 1, 1))
                nc.vector.scalar_tensor_tensor(kkb, ks, pp[:, KK:KK + 1], kkb, ALU.mult,
                                               ALU.mult).then_inc(kk_ready, 1)
                dve.wait_ge(kk_ready, at(i, 1, 1))
                own.on(nc.vector.scalar_tensor_tensor(bb, bb, 1.0, kkb, ALU.add, ALU.mult))
                dve.wait_ge(exp_ready, at(i, 3, 3))
                nc.vector.tensor_tensor(ar[:, 0, :].rearrange("p (c t) -> p c t", c=NC),
                                        kkb.rearrange("p (c t) -> p c t", c=NC), ee[:, :, 0:C],
                                        ALU.mult).then_inc(ab_ready, 1)
                nc.vector.tensor_tensor(ar[:, 1, :].rearrange("p (c t) -> p c t", c=NC),
                                        rs.rearrange("p (c t) -> p c t", c=NC), ee[:, :, 1:C + 1],
                                        ALU.mult).then_inc(ab_ready, 1)
                own.wait()
                nc.vector.scalar_tensor_tensor(bb, bb, 0.5, em, ALU.mult, ALU.mult).then_inc(ab_ready, 1)
                dve.wait_ge(ab_ready, at(i, 3, 3))
                dve.wait_ge(kq_ready, at(i, 1, 1))
                for h in range(2):
                    dve.wait_ge(sc_full[h], at(i, USES, X0 + 4))
                    nc.vector.tensor_tensor(em[:, h * HALF:(h + 1) * HALF], SC[h][:], vs[:, h * HALF:(h + 1) * HALF],
                                            ALU.mult).then_inc(sc_free[h], 1)
                nc.vector.memset(st, 0.0).then_inc(state_ready, 1)
                dve.wait_ge(gate_ready, at(i, 1, 1))
                z4 = ZB[:].rearrange("p (u t) -> p u t", u=4)
                x4 = xr[:].rearrange("p (u t) -> p u t", u=4)

                def late_mix(g, h):
                    if next_slabs:
                        mix(i + 1, g, h, pn)

                for g in range(GROUPS):
                    masks(i, g)
                    for k in range(LEVELS):
                        if k:
                            dve.wait_ge(z_full, at(i, 8 * GROUPS, 8 * g + k + 1))
                            src = z4
                        else:
                            dve.wait_ge(sc_free[0], at(i, USES, X0 + front(g) + 3))
                            dve.wait_ge(sc_free[1], at(i, USES, X0 + front(g) + 3))
                            src = scm[g % 2][:, :, 0:P]
                        nc.vector.tensor_tensor(x4, src, wide(cst[:, CN7 + k * P:CN7 + (k + 1) * P], 4),
                                                ALU.mult).then_inc(xt_ready, 1)
                        if g and k in (2, 5):
                            state(i, 2 * (g - 1) + k // 3)
                        if k == 1 and g:
                            late_mix(g - 1, 1)
                        if k == 5:
                            late_mix(g, 0)
                    dve.wait_ge(z_full, at(i, 8 * GROUPS, 8 * g + 8))
                    nc.vector.tensor_tensor(x4, wide(ident, 4), z4, ALU.subtract).then_inc(xt_ready, 1)
                    dve.wait_ge(corr_full, at(i, GROUPS, g + 1))
                    dve.wait_ge(dp_copied, at(i, 14 * GROUPS, 14 * g + 14))
                    nc.vector.tensor_tensor(pf[:, g % 2, :].rearrange("p (u t) -> p u t", u=4),
                                            dpr[:].rearrange("p (u a t) -> p u a t", u=4, a=2)[:, :, 1, :].bitcast(F32),
                                            DP[0][:].rearrange("p (u t) -> p u t", u=4), ALU.add).then_inc(pf_ready, 1)
                late_mix(GROUPS - 1, 1)
                for j in range(2):
                    state(i, NC - 2 + j)
                for h in range(2):
                    dve.wait_ge(sc_full[h], at(i, USES, X0 + U_MEAN + 1))
                    nc.vector.scalar_tensor_tensor(ysb[:, h * HALF:(h + 1) * HALF], SC[h][:], -1.0 / HD,
                                                   ysb[:, h * HALF:(h + 1) * HALF], ALU.mult,
                                                   ALU.add).then_inc(sc_free[h], 1)
                dve.wait_ge(ynorm_ready, at(i, 1, 1))
                own.on(nc.vector.tensor_tensor(ysb, ysb, kkb, ALU.mult))
                own.wait()
                own.on(nc.vector.tensor_scalar(ysb, ysb, pp[:, LNW:LNW + 1], pp[:, LNB:LNB + 1], ALU.mult, ALU.add))
                own.wait()
                own.on(nc.vector.tensor_tensor(ysb, ysb, em, ALU.add))
                own.wait()
                own.on(nc.vector.tensor_tensor(yT[:, bass.ds(i, 1), :], ysb.rearrange("p (o t) -> p o t", o=1),
                                               gb.rearrange("p (o t) -> p o t", o=1), ALU.mult))
                if next_slabs:
                    nc.vector.tensor_copy(pp[:], pn[:]).then_inc(pp_ready, 1)
                    dve.wait_ge(pp_ready, at(i, 1, 2))

            with dve.Fori(0, PAIRS - 1) as i:
                body(i, True)
                own.leave(PAIRS - 1)
            body(PAIRS - 1, False)

        SB = X0 + USES * PAIRS
        bias = zT[:, 0:2, :].rearrange("p a (b k) -> p (a b) k", b=4)
        kd = [zT[:, 2 + j, :] for j in range(KV)]
        qb = [zT[:, 4 + n, :] for n in range(4)]
        vch = work[:, 0:T]
        vtm = work[:, T:2 * T].rearrange("p (n c) -> p n c", n=NC)
        ps = work[:, 2 * T:4 * T].rearrange("p (g h k) -> p g h k", g=2, h=4)
        pt = work[:, 4 * T:6 * T].rearrange("p (g h a q) -> p g h a q", g=2, h=4, a=2)
        ob = work[:, 6 * T:6 * T + 512].rearrange("p (g c) -> p g c", g=2)
        GROUPS_B = KV * NC
        sm = soft[:]

        B_SLABS = [("v", 0), ("k", 0), ("q", 0), ("q", 1), ("g", 0), ("g", 1),
                   ("k", 1), ("q", 2), ("q", 3), ("g", 2), ("g", 3)]
        B_FIRST = 6

        def sync_b(sp):
            sp.dma_start(bias[:], bass.AP(scratch.tensor, 127, [[8 * 384 - 1, P], [384, 8], [1, 256]])).then_inc(scr_in, 16)
            for n, (kind, a) in enumerate(B_SLABS):
                s = SLAB_V + n
                if kind == "k":
                    load_slab(sp, s, s % 2, columns(w_in0, COL_BK + a * HD, HD))
                    sp.dma_start(w_raw[:, s % 2, :, HD:P], columns(w_in0, COL_BK + a * HD, HD)).then_inc(w_in[s % 2], 16)
                else:
                    load_slab(sp, s, s % 2,
                              columns(w_in0, {"v": COL_BV, "q": COL_Q, "g": COL_BG}[kind] + a * P))

        def pool_b(pool, own):
            extra = [0, 0]
            for n, (kind, a) in enumerate(B_SLABS):
                s = SLAB_V + n
                extra[s % 2] += kind == "k"
                split_slab(pool, own, s, s % 2, s // 2 + extra[s % 2])

        def tensor_b(pe):
            for n in range(B_FIRST):
                project(pe, SLAB_V + n, (SLAB_V + n) % 2)
                if n == 0:
                    pe.wait_ge(proj_free[0], SLAB_V + 1)
                    pe.wait_ge(proj_free[1], SLAB_V + 1)
                    for b in range(2):
                        for m in range(4):
                            mm = nc.tensor.transpose(DP[b][:, m * P:(m + 1) * P],
                                                     vch[:, (4 * b + m) * P:(4 * b + m + 1) * P], ident)
                        mm.then_inc(vt_full, 1)

            def scores(grp):
                j, n = grp // NC, grp % NC
                if n == 0:
                    for h in range(2):
                        pe.wait_ge(proj_free[h], SLAB_V + (4 if j == 0 else 9))
                for part in range(2):
                    hp = slice(part * HD, (part + 1) * HD)
                    pe.wait_ge(sc_free[part], SB + grp)
                    for qi in range(2):
                        w = P if n == 0 else 2 * P
                        mm = nc.tensor.matmul(SC[part][:, qi * 256 + 256 - w:qi * 256 + 256],
                                              qb[2 * j + qi][hp, n * P:(n + 1) * P],
                                              kd[j][hp, (n + 1) * P - w:(n + 1) * P], start=True, stop=True)
                    mm.then_inc(sc_full[part], 1)

            def attend(grp):
                j, n = grp // NC, grp % NC
                halves = (1,) if n == 0 else (0, 1)
                pe.wait_ge(p_ready, 4 * (grp + 1))
                if grp == 0:
                    pe.wait_ge(vt_ready, 2)
                for qi in range(2):
                    if grp:
                        pe.wait_ge(pt_copied[qi], grp)
                    for part in range(2):
                        for a in halves:
                            mm = nc.tensor.transpose(DP[qi][:, (2 * part + a) * P:(2 * part + a + 1) * P],
                                                     ps[:, grp % 2, 2 * qi + part, a * P:(a + 1) * P], ident)
                    mm.then_inc(pt_full[qi], 1)
                for qi in range(2):
                    pe.wait_ge(pt_copied[qi], grp + 1)
                    if qi == 0 and grp:
                        pe.wait_ge(o_ready, grp)
                    for part in range(2):
                        h = 2 * qi + part
                        for a in halves:
                            mm = nc.tensor.matmul(SQ[:, h * HD:(h + 1) * HD], pt[:, grp % 2, h, a, :],
                                                  vtm[:, n - 1 + a, j * HD:(j + 1) * HD],
                                                  start=a == halves[0], stop=a == 1)
                mm.then_inc(o_full, 1)

            def turn(grp):
                pe.wait_ge(o_ready, grp + 1)
                if grp:
                    pe.wait_ge(y_out, grp)
                for qi in range(2):
                    mm = nc.tensor.transpose(ZB[:, qi * P:(qi + 1) * P], ob[:, grp % 2, qi * P:(qi + 1) * P], ident)
                mm.then_inc(ot_full, 1)

            for grp in range(GROUPS_B + 2):
                if grp < GROUPS_B:
                    scores(grp)
                if 1 <= grp <= GROUPS_B:
                    attend(grp - 1)
                if grp >= 2:
                    turn(grp - 2)
                if grp < len(B_SLABS) - B_FIRST:
                    s = SLAB_V + B_FIRST + grp
                    project(pe, s, s % 2)

        def scalar_b(act, own):
            def evacuate(n):
                kind, a = B_SLABS[n]
                dst = {"v": [vch], "k": kd, "q": qb, "g": [yT[:, 4 + m, :] for m in range(4)]}[kind][a]
                for h in range(2):
                    act.wait_ge(proj_full[h], SLAB_V + n + 1)
                    nc.scalar.activation(dst[:, h * HALF:(h + 1) * HALF], PJ[h][:],
                                         ACT.Silu if kind == "g" else ACT.Copy,
                                         scale=HD ** -0.5 if kind == "q" else 1.0).then_inc(proj_free[h], 1)

            for n in range(B_FIRST):
                evacuate(n)
                if n == 0:
                    for b in range(2):
                        act.wait_ge(vt_full, b + 1)
                        nc.scalar.activation(vtm[:, 4 * b:4 * b + 4, :], DP[b][:].rearrange("p (n c) -> p n c", n=4),
                                             ACT.Copy).then_inc(vt_ready, 1)

            def probs(grp):
                n = grp % NC
                lo = P if n == 0 else 0
                v = grp % 2
                act.wait_ge(m_ready, 2 * grp + 2)
                if grp >= 2:
                    act.wait_ge(pt_full[1], grp - 1)
                for h in range(4):
                    nc.scalar.activation(ps[:, v, h, lo:], ps[:, v, h, lo:], ACT.Exp, bias=sm[:, v, 4 + h:5 + h],
                                         accum_out=sm[:, v, 12 + h:13 + h]).then_inc(p_ready, 1)
                nc.scalar.activation(sm[:, v, 16:20], sm[:, v, 8:12], ACT.Exp).then_inc(es_ready, 1)

            def copy_p(grp):
                act.wait_ge(pt_full[1], grp + 1)
                if grp >= 2:
                    act.wait_ge(o_full, grp - 1)
                a = 1 if grp % NC == 0 else 0
                nc.scalar.activation(pt[:, grp % 2, 2:4, a:2, :],
                                     DP[1][:].rearrange("p (h a q) -> p h a q", h=2, a=2)[:, :, a:2, :],
                                     ACT.Copy).then_inc(pt_copied[1], 1)

            for grp in range(GROUPS_B + 1):
                if grp < GROUPS_B:
                    probs(grp)
                if grp:
                    copy_p(grp - 1)
                if grp < len(B_SLABS) - B_FIRST:
                    evacuate(B_FIRST + grp)

        def vector_b(dve, own):
            def row_max(grp):
                j, n = grp // NC, grp % NC
                v = grp % 2
                lo = P if n == 0 else 0
                if grp == 0:
                    dve.wait_ge(scr_in, 16)
                    dve.wait_ge(small_in, 16 * 5)
                if grp >= 2:
                    dve.wait_ge(pt_full[1], grp - 1)
                for part in range(2):
                    dve.wait_ge(sc_full[part], SB + grp + 1)
                    for qi in range(2):
                        h = 2 * qi + part
                        ins = nc.vector.tensor_tensor_reduce(
                            ps[:, v, h, lo:], SC[part][:, qi * 256 + lo:qi * 256 + 256], bias[:, 4 * j + h, lo:], 1.0,
                            sinkb[:, 4 * j + h:4 * j + h + 1], ALU.add, ALU.max, sm[:, v, h:h + 1])
                        if qi:
                            ins.then_inc(sc_free[part], 1)
                        else:
                            own.on(ins)
                dve.wait_ge(sc_free[0], SB + grp + 1)
                dve.wait_ge(sc_free[1], SB + grp + 1)
                own.wait()
                nc.vector.tensor_scalar(sm[:, v, 4:8], sm[:, v, 0:4], -1.0, None, ALU.mult).then_inc(m_ready, 1)
                nc.vector.tensor_tensor(sm[:, v, 8:12], sinkb[:, 4 * j:4 * j + 4], sm[:, v, 0:4],
                                        ALU.subtract).then_inc(m_ready, 1)

            def copy_p(grp):
                dve.wait_ge(pt_full[0], grp + 1)
                if grp >= 2:
                    dve.wait_ge(o_full, grp - 1)
                a = 1 if grp % NC == 0 else 0
                nc.vector.tensor_copy(pt[:, grp % 2, 0:2, a:2, :],
                                      DP[0][:].rearrange("p (h a q) -> p h a q", h=2, a=2)[:, :, a:2, :]
                                      ).then_inc(pt_copied[0], 1)
                v = grp % 2
                dve.wait_ge(es_ready, grp + 1)
                dve.wait_ge(p_ready, 4 * grp + 4)
                own.on(nc.vector.tensor_tensor(sm[:, v, 20:24], sm[:, v, 12:16], sm[:, v, 16:20], ALU.add))
                own.wait()
                own.on(nc.vector.reciprocal(sm[:, v, 20:24], sm[:, v, 20:24]))
                own.wait()
                dve.wait_ge(o_full, grp + 1)
                if grp >= 2:
                    dve.wait_ge(ot_full, grp - 1)
                nc.vector.tensor_tensor(ob[:, v, :].rearrange("p (h c) -> p h c", h=4),
                                        SQ[:, 0:256].rearrange("p (h c) -> p h c", h=4),
                                        each(sm[:, v, 20:24], HD), ALU.mult).then_inc(o_ready, 1)

            def gate(grp):
                j, n = grp // NC, grp % NC
                if n == 0:
                    dve.wait_ge(proj_free[1], SLAB_V + (6 if j == 0 else 11))
                    dve.wait_ge(proj_free[0], SLAB_V + (6 if j == 0 else 11))
                dve.wait_ge(ot_full, grp + 1)
                y = yT[:, 4 + 2 * j:6 + 2 * j, n * P:(n + 1) * P]
                nc.vector.tensor_tensor(y, ZB[:, 0:256].rearrange("p (a t) -> p a t", a=2), y, ALU.mult).then_inc(y_out, 1)

            for grp in range(GROUPS_B + 2):
                if grp < GROUPS_B:
                    row_max(grp)
                if 1 <= grp <= GROUPS_B:
                    copy_p(grp - 1)
                if grp >= 2:
                    gate(grp - 2)

        sqb = [work[:, j * T:(j + 1) * T] for j in range(2)]
        rstd = work[:, 6 * T:7 * T]
        SO = [SB + GROUPS_B, SB + GROUPS_B + 2 + 4 * HEADS_C]
        xin = yT

        def sync_o(sp, layer, w_out):
            base = (SLAB_O0, SLAB_O1)[layer]
            with sp.Fori(0, 4) as i:
                for q in range(2):
                    s = base + q
                    load_slab(sp, at(i, 2, s), s % 2, columns_at(w_out, q * P, i, 2 * P))
            if layer == 0:
                sp.wait_ge(y_split, 8)
                for t in range(NC):
                    sp.dma_start(xin[:, t, :], x[t * P:(t + 1) * P, :]).then_inc(x_again, 16)
                for k in range(KT):
                    for h in range(2):
                        sp.wait_ge(xt_added[h], k + 1)
                    sp.dma_start(stream[k], zT[:, k, :]).then_inc(stream_out, 16)
                sp.wait_ge(stream_out, 16 * KT)
            else:
                for k in range(KT):
                    sp.dma_start(zT[:, k, :], stream[k]).then_inc(stream_in, 16)

        def pool_o(pool, own, layer):
            base = (SLAB_O0, SLAB_O1)[layer]
            for k in range(KT):
                pool.wait_ge(y_hi, 8 * layer + k + 1)
                nc.gpsimd.tensor_tensor(h_lo[:, k, :], yT[:, k, :], h_hi[:, k, :], ALU.subtract).then_inc(y_split, 1)
            with pool.Fori(0, 4) as i:
                own.enter(i, 2)
                for q in range(2):
                    s = base + q
                    split_slab(pool, own, at(i, 2, s), s % 2, at(i, 1, s // 2 + 1))
                own.leave(4)
            if layer == 0:
                for k in range(KT):
                    pool.wait_ge(h_hi_ready, k + 1)
                    nc.gpsimd.tensor_tensor(h_lo[:, k, :], h_stage[k % 2], h_hi[:, k, :],
                                            ALU.subtract).then_inc(h_lo_ready, 1)

        h_stage = [work[:, (2 + j) * T:(3 + j) * T] for j in range(2)]

        def tensor_norm(pe, n, first):
            for k in range(KT):
                pe.wait_ge(sq_ready, 8 * n + k + 1)
                for h in range(2):
                    if k == 0:
                        pe.wait_ge(sc_free[h], first)
                    mm = nc.tensor.matmul(SC[h][:], ones_all[:], sqb[k % 2][:, h * HALF:(h + 1) * HALF],
                                          start=k == 0, stop=k == KT - 1)
                    if k == KT - 1:
                        mm.then_inc(sc_full[h], 1)
                    elif h:
                        mm.then_inc(sq_used, 1)

        def scalar_norm(act, own, n, first, src, ready):
            for k in range(KT):
                for s in ready:
                    act.wait_ge(s, k + 1)
                if k >= 2:
                    act.wait_ge(sq_used, 7 * n + k - 1)
                nc.scalar.activation(sqb[k % 2], src(k), ACT.Square).then_inc(sq_ready, 1)
            for h in range(2):
                act.wait_ge(sc_full[h], first + 1)
                nc.scalar.activation(rstd[:, h * HALF:(h + 1) * HALF], SC[h][:], ACT.Ln, scale=1.0 / D,
                                     bias=eps[:, 0:1]).then_inc(sc_free[h], 1)
            act.wait_ge(sc_free[0], first + 1)
            act.wait_ge(sc_free[1], first + 1)
            nc.scalar.activation(rstd[:], rstd[:], ACT.Exp, scale=-0.5).then_inc(norm_ready, 1)

        def tensor_o(pe, layer):
            base = (SLAB_O0, SLAB_O1)[layer]
            pe.wait_ge(y_split, 8 * layer + 8)
            with pe.Fori(0, 4) as i:
                for q in range(2):
                    project(pe, at(i, 2, base + q), (base + q) % 2)
            tensor_norm(pe, 2 * layer, SO[layer])
            if layer == 0:
                for t in range(NC):
                    if t == 0:
                        pe.wait_ge(x_again, 16 * NC)
                for k in range(KT):
                    for h in range(2):
                        if k:
                            pe.wait_ge(xt_added[h], k)
                        for m in range(4):
                            mm = nc.tensor.transpose(DP[h][:, m * P:(m + 1) * P],
                                                     xin[:, 4 * h + m, k * P:(k + 1) * P], ident)
                        mm.then_inc(xt_full[h], 1)
                tensor_norm(pe, 1, SO[0] + 1)
            else:
                for t in range(NC):
                    for h in range(2):
                        if t:
                            pe.wait_ge(out_copied[h], t)
                        for m in range(4):
                            k = 4 * h + m
                            if t == 0:
                                pe.wait_ge(final_ready, k + 1)
                            mm = nc.tensor.transpose(DP[h][:, m * P:(m + 1) * P], yT[:, k, t * P:(t + 1) * P], ident)
                        mm.then_inc(out_full[h], 1)

        def scalar_o(act, own, layer):
            for k in range(KT):
                nc.scalar.activation(h_hi[:, k, :], yT[:, k, :], ACT.Copy).then_inc(y_hi, 1)
            base = (SLAB_O0, SLAB_O1)[layer]
            z = (zT, yT)[layer]
            act.wait_ge(proj_free[0], base + 8)
            act.wait_ge(proj_free[1], base + 8)
            scalar_norm(act, own, 2 * layer, SO[layer], lambda k: z[:, k, :], ())
            if layer == 0:
                scalar_norm(act, own, 1, SO[0] + 1, lambda k: zT[:, k, :], xt_added)
                for k in range(KT):
                    act.wait_ge(h_ready, k + 1)
                    nc.scalar.activation(h_hi[:, k, :], h_stage[k % 2], ACT.Copy).then_inc(h_hi_ready, 1)
            else:
                for t in range(NC):
                    act.wait_ge(out_full[1], t + 1)
                    if t >= 2:
                        act.wait_ge(out_done[t % 2], 16 * (t // 2))
                    nc.scalar.activation(out_stage[t % 2][:, HALF:T], DP[1][:], ACT.Copy).then_inc(out_copied[1], 1)

        def vector_o(dve, own, layer):
            base = (SLAB_O0, SLAB_O1)[layer]
            z = (zT, yT)[layer]
            if layer == 1:
                dve.wait_ge(y_split, 16)
            with dve.Fori(0, 4) as i:
                for q in range(2):
                    for h in range(2):
                        dve.wait_ge(proj_full[h], at(i, 2, base + q + 1))
                        nc.vector.tensor_scalar(z[:, bass.ds(i * 2 + q, 1), h * HALF:(h + 1) * HALF],
                                                PJ[h][:].rearrange("p (o t) -> p o t", o=1), 1.0, None,
                                                ALU.mult).then_inc(proj_free[h], 1)
            post = (POST0, POST1)[layer] - 44
            if layer == 1:
                dve.wait_ge(stream_in, 16 * KT)
            dve.wait_ge(norm_ready, 2 * layer + 1)
            for k in range(KT):
                own.on(nc.vector.scalar_tensor_tensor(z[:, k, :], z[:, k, :], oth[:, post + k:post + k + 1], rstd,
                                                      ALU.mult, ALU.mult))
                own.wait()
                if layer == 0:
                    for h in range(2):
                        dve.wait_ge(xt_full[h], k + 1)
                        nc.vector.tensor_tensor(z[:, k, h * HALF:(h + 1) * HALF], z[:, k, h * HALF:(h + 1) * HALF],
                                                DP[h][:], ALU.add).then_inc(xt_added[h], 1)
                else:
                    nc.vector.tensor_tensor(z[:, k, :], z[:, k, :], zT[:, k, :], ALU.add).then_inc(final_ready, 1)
            if layer == 0:
                dve.wait_ge(norm_ready, 2)
                for k in range(KT):
                    if k >= 2:
                        dve.wait_ge(h_lo_ready, k - 1)
                    nc.vector.scalar_tensor_tensor(h_stage[k % 2], zT[:, k, :], oth[:, PRE1 - 44 + k:PRE1 - 43 + k], rstd,
                                                   ALU.mult, ALU.mult).then_inc(h_ready, 1)
            else:
                for t in range(NC):
                    dve.wait_ge(out_full[0], t + 1)
                    if t >= 2:
                        dve.wait_ge(out_done[t % 2], 16 * (t // 2))
                    nc.vector.tensor_copy(out_stage[t % 2][:, 0:HALF], DP[0][:]).then_inc(out_copied[0], 1)

        out_stage = [work[:, (4 + j) * T:(5 + j) * T] for j in range(2)]

        def sync_out(sp):
            for t in range(NC):
                sp.wait_ge(out_copied[0], t + 1)
                sp.wait_ge(out_copied[1], t + 1)
                sp.dma_start(out[t * P:(t + 1) * P, :], out_stage[t % 2]).then_inc(out_done[t % 2], 16)
            sp.wait_ge(out_done[0], 16 * NC // 2)
            sp.wait_ge(out_done[1], 16 * NC // 2)

        qs2, vc2, fc2, og2 = ([zT[:, 4 * v + n, :] for v in range(2)] for n in range(4))
        oc2 = [work[:, n * T:(n + 1) * T] for n in range(2)]
        ec, sp_, gcm, osq, orn = (work[:, n * T:(n + 1) * T] for n in range(2, 7))
        fac2 = work[:, 7 * T:7 * T + 64].rearrange("p (v k n) -> p v k n", v=2, k=2)
        masks_room = cst[:, CL:CL + T]
        tmc = masks_room[:, 0:512].rearrange("p (j n) -> p j n", j=2)
        sst = masks_room[:, 512:1024].rearrange("p (j n) -> p j n", j=4)
        stc, sc2_t = (yT[:, 7, n * 256:(n + 1) * 256].rearrange("p (j n) -> p j n", j=2) for n in range(2))
        C_COLS = (D, 0, 2 * D, 3 * D)
        H = C // 2
        INC = [SQ, DP[0]]
        NORM = DP[1]
        NS = 2 * NC
        SCC = SO[0] + 2
        CB = 4

        def nth(i, o, per, n):
            return at(i, 2 * per, o * per + n)

        def heads(eng, own, head, per):
            head(0, 0, first=True)
            with eng.Fori(0, HEADS_C // 2 - 1) as i:
                if own:
                    own.enter(i, per)
                head(i, 1)
                head(i, 2)
                if own:
                    own.leave(HEADS_C // 2 - 1)
            head(HEADS_C // 2 - 1, 1, last=True)

        def sync_c(sp):
            first = C_COLS[0] // P
            with sp.Fori(first, first + HEADS_C) as i:
                for q, col in enumerate(C_COLS):
                    load_slab(sp, at(i, 4, SLAB_C + q - 4 * first), q % 2, columns_at(w_in1, col - C_COLS[0], i, P))

        def pool_c(pool, own):
            with pool.Fori(0, HEADS_C) as i:
                own.enter(i, 4)
                for q in range(4):
                    split_slab(pool, own, at(i, 4, SLAB_C + q), q % 2, at(i, 2, (SLAB_C + q) // 2 + 1))
                own.leave(HEADS_C)

        def tensor_c(pe):
            def norm(i, o, h):
                if h == 0:
                    pe.wait_ge(osq_ready, nth(i, o, 1, 1))
                else:
                    pe.wait_ge(norm_free, nth(i, o, 2, 1))
                nc.tensor.matmul(NORM[:], ones_all[:], osq[:, h * HALF:(h + 1) * HALF], start=True,
                                 stop=True).then_inc(norm_full, 1)

            def head(i, o, first=False, last=False):
                v = o % 2
                qs, vc, fc = qs2[v], vc2[v], fc2[v]
                pe.wait_ge(kc_ready, nth(i, o, 1, 1))
                pe.wait_ge(qc_ready, nth(i, o, 1, 1))
                pe.wait_ge(proj_free[0], nth(i, o, 4, SLAB_C + 3))
                pe.wait_ge(proj_free[1], nth(i, o, 4, SLAB_C + 3))

                def turn(c):
                    cs = slice(c * C, (c + 1) * C)
                    j = c % 2
                    pe.wait_ge(sc_free[j], nth(i, o, CB, SCC + c // 2))
                    nc.tensor.transpose(SC[j][:, 0:P], vc[:, cs], ident)
                    nc.tensor.transpose(SC[j][:, P:2 * P], fc[:, cs], ident)
                    for b in range(2):
                        hs = slice(c * C + b * H, c * C + (b + 1) * H)
                        mm = nc.tensor.matmul(SC[j][b * H:(b + 1) * H, 256 + b * H:256 + (b + 1) * H], fc[:, hs], qs[:, hs],
                                              start=True, stop=True)
                    mm.then_inc(sc_full[j], 1)

                def ahead(c, part):
                    if not last:
                        project_part(pe, nth(i, o, 4, SLAB_C + 4 + c // 2), c // 2 % 2, c % 2, 8 * part, 8)

                turn(0)
                for c in range(NC):
                    j = c % 2
                    ahead(c, 0)
                    if c + 1 < NC:
                        turn(c + 1)
                    if c == 1 and not first:
                        norm(i, o - 1, 0)
                    pe.wait_ge(tc_ready, nth(i, o, NC, c + 1))
                    pe.wait_ge(sc_state, nth(i, o, NS, 2 * c + 1))
                    for b in range(2):
                        hb = slice(b * H, (b + 1) * H)
                        nc.tensor.matmul(INC[b][:, 0:P], tmc[hb, j, P:2 * P], tmc[hb, j, 0:P], start=True,
                                         stop=True).then_inc(inc_full[b], 1)
                    ahead(c, 1)
                    pe.wait_ge(sc_free[j], nth(i, o, CB, SCC + c // 2 + 1))
                    pe.wait_ge(oc_copied, nth(i, o, NC, c + 1))
                    nc.tensor.matmul(ZB[:, 0:P], tmc[:, j, 0:P], stc[:, j, :], start=True, stop=True)
                    for b in range(2):
                        pe.wait_ge(sc_state, nth(i, o, NS, 2 * c + 1 + b))
                        mm = nc.tensor.matmul(ZB[:, b * H:(b + 1) * H], sst[:, (2 * c + b) % 4, :],
                                              qs[:, c * C + b * H:c * C + (b + 1) * H],
                                              start=False, stop=True, skip_group_check=True)
                    mm.then_inc(oc_full, 1)
                    ahead(c, 2)
                    if c == 1 and not first:
                        norm(i, o - 1, 1)

            for q in range(4):
                project(pe, SLAB_C + q, q % 2)
            heads(pe, None, head, 0)
            for h in range(2):
                norm(HEADS_C // 2 - 1, 1, h)

        def scalar_c(act, own):
            nc.scalar.activation(eps[:, 3:4], eps[:, 3:4], ACT.Copy).then_inc(oc_copied, 1)
            act.wait_ge(lb_step, 2)
            nc.scalar.activation(lbp[:, 2:4, :], lbp[:, 2:4, :], ACT.Exp).then_inc(lb_exp, 1)
            act.wait_ge(lb_step, 3)
            nc.scalar.activation(lbp[:, 5, :], lbp[:, 5, :], ACT.Ln).then_inc(lb_exp, 1)

            def logs(i, o):
                for h in range(2):
                    act.wait_ge(proj_free[h], nth(i, o, 4, SLAB_C + 1))
                act.wait_ge(lb_ready, nth(i, o, 1, 1))
                own.on(nc.scalar.activation(ec, fc2[o % 2], ACT.Exp, scale=-1.0))
                own.wait()
                nc.scalar.activation(sp_, ec, ACT.Ln, bias=1.0).then_inc(ln_ready, 1)
                nc.scalar.activation(ec, ec, ACT.Ln, bias=1.0, scale=lbc[:, 0:1]).then_inc(ln_ready, 1)

            def query(i, o, h):
                act.wait_ge(proj_full[h], nth(i, o, 4, SLAB_C + 2))
                nc.scalar.activation(qs2[o % 2][:, h * HALF:(h + 1) * HALF], PJ[h][:], ACT.Silu).then_inc(proj_free[h], 1)

            def gate(i, o):
                for h in range(2):
                    act.wait_ge(proj_free[h], nth(i, o, 4, SLAB_C + 4))
                nc.scalar.activation(og2[o % 2], og2[o % 2], ACT.Silu).then_inc(gate_c_ready, 1)

            def decays(i, o, part):
                if part == 0:
                    act.wait_ge(gcc_ready, nth(i, o, 2, 1))
                    nc.scalar.activation(gcm, ec, ACT.Exp).then_inc(expc_ready, 1)
                    nc.scalar.activation(fac2[:, o % 2, 1, 0:NS - 1], fac2[:, o % 2, 0, 0:NS - 1],
                                         ACT.Exp).then_inc(expc_ready, 1)
                else:
                    act.wait_ge(gcc_ready, nth(i, o, 2, 2))
                    nc.scalar.activation(fc2[o % 2], fc2[o % 2], ACT.Exp, scale=-1.0, bias=lbc[:, 1:2]).then_inc(kc_ready, 1)

            def squares(i, o):
                act.wait_ge(oc_copied, nth(i, o, NC, NC + 1))
                nc.scalar.activation(osq, oc2[o % 2], ACT.Square).then_inc(osq_ready, 1)

            def norm(i, o, h):
                if h == 0:
                    act.wait_ge(head_done, nth(i, o, 1, 1))
                act.wait_ge(norm_full, nth(i, o, 2, h + 1))
                nc.scalar.activation(orn[:, h * HALF:(h + 1) * HALF], NORM[:], ACT.Ln, scale=1.0 / C,
                                     bias=eps[:, 0:1]).then_inc(norm_free, 1)
                if h:
                    act.wait_ge(norm_free, nth(i, o, 2, 2))
                    nc.scalar.activation(orn, orn, ACT.Exp, scale=-0.5).then_inc(orn_ready, 1)

            def head(i, o, first=False, last=False):
                if not first:
                    squares(i, o - 1)
                for c in range(NC):
                    j = c % 2
                    act.wait_ge(sc_full[j], nth(i, o, CB, SCC + c // 2 + 1))
                    nc.scalar.activation(tmc[:, j, :], SC[j][:, 0:256], ACT.Copy).then_inc(tc_ready, 1)
                    if c == 2 and not first:
                        for h in range(2):
                            norm(i, o - 1, h)
                    if c == 3:
                        if not last:
                            logs(i, o + 1)
                        nc.scalar.preload_act_table(ACT.Silu)
                        if not last:
                            query(i, o + 1, 0)
                        gate(i, o)
                    if c == 4 and not last:
                        query(i, o + 1, 1)
                        nc.scalar.preload_act_table_set("natural_log_exp_and_others")
                    if c == 6 and not last:
                        decays(i, o + 1, 0)
                    if c == 7 and not last:
                        decays(i, o + 1, 1)
                    act.wait_ge(oc_full, nth(i, o, NC, c + 1))
                    nc.scalar.activation(oc2[o % 2][:, c * C:(c + 1) * C], ZB[:, 0:P], ACT.Copy).then_inc(oc_copied, 1)

            logs(0, 0)
            nc.scalar.preload_act_table(ACT.Silu)
            for h in range(2):
                query(0, 0, h)
            nc.scalar.preload_act_table_set("natural_log_exp_and_others")
            for part in range(2):
                decays(0, 0, part)
            heads(act, own, head, 2)
            nc.scalar.preload_act_table_set("natural_log_exp_and_others")
            squares(HEADS_C // 2 - 1, 1)
            for h in range(2):
                norm(HEADS_C // 2 - 1, 1, h)

        def vector_c(dve, own):
            lb0, lb1 = oth[:, LB0 - 44:LB0 - 36], oth[:, LB1 - 44:LB1 - 36]
            own.on(nc.vector.tensor_tensor(lbp[:, 1, :], lb0, lb1, ALU.max))
            own.wait()
            nc.vector.tensor_tensor(lbp[:, 2, :], lb0, lbp[:, 1, :], ALU.subtract).then_inc(lb_step, 1)
            nc.vector.tensor_tensor(lbp[:, 3, :], lb1, lbp[:, 1, :], ALU.subtract).then_inc(lb_step, 1)
            dve.wait_ge(lb_exp, 1)
            own.on(nc.vector.tensor_tensor(lbp[:, 1, :], lbp[:, 2, :], lbp[:, 3, :], ALU.add))
            own.wait()
            own.on(nc.vector.reciprocal(lbp[:, 1, :], lbp[:, 1, :]))
            own.wait()
            own.on(nc.vector.tensor_tensor(lbp[:, 4, :], lbp[:, 3, :], lbp[:, 1, :], ALU.mult))
            nc.vector.tensor_tensor(lbp[:, 5, :], lbp[:, 2, :], lbp[:, 1, :], ALU.mult).then_inc(lb_step, 1)
            own.on(nc.vector.memset(stc, 0.0))
            nc.vector.memset(sc2_t, 0.0).then_inc(head_done, 1)
            own.on(nc.vector.memset(reset[:], 1.0))
            own.wait()
            own.on(nc.vector.memset(reset[:].rearrange("p (c t) -> p c t", t=H)[:, :, 0:1], 0.0))
            own.wait()
            dve.wait_ge(lb_exp, 2)

            def evacuate(i, o, q, h):
                dst = (fc2, None, vc2, og2)[q][o % 2][:, h * HALF:(h + 1) * HALF]
                dve.wait_ge(proj_full[h], nth(i, o, 4, SLAB_C + q + 1))
                if q == 0:
                    nc.vector.tensor_scalar(dst, PJ[h][:], -43.0, None, ALU.max).then_inc(proj_free[h], 1)
                else:
                    nc.vector.tensor_scalar(dst, PJ[h][:], 1.0, None, ALU.mult).then_inc(proj_free[h], 1)

            def bounds(i, o):
                n = bass.ds(at(i, 2, o), 1)
                nc.vector.tensor_scalar(lbc[:, 0:2].rearrange("p (k o) -> p k o", o=1), lbp[:, 4:6, n], 1.0,
                                        None, ALU.mult).then_inc(lb_ready, 1)

            def sums(i, o):
                dve.wait_ge(ln_ready, nth(i, o, 2, 2))
                own.on(nc.vector.tensor_tensor(ec, ec, sp_, ALU.subtract))
                own.on(nc.vector.tensor_tensor(fc2[o % 2], fc2[o % 2], sp_, ALU.add))
                own.wait()
                for h in range(2):
                    own.on(nc.vector.tensor_tensor_scan(gcm[:, h * HALF:(h + 1) * HALF], reset[:],
                                                        ec[:, h * HALF:(h + 1) * HALF], 0.0, ALU.mult, ALU.add))
                own.wait()

            def centre(i, o):
                g3 = gcm.rearrange("p (c t) -> p c t", c=NS)
                e3 = ec.rearrange("p (c t) -> p c t", c=NS)
                mid = H // 2 - 1
                own.on(nc.vector.tensor_tensor(e3, g3, g3[:, :, mid:mid + 1].broadcast_to([P, NS, H]), ALU.subtract))
                own.wait()
                nc.vector.tensor_tensor(fac2[:, o % 2, 0, 0:NS - 1], e3[:, 0:NS - 1, H - 1:H].rearrange("p c o -> p (c o)"),
                                        g3[:, 1:NS, mid:mid + 1].rearrange("p c o -> p (c o)"),
                                        ALU.add).then_inc(gcc_ready, 1)
                nc.vector.tensor_tensor(fc2[o % 2], fc2[o % 2], ec, ALU.add).then_inc(gcc_ready, 1)

            def decay_queries(i, o):
                dve.wait_ge(expc_ready, nth(i, o, 2, 2))
                nc.vector.tensor_tensor(qs2[o % 2], qs2[o % 2], gcm, ALU.mult).then_inc(qc_ready, 1)

            def finish(i, o):
                oc, og = oc2[o % 2], og2[o % 2]
                dve.wait_ge(orn_ready, nth(i, o, 1, 1))
                dve.wait_ge(gate_c_ready, nth(i, o, 1, 1))
                own.on(nc.vector.scalar_tensor_tensor(oc, oc, oth[:, CN - 44:CN - 43], orn, ALU.mult, ALU.mult))
                own.wait()
                nc.vector.tensor_tensor(yT[:, bass.ds(at(i, 2, o), 1), :], oc.rearrange("p (o t) -> p o t", o=1),
                                        og.rearrange("p (o t) -> p o t", o=1), ALU.mult).then_inc(head_done, 1)

            def head(i, o, first=False, last=False):
                fac = fac2[:, o % 2, 1, :]
                dve.wait_ge(oc_copied, nth(i, o, NC, 1))
                nc.vector.memset(sst[:, 0, :], 0.0).then_inc(sc_state, 1)
                for c in range(NC):
                    j = c % 2
                    dve.wait_ge(sc_full[j], nth(i, o, CB, SCC + c // 2 + 1))
                    dve.wait_ge(tc_ready, nth(i, o, NC, c + 1))
                    own.on(nc.vector.tensor_tensor(stc[0:64, j, 0:64], SC[j][0:64, 256:320], cst[0:64, CM + P:CM + P + 64],
                                                   ALU.mult))
                    nc.vector.tensor_tensor(stc[64:128, j, 64:128], SC[j][64:128, 320:384],
                                            cst[64:128, CM + P + 64:CM + 2 * P], ALU.mult).then_inc(sc_free[j], 1)
                    for b in range(2):
                        n = 2 * c + b
                        if n == NS - 1:
                            break
                        dve.wait_ge(inc_full[b], nth(i, o, NC, c + 1))
                        own.on(nc.vector.tensor_scalar(sc2_t[:, b, :], INC[b][:, 0:P], fac[:, n:n + 1], None, ALU.mult))
                        own.wait()
                        dve.wait_ge(sc_state, nth(i, o, NS, n + 1))
                        if c:
                            dve.wait_ge(oc_full, nth(i, o, NC, c))
                        nc.vector.scalar_tensor_tensor(sst[:, (n + 1) % 4, :], sst[:, n % 4, :], fac[:, n:n + 1],
                                                       sc2_t[:, b, :], ALU.mult, ALU.add).then_inc(sc_state, 1)
                    if not last:
                        if c == 1:
                            dve.wait_ge(kc_ready, nth(i, o, 1, 1))
                            bounds(i, o + 1)
                        if c in (1, 2):
                            evacuate(i, o + 1, 0, c - 1)
                        if c == 4:
                            sums(i, o + 1)
                        if c == 5:
                            centre(i, o + 1)
                        if c in (5, 6):
                            evacuate(i, o + 1, 2, c - 5)
                        if c == 6:
                            decay_queries(i, o + 1)
                        if c == 7:
                            for h in range(2):
                                evacuate(i, o + 1, 3, h)
                    if c == 3 and not first:
                        finish(i, o - 1)

            bounds(0, 0)
            for h in range(2):
                evacuate(0, 0, 0, h)
            sums(0, 0)
            for h in range(2):
                evacuate(0, 0, 2, h)
            centre(0, 0)
            decay_queries(0, 0)
            for h in range(2):
                evacuate(0, 0, 3, h)
            heads(dve, own, head, 2 * (NC + NS - 1 + 5 + 1))
            finish(HEADS_C // 2 - 1, 1)

        block = ctx.enter_context(nc.Block())

        @block.sync
        def _(sp):
            sync_0(sp)
            phase_end(sp, 0)
            sync_a(sp)
            phase_end(sp, 1)
            sync_b(sp)
            phase_end(sp, 2)
            sync_o(sp, 0, w_out0)
            phase_end(sp, 3)
            sync_c(sp)
            phase_end(sp, 4)
            sync_o(sp, 1, w_out1)
            sync_out(sp)

        @block.gpsimd
        def _(pool):
            own = Steps(pool, own_pool)
            pool_0(pool, own)
            phase_end(pool, 0)
            pool_a(pool, own)
            phase_end(pool, 1)
            pool_b(pool, own)
            phase_end(pool, 2)
            pool_o(pool, own, 0)
            phase_end(pool, 3)
            pool_c(pool, own)
            phase_end(pool, 4)
            pool_o(pool, own, 1)

        @block.tensor
        def _(pe):
            tensor_0(pe)
            phase_end(pe, 0)
            tensor_a(pe)
            phase_end(pe, 1)
            tensor_b(pe)
            phase_end(pe, 2)
            tensor_o(pe, 0)
            phase_end(pe, 3)
            tensor_c(pe)
            phase_end(pe, 4)
            tensor_o(pe, 1)

        @block.scalar
        def _(act):
            own = Steps(act, own_act)
            scalar_0(act, own)
            phase_end(act, 0)
            scalar_a(act, own)
            phase_end(act, 1)
            scalar_b(act, own)
            phase_end(act, 2)
            scalar_o(act, own, 0)
            phase_end(act, 3)
            scalar_c(act, own)
            phase_end(act, 4)
            scalar_o(act, own, 1)

        @block.vector
        def _(dve):
            own = Steps(dve, own_dve)
            vector_0(dve, own)
            phase_end(dve, 0)
            vector_a(dve, own)
            phase_end(dve, 1)
            vector_b(dve, own)
            phase_end(dve, 2)
            vector_o(dve, own, 0)
            phase_end(dve, 3)
            vector_c(dve, own)
            phase_end(dve, 4)
            vector_o(dve, own, 1)


_INS = ["x", "rel_bias_table", "lower_bounds", "l0_pre_norm", "l0_post_norm", "l0_w_in", "l0_w_out",
        "a_mu", "a_w0", "a_w2", "a_a0", "a_a2", "a_k_k", "a_k_a", "a_r_k", "a_ln_w", "a_ln_b", "b_sinks",
        "l1_pre_norm", "l1_post_norm", "l1_w_in", "l1_w_out", "c_norm_w"]


def kernel(**inputs):
    import concourse.bacc as bacc
    from concourse.bass_utils import run_bass_kernel_spmd

    nc = bacc.Bacc("TRN2", target_bir_lowering=False, num_devices=1)
    arrays = {name: np.ascontiguousarray(inputs[name]) for name in _INS}
    arrays["x"] = arrays["x"].reshape(T, D)
    arrays["constants"] = constants()
    arrays["buckets"] = bucket_table()
    args = [nc.dram_tensor(f"in_{name}", a.shape, F32, kind="ExternalInput").ap() for name, a in arrays.items()]
    args.append(nc.dram_tensor("bias_rows", (P, 8, 384), F32).ap())
    args.append(nc.dram_tensor("stream", (KT, P, T), F32).ap())
    out = nc.dram_tensor("out_0", (T, D), F32, kind="ExternalOutput").ap()
    trunk(nc, *args, out)
    r = run_bass_kernel_spmd(nc, [{f"in_{name}": a for name, a in arrays.items()}], core_ids=[0])
    return r.results[0]["out_0"].reshape(1, T, D)
```

```python
from contextlib import ExitStack

import numpy as np

import concourse.bass as bass
from concourse import mybir

ALU = mybir.AluOpType
ACT = mybir.ActivationFunctionType
F32 = mybir.dt.float32
F32R = mybir.dt.float32r

P = 128
D = 1024
T = 1024
KT = D // P
HALF = 512
C = 128
NC = T // C
HD = 64
PAIRS = 4
LEVELS = 7
LORA = 64
NORM_EPS = 1e-6
GN_EPS = 64e-5
DECAY = float(np.exp(-0.5))
BUCKETS = 32
A_COLS = 2112
COL_R, COL_K, COL_V, COL_LORA, COL_AG = 0, 512, 1024, 1536, 1600
COL_Q, COL_BK, COL_BV, COL_BG = A_COLS, A_COLS + 512, A_COLS + 640, A_COLS + 768
KV = 2
HEADS_C = 8
NEG = -1e30

SLAB_LORA = 0
SLAB_A = 1
SLAB_B = SLAB_A + 4 * PAIRS
SLAB_O0 = SLAB_B + 1 + 5 * KV
SLAB_C = SLAB_O0 + 8
SLAB_O1 = SLAB_C + 4 * HEADS_C

RAW_KINDS = 11
MU, W0, A0, KK, KA, RK, LNW, LNB = 0, 4, 5, 6, 7, 8, 9, 10
OMU, W0H, A0H, KAH, OKAH = 11, 15, 16, 17, 18
KINDS = 19
PRE0, POST0, PRE1, POST1, LB0, LB1, CN, MUL = 44, 52, 60, 68, 76, 84, 92, 93
ROWS = 94

CI, CO64, CM, CL, CN7 = 0, 128, 256, 768, 896
CONSTS = CN7 + 128 * LEVELS


def constants():
    s = np.arange(P)[:, None]
    t = np.arange(P)[None, :]
    c = np.zeros((P, CONSTS), np.float32)
    c[:, CI:CI + P] = s == t
    c[:, CO64:CO64 + P] = s // HD == t // HD
    for q in range(4):
        c[:, CM + P * q:CM + P * (q + 1)] = (s < t) if q % 2 == 0 else (s <= t)
    c[:, CL:CL + P] = s > t
    for k in range(LEVELS):
        b = 1 << k
        m = (s // (2 * b) == t // (2 * b)) & ((s // b) % 2 == 0) & ((t // b) % 2 == 1)
        c[:, CN7 + P * k:CN7 + P * (k + 1)] = -1.0 * m
    return c


def bucket_table():
    c = np.zeros((BUCKETS, 768), np.float32)
    half = BUCKETS // 2
    c[:, 384:768] = NEG
    for m in range(128, 256):
        dist = 255 - m
        far = half + int(np.log(np.float32(max(dist, 1)) / half) / np.log(128 / half) * half)
        c[dist if dist < half else min(far, BUCKETS - 1), m] = 1.0
        c[:, 384 + m] = 0.0
    return c


class Steps:

    def __init__(self, eng, sem):
        self.eng, self.sem, self.n, self.i, self.per, self.start = eng, sem, 0, None, 0, 0

    def on(self, ins):
        ins.then_inc(self.sem, 1)
        self.n += 1

    def wait(self):
        self.eng.wait_ge(self.sem, self.n if self.i is None else self.i * self.per + self.n)

    def enter(self, i, per):
        self.i, self.per, self.start = i, per, self.n

    def leave(self, times):
        assert self.n - self.start == self.per, (self.n - self.start, self.per)
        self.n, self.i = self.start + self.per * times, None


def trunk(nc, x, table, lbs, pre0, post0, w_in0, w_out0, mu, w0, w2, a0, a2, k_k, k_a, r_k, ln_w,
          ln_b, sinks, pre1, post1, w_in1, w_out1, c_norm, cst_in, buckets, scratch, stream, out):
    with ExitStack() as ctx:
        def sb(name, shape, dt=F32):
            return ctx.enter_context(nc.sbuf_tensor(name, shape, dt))

        def sem(name):
            return ctx.enter_context(nc.semaphore(name))

        bank = [ctx.enter_context(nc.psum_tensor(f"bank{i}", [P, HALF], F32)) for i in range(8)]
        PJ, SC, ZB, DP, SQ = bank[0:2], bank[2:4], bank[4], bank[5:7], bank[7]

        h_hi = sb("h_hi", [P, KT, T], F32R)
        h_lo = sb("h_lo", [P, KT, T], F32R)
        yT = sb("yT", [P, KT, T])
        zT = sb("zT", [P, KT, T])
        w_raw = sb("w_raw", [P, 2, KT, P])
        w_hi = sb("w_hi", [P, 2, KT, P], F32R)
        w_lo = sb("w_lo", [P, 2, KT, P], F32R)
        cst = sb("cst", [P, CONSTS])
        work = sb("work", [P, 8488])
        par_raw = work[0:ROWS, 128:256]
        par = sb("par", [P, KINDS, 4])
        oth = sb("oth", [P, ROWS - 44])
        lbp = sb("lbp", [P, 6, 8])
        pp = sb("pp", [P, KINDS])
        rms = sb("rms", [P, 16])
        lw = sb("lw", [LORA, HALF])
        lwp = sb("lwp", [LORA, P])
        rkm = sb("rkm", [P, P])
        eps = sb("eps", [P, 4])
        fac = sb("fac", [P, 2, 16])
        xr = sb("xr", [P, HALF], F32R)
        dpr = sb("dpr", [P, 2 * HALF], F32R)
        lmr = sb("lmr", [P, HALF], F32R)
        ident_r = sb("ident_r", [P, P], F32R)
        pn = sb("pn", [P, KINDS])
        ln = sb("ln", [P, 2])
        sinkb = sb("sinkb", [P, 8])
        tb = sb("tb", [BUCKETS, 8])
        soft = sb("soft", [P, 2, 24])
        lbc = sb("lbc", [P, 2])
        ones_all = sb("ones_all", [P, P])
        reset = sb("reset", [P, HALF])
        ident = cst[:, CI:CI + P]
        ones64 = cst[:, CO64:CO64 + P]

        own_act, own_dve, own_pool = (sem(f"own_{e}") for e in ("act", "dve", "pool"))
        phase_done = sem("phase_done")
        par_zeroed, const_in, par_in, small_in = (sem(n) for n in ("par_zeroed", "const_in", "par_in", "small_in"))
        x_in = [sem(f"x_in{i}") for i in range(2)]
        w_in = [sem(f"weights_in{i}") for i in range(2)]
        w_split = sem("weights_split")
        proj_full = [sem(f"proj_full{i}") for i in range(2)]
        proj_free = [sem(f"proj_free{i}") for i in range(2)]
        sc_full = [sem(f"sc_full{i}") for i in range(2)]
        sc_free = [sem(f"sc_free{i}") for i in range(2)]
        par_full, bias_full, bias_row, scr_in, scr_out = (
            sem(n) for n in ("par_full", "bias_full", "bias_row", "scr_in", "scr_out"))
        par_ready, eps_ready = sem("par_ready"), sem("eps_ready")
        rstd_ready, xn_ready, hi_ready, lo_ready = (sem(n) for n in ("rstd_ready", "xn_ready", "hi_ready", "lo_ready"))
        pp_ready, lwp_ready, rkm_ready, mix_scaled, lora_ready, gate_ready = (
            sem(n) for n in ("pp_ready", "lwp_ready", "rkm_ready", "mix_scaled", "lora_ready", "gate_ready"))
        ksq_ready, gc_ready, exp_ready, rn_ready, kk_ready, t_ready, kp_ready, kq_ready, rk_ready, ab_ready = (
            sem(n) for n in ("ksq_ready", "gc_ready", "exp_ready", "rn_ready", "kk_ready", "t_ready",
                             "kp_ready", "kq_ready", "rk_ready", "ab_ready"))
        z_full, lm_ready, xt_ready = sem("z_full"), sem("lm_ready"), sem("xt_ready")
        dp_full = [sem(f"dp_full{i}") for i in range(2)]
        dp_copied = sem("dp_copied")
        rhs_full, nr_ready, sa_full, sa_ready, state_ready = (
            sem(n) for n in ("rhs_full", "nr_ready", "sa_full", "sa_ready", "state_ready"))
        vt_full, vt_ready, m_ready, p_ready, es_ready, o_full, o_ready, ot_full, y_out = (
            sem(n) for n in ("vt_full", "vt_ready", "m_ready", "p_ready", "es_ready", "o_full", "o_ready", "ot_full", "y_out"))
        pt_full = [sem(f"pt_full{i}") for i in range(2)]
        pt_copied = [sem(f"pt_copied{i}") for i in range(2)]
        y_hi, y_split, x_again, h_ready, h_hi_ready, h_lo_ready, sq_ready, sq_used, norm_ready, final_ready = (
            sem(n) for n in ("y_hi", "y_split", "x_again", "h_ready", "h_hi_ready", "h_lo_ready", "sq_ready",
                             "sq_used", "norm_ready", "final_ready"))
        xt_full, xt_added, out_full, out_copied, out_done = (
            [sem(f"{n}{i}") for i in range(2)] for n in ("xt_full", "xt_added", "out_full", "out_copied", "out_done"))
        lb_step, lb_exp, lb_ready, ln_ready, gcc_ready, expc_ready, kc_ready, qc_ready = (
            sem(n) for n in ("lb_step", "lb_exp", "lb_ready", "ln_ready", "gcc_ready", "expc_ready", "kc_ready", "qc_ready"))
        inc_full = [sem(f"inc_full{i}") for i in range(2)]
        tc_ready, oc_full, oc_copied, sc_state, osq_ready, orn_ready = (
            sem(n) for n in ("tc_ready", "oc_full", "oc_copied", "sc_state", "osq_ready", "orn_ready"))
        head_done = sem("head_done")
        z_sq_ready, z_sum_ready, h_lo_odd, z_scaled, final_odd = (
            sem(n) for n in ("z_sq_ready", "z_sum_ready", "h_lo_odd", "z_scaled", "final_odd"))
        norm_full, norm_free, gate_c_ready, stream_out, stream_in = (
            sem(n) for n in ("norm_full", "norm_free", "gate_c_ready", "stream_out", "stream_in"))
        ysq_ready, ynorm_ready = sem("ysq_ready"), sem("ynorm_ready")
        pair_done = sem("pair_done")
        pn_ready, lmr_ready, corr_full, pf_ready, ident_ready = (
            sem(n) for n in ("pn_ready", "lmr_ready", "corr_full", "pf_ready", "ident_ready"))

        def phase_end(eng, k, meanwhile=None):
            eng.drain().then_inc(phase_done, 1)
            if meanwhile:
                meanwhile(eng)
            eng.wait_ge(phase_done, 3 * (k + 1))

        xt = [zT[:, j, :] for j in range(2)]
        xn = [zT[:, 2 + j, :] for j in range(2)]
        hf = [zT[:, 4 + j, :].rearrange("p (k t) -> p k t", k=KT) for j in range(2)]
        bk = zT[0:BUCKETS, 6, 0:768]
        brow = zT[0:8, 7, 0:384]
        stage = yT[:, 4:8, :]
        rs, ks, vs, gs = (yT[:, 4 + n, :] for n in range(4))
        lora = yT[0:LORA, 3, :]
        scm = [zT[:, 0:2, :].rearrange("p a (b t) -> p (a b) t", b=2),
               work[:, 1032:1032 + 4 * HALF].rearrange("p (b t) -> p b t", b=4)]
        vtm_a = zT[:, 2, :].rearrange("p (n c) -> p n c", n=NC)
        gb, bb, kt = (zT[:, n, :] for n in (3, 4, 7))
        ar = zT[:, 5:7, :]
        u = work[:, 0:T + 1]
        gc = work[:, 1032:2064].rearrange("p (c t) -> p c t", c=NC)
        ysq = work[:, 1032:1032 + T]
        rk = ysq
        kkb = work[:, 2064:2064 + T]
        ee = work[:, 3096:4128].rearrange("p (c t) -> p c t", c=NC)
        ysb = work[:, 3096:3096 + T]
        ldb, gcum, em = (work[:, 4128 + n * T:4128 + (n + 1) * T] for n in range(3))
        tmb = [ldb[:, n * HALF:(n + 1) * HALF].rearrange("p (j t) -> p j t", j=2) for n in range(2)]
        pf = gcum.rearrange("p (g t) -> p g t", g=2)
        rest = work[:, 4128 + 3 * T:]
        nr = rest[:, 0:256].rearrange("p (j n) -> p j n", j=2)
        sa = rest[:, 256:512].rearrange("p (j n) -> p j n", j=2)
        st, st2 = rest[:, 512:640], rest[:, 640:768]
        lm = rest[:, 768:1280]

        def dpt(un):
            d0 = un // 2 * HALF + un % 2 * 256
            return dpr[:, d0:d0 + P], dpr[:, d0 + P:d0 + 2 * P]

        def load_slab(sp, s, slot, src):
            if not (isinstance(s, int) and s < 2):
                sp.wait_ge(w_split, s - 1)
            sp.dma_start(w_raw[:, slot, :, 0:src.shape[-1]], src).then_inc(w_in[slot], 16)

        def split_slab(pool, own, s, slot, uses, n=P):
            pool.wait_ge(w_in[slot], uses * 16 + 16)
            if not (isinstance(s, int) and s < 2):
                pool.wait_ge(proj_full[1], s - 1)
            own.on(nc.gpsimd.tensor_tensor(w_hi[:, slot, :, 0:n], w_raw[:, slot, :, 0:n],
                                           zeros[:].rearrange("p (a b) -> p a b", a=1).broadcast_to([P, KT, n]), ALU.add))
            own.wait()
            nc.gpsimd.tensor_tensor(w_lo[:, slot, :, 0:n], w_raw[:, slot, :, 0:n],
                                    w_hi[:, slot, :, 0:n], ALU.subtract).then_inc(w_split, 1)

        def project(pe, s, slot, m=P, ready=None):
            pe.wait_ge(w_split, s + 1)
            for h in range(2):
                if not (isinstance(s, int) and s == 0):
                    pe.wait_ge(proj_free[h], s)
                n = 0
                for k in range(KT):
                    if ready and h == 0:
                        ready(k)
                    for a, b in ((w_hi, h_hi), (w_lo, h_hi), (w_hi, h_lo)):
                        mm = nc.tensor.matmul(PJ[h][0:m, :], a[:, slot, k, 0:m],
                                              b[:, k, h * HALF:(h + 1) * HALF],
                                              start=n == 0, stop=n == 3 * KT - 1)
                        n += 1
                mm.then_inc(proj_full[h], 1)

        def project_part(pe, s, slot, h, n0, count):
            if n0 == 0:
                if h == 0:
                    pe.wait_ge(w_split, s + 1)
                pe.wait_ge(proj_free[h], s)
            for n in range(n0, n0 + count):
                a, b = ((w_hi, h_hi), (w_lo, h_hi), (w_hi, h_lo))[n % 3]
                mm = nc.tensor.matmul(PJ[h][:], a[:, slot, n // 3, :], b[:, n // 3, h * HALF:(h + 1) * HALF],
                                      start=n == 0, stop=n == 3 * KT - 1)
            if n0 + count == 3 * KT:
                mm.then_inc(proj_full[h], 1)

        def columns(w, c0, n=P):
            return w.rearrange("(k p) c -> p k c", p=P)[:, :, c0:c0 + n]

        def columns_at(w, c0, i, step):
            return w.rearrange("(k p) c -> p k c", p=P)[:, :, bass.ds(i * step + c0, P)]

        def at(i, per, n):
            return i * per + n

        zeros = sb("zeros", [P, 1])

        def wide(ap, n):
            return ap.rearrange("p (o m) -> p o m", o=1).broadcast_to([ap.shape[0], n, ap.shape[1]])

        def each(ap, n):
            return ap.rearrange("p (m o) -> p m o", o=1).broadcast_to([ap.shape[0], ap.shape[1], n])

        X0 = 8

        def sync_0(sp):
            sp.dma_start(cst[:], cst_in).then_inc(const_in, 16)
            sp.wait_ge(par_zeroed, 1)
            rows = [(0, 12, mu[0:1536]), (12, 4, mu[1600:2112]), (16, 4, w0), (20, 4, a0), (24, 4, k_k),
                    (28, 4, k_a), (36, 4, ln_w), (40, 4, ln_b), (PRE0, 8, pre0),
                    (POST0, 8, post0), (PRE1, 8, pre1), (POST1, 8, post1), (CN, 1, c_norm)]
            for r0, n, src in rows:
                sp.dma_start(par_raw[r0:r0 + n, :], src.rearrange("(r c) -> r c", c=P)).then_inc(par_in, 16)
            sp.dma_start(par_raw[32:36, :], r_k.rearrange("(g h) c -> g (h c)", h=2)).then_inc(par_in, 16)
            sp.dma_start(par_raw[LB0:LB0 + 16, :], lbs.rearrange("l (r c) -> (l r) c", c=P)).then_inc(par_in, 16)
            sp.dma_start(par_raw[MUL:MUL + 1, 0:LORA],
                         mu[1536:1600].rearrange("(r c) -> r c", r=1)).then_inc(par_in, 16)
            for tile in range(NC):
                j = tile % 2
                if tile >= 2:
                    sp.wait_ge(xn_ready, tile - 1)
                sp.dma_start(xt[j], x[tile * P:(tile + 1) * P, :]).then_inc(x_in[j], 16)
                if tile == 1:
                    load_slab(sp, SLAB_LORA, 0, columns(w_in0, COL_LORA, LORA))
                    load_slab(sp, SLAB_A, 1, columns(w_in0, COL_R))
                if tile == 3:
                    sp.dma_start(lw[0:32, :], w2).then_inc(small_in, 16)
                    sp.dma_start(lw[32:64, :], a2).then_inc(small_in, 16)
                    sp.dma_start(tb[:], table).then_inc(small_in, 16)
                    sp.dma_start(bk, buckets).then_inc(small_in, 16)
                    sp.dma_start(sinkb[:], sinks.rearrange("(o h) -> o h", o=1).broadcast_to([P, 8])).then_inc(small_in, 16)
            sp.wait_ge(bias_row, 1)
            sp.dma_start(scratch.rearrange("q h m -> h q m"),
                         brow.rearrange("h (o m) -> h o m", o=1).broadcast_to([8, P, 384])).then_inc(scr_out, 16)
            sp.wait_ge(scr_out, 16)

        def pool_0(pool, own):
            nc.gpsimd.memset(par_raw, 0.0).then_inc(par_zeroed, 1)
            own.on(nc.gpsimd.memset(zeros[:], 0.0))
            nc.gpsimd.memset(ones_all[:], 1.0)
            for n, v in enumerate((NORM_EPS, GN_EPS, 20 * float(np.log(2.0)), 1.0)):
                ins = nc.gpsimd.memset(eps[:, n:n + 1], v)
            ins.then_inc(eps_ready, 1)
            own.wait()
            split_slab(pool, own, SLAB_LORA, 0, 0, LORA)
            split_slab(pool, own, SLAB_A, 1, 0)
            for tile in range(NC):
                j = tile % 2
                pool.wait_ge(hi_ready, tile + 1)
                nc.gpsimd.tensor_tensor(h_lo[:, :, tile * P:(tile + 1) * P], hf[j],
                                        h_hi[:, :, tile * P:(tile + 1) * P], ALU.subtract).then_inc(lo_ready, 1)

        def tensor_0(pe):
            pe.wait_ge(const_in, 16)
            pe.wait_ge(par_in, 16 * 16)
            nc.tensor.transpose(ZB[:, 0:ROWS], par_raw, cst[0:ROWS, CI:CI + ROWS]).then_inc(par_full, 1)
            for tile in range(NC):
                j = tile % 2
                pe.wait_ge(xn_ready, tile + 1)
                for b in range(2):
                    if tile:
                        pe.wait_ge(sc_free[b], tile)
                    for k in range(4):
                        kk = 4 * b + k
                        mm = nc.tensor.transpose(SC[b][:, k * P:(k + 1) * P], xn[j][:, kk * P:(kk + 1) * P], ident)
                    mm.then_inc(sc_full[b], 1)
            pe.wait_ge(small_in, 16 * 5)
            nc.tensor.matmul(DP[0][0:8, 0:384], tb[:], bk[:, 0:384], start=True, stop=True).then_inc(bias_full, 1)

        def scalar_0(act, own):
            act.wait_ge(const_in, 16)
            nc.scalar.activation(ident_r[:], ident, ACT.Copy).then_inc(ident_ready, 1)
            act.wait_ge(eps_ready, 1)
            nc.scalar.preload_act_table_set("natural_log_exp_and_others")
            def copy_hi(tile):
                act.wait_ge(sc_free[1], tile + 1)
                act.wait_ge(sc_free[0], tile + 1)
                nc.scalar.activation(h_hi[:, :, tile * P:(tile + 1) * P], hf[tile % 2], ACT.Copy).then_inc(hi_ready, 1)

            for tile in range(NC):
                j = tile % 2
                act.wait_ge(x_in[j], 16 * (tile // 2 + 1))
                if tile >= 2:
                    act.wait_ge(sc_full[1], tile - 1)
                own.on(nc.scalar.activation(xn[j], xt[j], ACT.Square, accum_out=rms[:, j:j + 1]))
                own.wait()
                own.on(nc.scalar.activation(rms[:, 2 + j:3 + j], rms[:, j:j + 1], ACT.Ln, scale=1.0 / D, bias=eps[:, 0:1]))
                own.wait()
                nc.scalar.activation(rms[:, 4 + j:5 + j], rms[:, 2 + j:3 + j], ACT.Exp, scale=-0.5).then_inc(rstd_ready, 1)
                if tile >= 2:
                    copy_hi(tile - 2)
            for tile in (NC - 2, NC - 1):
                copy_hi(tile)

        def vector_0(dve, own):
            dve.wait_ge(par_full, 1)
            own.on(nc.vector.tensor_copy(par[:, 0:RAW_KINDS, :].rearrange("p k f -> p (k f)"), ZB[:, 0:44]))
            own.on(nc.vector.tensor_copy(oth[:], ZB[:, 44:ROWS]))
            own.wait()
            nc.vector.tensor_scalar(par[:, OMU:OMU + 4, :], par[:, 0:4, :], -1.0, 1.0, ALU.mult, ALU.add)
            nc.vector.tensor_scalar(par[:, W0H:W0H + 2, :], par[:, W0:W0 + 2, :], 0.5, None, ALU.mult)
            nc.vector.tensor_scalar(par[:, KAH:KAH + 1, :], par[:, KA:KA + 1, :], 0.5, None, ALU.mult)
            nc.vector.tensor_scalar(par[:, OKAH:OKAH + 1, :], par[:, KA:KA + 1, :], -0.5, 1.0, ALU.mult, ALU.add)
            own.on(nc.vector.tensor_scalar(lbp[:, 0, 0:1], oth[:, MUL - 44:MUL - 43], -1.0, 1.0, ALU.mult, ALU.add))
            own.on(nc.vector.memset(u[:, 0:1], 0.0))
            own.on(nc.vector.memset(reset[:], 1.0))
            own.wait()
            nc.vector.memset(reset[:].rearrange("p (c t) -> p c t", t=C)[:, :, 0:1], 0.0).then_inc(par_ready, 1)
            def scale_columns(tile):
                j = tile % 2
                if tile >= 2:
                    dve.wait_ge(lo_ready, tile - 1)
                for b in range(2):
                    dve.wait_ge(sc_full[b], tile + 1)
                    nc.vector.tensor_tensor(hf[j][:, 4 * b:4 * b + 4, :], SC[b][:].rearrange("p (k t) -> p k t", k=4),
                                            each(oth[:, PRE0 - 44 + 4 * b:PRE0 - 44 + 4 * b + 4], P),
                                            ALU.mult).then_inc(sc_free[b], 1)

            for tile in range(NC):
                j = tile % 2
                dve.wait_ge(rstd_ready, tile + 1)
                nc.vector.tensor_scalar(xn[j], xt[j], rms[:, 4 + j:5 + j], None, ALU.mult).then_inc(xn_ready, 1)
                if tile:
                    scale_columns(tile - 1)
            scale_columns(NC - 1)
            dve.wait_ge(bias_full, 1)
            nc.vector.tensor_tensor(brow, DP[0][0:8, 0:384], bk[0:8, 384:768], ALU.add).then_inc(bias_row, 1)

        GROUPS = NC // 2
        SLOTS = LEVELS + 1
        USES = 23
        U_W, U_A, U_SS, U_V = range(4)
        U_BONUS = 7
        U_MEAN, U_VAR = 21, 22

        def front(g):
            return 4 + 4 * g

        def out_use(g):
            return front(g + 1) + (3 if g + 1 < GROUPS else 0)

        A_SLABS = (COL_R, COL_K, COL_V, COL_AG)

        def slab_a(i, q):
            return at(i, 4, SLAB_A + q)

        def sync_a(sp):
            for q, col in list(enumerate(A_SLABS))[1:]:
                load_slab(sp, SLAB_A + q, (SLAB_A + q) % 2, columns(w_in0, col))
            with sp.Fori(0, PAIRS - 1) as i:
                for q, col in enumerate(A_SLABS):
                    load_slab(sp, at(i, 4, SLAB_A + 4 + q), (SLAB_A + q) % 2, columns_at(w_in0, col + P, i, P))

        def pool_a(pool, own):
            for q in range(1, 4):
                split_slab(pool, own, SLAB_A + q, (SLAB_A + q) % 2, (SLAB_A + q) // 2)

            pool.wait_ge(scr_out, 16)

            def prepare(i):
                pool.wait_ge(t_ready, at(i, 1, 1))
                nc.gpsimd.tensor_tensor(gcum, gcum, ks, ALU.mult).then_inc(kp_ready, 1)
                pool.wait_ge(kp_ready, at(i, 1, 1))
                pool.wait_ge(exp_ready, at(i, 3, 1))
                nc.gpsimd.tensor_tensor(kt, gcum, em, ALU.mult).then_inc(kq_ready, 1)
                pool.wait_ge(exp_ready, at(i, 3, 3))
                nc.gpsimd.tensor_tensor(rk, gcum, rs, ALU.mult).then_inc(rk_ready, 1)

            def split_next(i, q):
                s = SLAB_A + 4 + q
                split_slab(pool, own, at(i, 4, s), s % 2, at(i, 2, s // 2))

            split_next(0, 0)
            prepare(0)
            split_next(0, 1)
            with pool.Fori(0, PAIRS - 1) as i:
                own.enter(i, 4)
                for q in range(2, 6):
                    split_next(i, q)
                prepare(i + 1)
                own.leave(PAIRS - 1)

        def tensor_a_first(pe):
            pe.wait_ge(lo_ready, NC)
            project(pe, SLAB_LORA, 0, LORA)

        def tensor_a(pe):
            pe.wait_ge(ident_ready, 1)

            def sc_use(h, i, use):
                pe.wait_ge(sc_free[h], at(i, USES, X0 + use))

            def channel_sums(i, use, lhs, src):
                for h in range(2):
                    sc_use(h, i, use)
                    nc.tensor.matmul(SC[h][:], lhs, src[:, h * HALF:(h + 1) * HALF],
                                     start=True, stop=True).then_inc(sc_full[h], 1)

            def low_rank(i):
                pe.wait_ge(lora_ready, 2)
                pe.wait_ge(lwp_ready, at(i, 1, 1))
                for r in range(2):
                    channel_sums(i, U_W + r, lwp[32 * r:32 * r + 32, :], lora[32 * r:32 * r + 32, :])

            def key_sums(i):
                pe.wait_ge(ksq_ready, at(i, 1, 1))
                channel_sums(i, U_SS, ones64, kkb)

            def prepare(i):
                for h in range(2):
                    pe.wait_ge(proj_free[h], slab_a(i, 4))
                for j in range(2):
                    sc_use(j, i, U_V)
                    for n in range(4):
                        mm = nc.tensor.transpose(SC[j][:, n * P:(n + 1) * P], vs[:, (4 * j + n) * C:(4 * j + n + 1) * C],
                                                 ident)
                    mm.then_inc(sc_full[j], 1)
                project_part(pe, at(i, 4, SLAB_A + 4), SLAB_A % 2, 0, 0, 3 * KT)
                pe.wait_ge(kq_ready, at(i, 1, 1))
                pe.wait_ge(ab_ready, at(i, 3, 3))

            def scores(i, g):
                for j in range(2):
                    c = slice((2 * g + j) * C, (2 * g + j + 1) * C)
                    sc_use(j, i, front(g))
                    for n, src in enumerate((bb, kt)):
                        mm = nc.tensor.transpose(SC[j][:, n * P:(n + 1) * P], src[:, c], ident)
                    mm.then_inc(sc_full[j], 1)
                if g:
                    pe.wait_ge(pf_ready, at(i, GROUPS, g))
                for j in range(2):
                    c = slice((2 * g + j) * C, (2 * g + j + 1) * C)
                    for h in range(2):
                        hp = slice(h * HD, (h + 1) * HD)
                        dst = DP[0] if h else ZB
                        mm = nc.tensor.matmul(dst[:, j * P:(j + 1) * P], ar[hp, 0, c], bb[hp, c],
                                              start=True, stop=True)
                mm.then_inc(z_full, 1)
                for j in range(2):
                    c = slice((2 * g + j) * C, (2 * g + j + 1) * C)
                    for h in range(2):
                        hp = slice(h * HD, (h + 1) * HD)
                        sc_use(h, i, front(g) + 1 + j)
                        for n, src in enumerate((bb, kt)):
                            mm = nc.tensor.matmul(SC[h][:, n * 256:(n + 1) * 256].rearrange("p (a t) -> p a t", a=2),
                                                  src[hp, c], ar[hp, :, c], start=True, stop=True)
                        mm.then_inc(sc_full[h], 1)

            def level(i, g, k, between):
                if k:
                    pe.wait_ge(dp_copied, at(i, 14 * GROUPS, 14 * g + 2 * k))
                    if k == 1:
                        pe.wait_ge(lmr_ready, at(i, GROUPS, g + 1))
                    for un in range(4):
                        mm = nc.tensor.matmul(ZB[:, un * P:(un + 1) * P], lmr[:, un * P:(un + 1) * P], dpt(un)[1],
                                              start=True, stop=True)
                    mm.then_inc(z_full, 1)
                else:
                    pe.wait_ge(lm_ready, at(i, 2 * GROUPS, 2 * g + 2))
                    for b in range(2):
                        nc.tensor.matmul(DP[b][:].rearrange("p (n t) -> p n t", n=4), ident_r[:], wide(ident_r[:], 4),
                                         start=True, stop=True, skip_group_check=True)
                between()
                pe.wait_ge(xt_ready, at(i, 8 * GROUPS, 8 * g + k + 1))
                for un in range(4):
                    b, v = un // 2, un % 2
                    xs = xr[:, un * P:(un + 1) * P]
                    dk = ident_r[:] if k == 0 else dpt(un)[0]
                    nc.tensor.matmul(DP[b][:, v * 256:v * 256 + P], xs, dk, start=False, stop=True, skip_group_check=True)
                    mm = nc.tensor.matmul(DP[b][:, v * 256 + P:v * 256 + 256], dk, xs, start=False, stop=True,
                                          skip_group_check=True)
                    if v:
                        mm.then_inc(dp_full[b], 1)

            def refine(i, g, between):
                pe.wait_ge(dp_copied, at(i, 14 * GROUPS, 14 * g + 14))
                for un in range(4):
                    zs = ZB[:, un * P:(un + 1) * P]
                    nc.tensor.matmul(zs, lm[:, un * P:(un + 1) * P], dpt(un)[1].bitcast(F32), start=True, stop=False)
                    mm = nc.tensor.matmul(zs, ident_r[:], dpt(un)[1], start=False, stop=True)
                mm.then_inc(z_full, 1)
                between()
                pe.wait_ge(xt_ready, at(i, 8 * GROUPS, 8 * g + 8))
                for un in range(4):
                    mm = nc.tensor.matmul(DP[0][:, un * P:(un + 1) * P], dpt(un)[0], xr[:, un * P:(un + 1) * P],
                                          start=True, stop=True)
                mm.then_inc(corr_full, 1)

            def chain(i, g, piece):
                j, stage = piece // 3, piece % 3
                cn = 2 * g + j
                c = slice(cn * C, (cn + 1) * C)
                sp_ = scm[g % 2]
                tb2 = tmb[g % 2]
                if stage == 0:
                    if j == 0:
                        pe.wait_ge(pf_ready, at(i, GROUPS, g + 1))
                        sc_use(0, i, front(g) + 3)
                        sc_use(1, i, front(g) + 3)
                    pe.wait_ge(state_ready, at(i, 9, cn + 1))
                    nc.tensor.matmul(SQ[:, 0:P], ar[:, 0, c], st, start=True, stop=True)
                    for h in range(2):
                        hp = slice(h * HD, (h + 1) * HD)
                        mm = nc.tensor.matmul(SQ[:, hp], sp_[:, 2 * j + h, 256:384], vtm_a[:, cn, hp], start=False, stop=True,
                                              skip_group_check=True)
                    mm.then_inc(rhs_full, 1)
                elif stage == 1:
                    pe.wait_ge(nr_ready, at(i, 8, cn + 1))
                    for h in range(2):
                        mm = nc.tensor.matmul(SQ[:, P + h * HD:P + (h + 1) * HD],
                                              pf[:, g % 2, (2 * j + h) * P:(2 * j + h + 1) * P],
                                              nr[:, j, h * HD:(h + 1) * HD], start=True, stop=True)
                    mm.then_inc(sa_full, 1)
                else:
                    pe.wait_ge(sa_ready, at(i, 8, cn + 1))
                    nc.tensor.matmul(SQ[:, 256:384], tb2[:, j, 0:P], sa[:, j, :], start=True, stop=False)
                    nc.tensor.matmul(SQ[:, 256:384], tb2[:, j, P:2 * P], vtm_a[:, cn, :], start=False,
                                     stop=True)
                    sc_use(j, i, out_use(g))
                    nc.tensor.matmul(SC[j][:, 0:P], st, ar[:, 1, c], start=True, stop=True)
                    for h in range(2):
                        hp = slice(h * HD, (h + 1) * HD)
                        nc.tensor.matmul(SC[j][hp, 0:P], sa[:, j, hp], sp_[:, 2 * j + h, P:2 * P], start=False, stop=True,
                                         skip_group_check=True)
                        mm = nc.tensor.matmul(SC[j][hp, 0:P], vtm_a[:, cn, hp], sp_[:, 2 * j + h, 3 * P:4 * P],
                                              start=False, stop=True, skip_group_check=True)
                    mm.then_inc(sc_full[j], 1)

            def body(i, next_slabs):
                prepare(i)
                for g in range(GROUPS):
                    scores(i, g)
                    for k in range(SLOTS):
                        def ahead(n0, count):
                            if g == 0:
                                project_part(pe, at(i, 4, SLAB_A + 4), SLAB_A % 2, 1, 3 * k + n0, count)
                                return
                            project_part(pe, at(i, 4, SLAB_A + 4 + g), (SLAB_A + g) % 2, k // 4,
                                         k % 4 * 6 + n0, count)

                        first, count = (1, 3) if g == 0 else (2, 6) if k < 6 else (3, 6)

                        def between():
                            if g and k < 6:
                                chain(i, g - 1, k)
                            ahead(0, first)
                        if k < LEVELS:
                            level(i, g, k, between)
                        else:
                            refine(i, g, between)
                        ahead(first, count - first)
                        if g == 0 and k == 1:
                            pe.wait_ge(rkm_ready, at(i, 1, 1))
                            pe.wait_ge(rk_ready, at(i, 1, 1))
                            channel_sums(i, U_BONUS, rkm[:], rk)
                for piece in range(6):
                    chain(i, GROUPS - 1, piece)
                    if not next_slabs:
                        s = SLAB_B + N_V
                        project_part(pe, s, s % 2, piece // 3, piece % 3 * 8, 8)
                if not next_slabs:
                    s = SLAB_B + N_K0
                    project_part(pe, s, s % 2, 0, 0, 3 * KT)
                sc_use(0, i, U_MEAN)
                sc_use(1, i, U_MEAN)
                channel_sums(i, U_MEAN, ones64, ysb)
                if not next_slabs:
                    project_part(pe, s, s % 2, 1, 0, 3 * KT)
                pe.wait_ge(ysq_ready, at(i, 1, 1))
                channel_sums(i, U_VAR, ones64, ysq)
                if next_slabs:
                    low_rank(i + 1)
                    key_sums(i + 1)

            project(pe, SLAB_A, SLAB_A % 2)
            low_rank(0)
            for q in (1, 2):
                project(pe, SLAB_A + q, (SLAB_A + q) % 2)
            key_sums(0)
            project(pe, SLAB_A + 3, (SLAB_A + 3) % 2)
            with pe.Fori(0, PAIRS - 1) as i:
                body(i, True)
            body(PAIRS - 1, False)

        def scalar_a(act, own):
            act.wait_ge(par_ready, 1)
            act.wait_ge(lo_ready, NC)

            def scale_shifted(s, h, m, col):
                if h == 0 and not (isinstance(s, int) and s == 0):
                    act.wait_ge(proj_free[1], s)
                act.wait_ge(proj_full[h], s + 1)
                nc.scalar.activation(u[0:m, 1 + h * HALF:1 + (h + 1) * HALF], PJ[h][0:m, :], ACT.Copy,
                                     scale=col).then_inc(mix_scaled, 1)

            for h in range(2):
                scale_shifted(SLAB_LORA, h, LORA, oth[0:LORA, MUL - 44:MUL - 43])
            act.wait_ge(proj_free[0], 1)
            act.wait_ge(proj_free[1], 1)
            nc.scalar.activation(lora[0:32, :], lora[0:32, :], ACT.Tanh).then_inc(lora_ready, 1)
            nc.scalar.activation(lora[32:64, 0:1], lora[32:64, 0:1], ACT.Copy).then_inc(lora_ready, 1)
            act.wait_ge(pp_ready, 1)

            def low_rank(i):
                nc.scalar.preload_act_table(ACT.Silu)
                act.wait_ge(pp_ready, at(i, 1, 1))
                for r, (dst, kind) in enumerate(((ldb, W0H), (bb, A0H))):
                    for h in range(2):
                        act.wait_ge(sc_full[h], at(i, USES, X0 + r + 1))
                        nc.scalar.activation(dst[:, h * HALF:(h + 1) * HALF], SC[h][:], ACT.Tanh, scale=0.5,
                                             bias=pp[:, kind:kind + 1]).then_inc(sc_free[h], 1)

            def square_keys(i):
                act.wait_ge(pair_done, at(i, 1, 1))
                for h in range(2):
                    act.wait_ge(proj_free[h], slab_a(i, 2))
                nc.scalar.activation(kkb, ks, ACT.Square, scale=pp[:, KK:KK + 1]).then_inc(ksq_ready, 1)

            def gate(i):
                for h in range(2):
                    act.wait_ge(proj_free[h], slab_a(i, 4))
                nc.scalar.activation(gb, gs, ACT.Silu).then_inc(gate_ready, 1)

            def decays(i):
                nc.scalar.preload_act_table_set("natural_log_exp_and_others")
                act.wait_ge(sc_free[0], at(i, USES, X0 + 3))
                act.wait_ge(sc_free[1], at(i, USES, X0 + 3))
                own.on(nc.scalar.activation(kkb, kkb, ACT.Ln, scale=2.0 ** 40))
                own.wait()
                nc.scalar.activation(kkb, kkb, ACT.Exp, scale=-0.5, bias=eps[:, 2:3]).then_inc(rn_ready, 1)
                act.wait_ge(gc_ready, at(i, 1, 1))
                nc.scalar.activation(em.rearrange("p (c t) -> p c t", c=NC), gc[:, :, 1:C + 1], ACT.Exp,
                                     scale=-1.0).then_inc(exp_ready, 1)
                nc.scalar.activation(ee[:, :, 0:C + 1], gc[:, :, 0:C + 1], ACT.Exp).then_inc(exp_ready, 1)
                nc.scalar.activation(fac[:, 1, 0:7], fac[:, 0, 0:7], ACT.Exp).then_inc(exp_ready, 1)

            def first_mix(q):
                for h in range(2):
                    scale_shifted(SLAB_A + q, h, P, pp[:, MU + q:MU + q + 1])

            first_mix(0)
            low_rank(0)
            first_mix(1)
            square_keys(0)
            first_mix(2)
            decays(0)
            first_mix(3)
            gate(0)

            def prepare(i):
                for j in range(2):
                    act.wait_ge(sc_full[j], at(i, USES, X0 + U_V + 1))
                    nc.scalar.activation(vtm_a[:, 4 * j:4 * j + 4, :], SC[j][:].rearrange("p (n c) -> p n c", n=4),
                                         ACT.Copy).then_inc(sc_free[j], 1)

            def chain(i, g, piece):
                j, stage = piece // 3, piece % 3
                cn = 2 * g + j
                if stage == 0:
                    act.wait_ge(rhs_full, at(i, 8, cn + 1))
                    nc.scalar.activation(nr[:, j, :], SQ[:, 0:P], ACT.Copy, scale=-1.0).then_inc(nr_ready, 1)
                elif stage == 1:
                    act.wait_ge(sa_full, at(i, 8, cn + 1))
                    nc.scalar.activation(sa[:, j, :], SQ[:, P:2 * P], ACT.Copy).then_inc(sa_ready, 1)
                else:
                    act.wait_ge(sc_full[j], at(i, USES, X0 + out_use(g) + 1))
                    nc.scalar.activation(ysb[:, cn * C:(cn + 1) * C], SC[j][:, 0:P], ACT.Copy).then_inc(sc_free[j], 1)

            def body(i, next_slabs):
                if next_slabs:
                    own.enter(i, 1)
                prepare(i)

                def mix(g, h):
                    if next_slabs:
                        scale_shifted(at(i, 4, SLAB_A + 4 + g), h, P, pn[:, MU + g:MU + g + 1])
                    else:
                        evacuate_b(act, g, h)

                if next_slabs:
                    act.wait_ge(pn_ready, at(i, 1, 1))
                else:
                    nc.scalar.preload_act_table(ACT.Silu)
                for g in range(GROUPS):
                    for j in range(2):
                        act.wait_ge(sc_full[j], at(i, USES, X0 + front(g) + 1))
                        nc.scalar.activation(tmb[g % 2][:, j, :], SC[j][:, 0:256], ACT.Copy).then_inc(sc_free[j], 1)
                    act.wait_ge(lm_ready, at(i, 2 * GROUPS, 2 * g + 2))
                    nc.scalar.activation(lmr[:], lm, ACT.Copy).then_inc(lmr_ready, 1)
                    for k in range(SLOTS):
                        if g and k < 6:
                            chain(i, g - 1, k)
                        if k < LEVELS:
                            act.wait_ge(dp_full[0], at(i, LEVELS * GROUPS, LEVELS * g + k + 1))
                            nc.scalar.activation(dpr[:, 0:HALF], DP[0][:], ACT.Copy).then_inc(dp_copied, 1)
                        if k == 0 and g:
                            mix(g - 1, 1)
                        if k == 4:
                            mix(g, 0)
                mix(GROUPS - 1, 1)
                for piece in range(6):
                    chain(i, GROUPS - 1, piece)
                    if not next_slabs and piece % 3 == 2:
                        evacuate_b(act, N_V, piece // 3)
                if not next_slabs:
                    nc.scalar.preload_act_table_set("natural_log_exp_and_others")
                    evacuate_b(act, N_K0, 0)
                act.wait_ge(sc_free[0], at(i, USES, X0 + U_MEAN + 1))
                act.wait_ge(sc_free[1], at(i, USES, X0 + U_MEAN + 1))
                nc.scalar.activation(ysq, ysb, ACT.Square).then_inc(ysq_ready, 1)
                if not next_slabs:
                    evacuate_b(act, N_K0, 1)
                for h in range(2):
                    act.wait_ge(sc_full[h], at(i, USES, X0 + U_VAR + 1))
                    nc.scalar.activation(kkb[:, h * HALF:(h + 1) * HALF], SC[h][:], ACT.Ln, scale=1.0 / HD,
                                         bias=eps[:, 1:2]).then_inc(sc_free[h], 1)
                act.wait_ge(sc_free[0], at(i, USES, X0 + U_VAR + 1))
                act.wait_ge(sc_free[1], at(i, USES, X0 + U_VAR + 1))
                nc.scalar.activation(kkb, kkb, ACT.Exp, scale=-0.5).then_inc(ynorm_ready, 1)
                if next_slabs:
                    low_rank(i + 1)
                    square_keys(i + 1)
                    gate(i + 1)
                    decays(i + 1)

            with act.Fori(0, PAIRS - 1) as i:
                body(i, True)
                own.leave(PAIRS - 1)
            body(PAIRS - 1, False)

        DVE_STEPS = 16

        def vector_a(dve, own):
            dve.wait_ge(lo_ready, NC)
            for h in range(2):
                dve.wait_ge(proj_full[h], 1)
                dve.wait_ge(mix_scaled, h + 1)
                nc.vector.scalar_tensor_tensor(lora[:, h * HALF:(h + 1) * HALF], PJ[h][0:LORA, :], lbp[0:LORA, 0, 0:1],
                                               u[0:LORA, h * HALF:(h + 1) * HALF], ALU.mult,
                                               ALU.add).then_inc(proj_free[h], 1)

            def mix(i, q, h, cols):
                dve.wait_ge(proj_full[h], slab_a(i, q + 1))
                dve.wait_ge(mix_scaled, at(i, 8, 2 + 2 * q + h + 1))
                nc.vector.scalar_tensor_tensor(stage[:, q, h * HALF:(h + 1) * HALF], PJ[h][:],
                                               cols[:, OMU + q:OMU + q + 1], u[:, h * HALF:(h + 1) * HALF], ALU.mult,
                                               ALU.add).then_inc(proj_free[h], 1)

            def weights(i):
                nc.vector.tensor_scalar(lwp[:], lw[:, bass.ds(i * P, P)], 1.0, None, ALU.mult).then_inc(lwp_ready, 1)
                nc.vector.tensor_scalar(rkm[:], ones64, pp[:, RK:RK + 1], None, ALU.mult).then_inc(rkm_ready, 1)

            dve.wait_ge(small_in, 16 * 5)
            nc.vector.tensor_scalar(pp[:].rearrange("p (k o) -> p k o", o=1), par[:, :, 0:1], 1.0, None,
                                    ALU.mult).then_inc(pp_ready, 1)
            dve.wait_ge(pp_ready, 1)
            nc.vector.memset(st2, 0.0).then_inc(pair_done, 1)
            weights(0)

            def decays(i):
                dve.wait_ge(sc_free[0], at(i, USES, X0 + 2))
                dve.wait_ge(sc_free[1], at(i, USES, X0 + 2))
                own.on(nc.vector.tensor_scalar(ldb, ldb, -0.5 * DECAY, -0.5 * DECAY, ALU.mult, ALU.add))
                own.wait()
                for h in range(2):
                    own.on(nc.vector.tensor_tensor_scan(gcum[:, h * HALF:(h + 1) * HALF], reset[:],
                                                        ldb[:, h * HALF:(h + 1) * HALF], 0.0, ALU.mult, ALU.add))

            def centre(i):
                for h in range(2):
                    dve.wait_ge(sc_full[h], at(i, USES, X0 + 3))
                    nc.vector.tensor_scalar(kkb[:, h * HALF:(h + 1) * HALF], SC[h][:], 1e-24, None,
                                            ALU.max).then_inc(sc_free[h], 1)
                own.wait()
                g3 = gcum.rearrange("p (c t) -> p c t", c=NC)
                own.on(nc.vector.tensor_tensor(gc[:, :, 1:C + 1], g3, g3[:, :, 63:64].broadcast_to([P, NC, C]),
                                               ALU.subtract))
                own.on(nc.vector.tensor_scalar(gc[:, :, 0:1], g3[:, :, 63:64], -1.0, None, ALU.mult))
                own.wait()
                nc.vector.tensor_tensor(fac[:, 0, 0:7], gc[:, 0:7, C:C + 1].rearrange("p c o -> p (c o)"),
                                        g3[:, 1:8, 63:64].rearrange("p c o -> p (c o)"), ALU.add).then_inc(gc_ready, 1)
                dve.wait_ge(gc_ready, at(i, 1, 1))
                nc.vector.tensor_scalar(gcum, bb, pp[:, KAH:KAH + 1], pp[:, OKAH:OKAH + 1], ALU.mult,
                                        ALU.add).then_inc(t_ready, 1)

            def factors(i):
                dve.wait_ge(rn_ready, at(i, 1, 1))
                nc.vector.scalar_tensor_tensor(kkb, ks, pp[:, KK:KK + 1], kkb, ALU.mult,
                                               ALU.mult).then_inc(kk_ready, 1)
                dve.wait_ge(kk_ready, at(i, 1, 1))
                own.on(nc.vector.scalar_tensor_tensor(bb, bb, 1.0, kkb, ALU.add, ALU.mult))
                dve.wait_ge(exp_ready, at(i, 3, 3))
                nc.vector.tensor_tensor(ar[:, 0, :].rearrange("p (c t) -> p c t", c=NC),
                                        kkb.rearrange("p (c t) -> p c t", c=NC), ee[:, :, 0:C],
                                        ALU.mult).then_inc(ab_ready, 1)
                nc.vector.tensor_tensor(ar[:, 1, :].rearrange("p (c t) -> p c t", c=NC),
                                        rs.rearrange("p (c t) -> p c t", c=NC), ee[:, :, 1:C + 1],
                                        ALU.mult).then_inc(ab_ready, 1)
                own.wait()
                nc.vector.scalar_tensor_tensor(bb, bb, 0.5, em, ALU.mult, ALU.mult).then_inc(ab_ready, 1)

            def first_mix(q):
                for h in range(2):
                    mix(0, q, h, pp)

            first_mix(0)
            first_mix(1)
            decays(0)
            first_mix(2)
            centre(0)
            factors(0)
            first_mix(3)

            def masks(i, g):
                dve.wait_ge(z_full, at(i, 8 * GROUPS, 8 * g + 1))
                for h, src in enumerate((ZB, DP[0])):
                    nc.vector.tensor_tensor(lm.rearrange("p (j h t) -> p j h t", j=2, h=2)[:, :, h, :],
                                            src[:, 0:256].rearrange("p (j t) -> p j t", j=2),
                                            wide(cst[:, CL:CL + P], 2), ALU.mult).then_inc(lm_ready, 1)
                for un in range(4):
                    h, j = un % 2, un // 2
                    dve.wait_ge(sc_full[h], at(i, USES, X0 + front(g) + 2 + j))
                    nc.vector.tensor_tensor(scm[g % 2][:, un, :], SC[h][:], cst[:, CM:CM + 512],
                                            ALU.mult).then_inc(sc_free[h], 1)

            def state(i, cn):
                j = cn % 2
                dve.wait_ge(sc_full[j], at(i, USES, X0 + out_use(cn // 2) + 1))
                if cn < NC - 1:
                    own.on(nc.vector.scalar_tensor_tensor(st2, SQ[:, 256:384], fac[:, 1, cn:cn + 1], ones64,
                                                          ALU.mult, ALU.mult))
                    own.wait()
                    nc.vector.scalar_tensor_tensor(st, st, fac[:, 1, cn:cn + 1], st2, ALU.mult,
                                                   ALU.add).then_inc(state_ready, 1)
                else:
                    nc.vector.memset(st2, 0.0).then_inc(state_ready, 1)

            def body(i, next_slabs):
                if next_slabs:
                    own.enter(i, DVE_STEPS)
                    nc.vector.tensor_scalar(pn[:].rearrange("p (k o) -> p k o", o=1), par[:, :, bass.ds(i + 1, 1)], 1.0, None,
                                            ALU.mult).then_inc(pn_ready, 1)
                nc.vector.memset(st, 0.0).then_inc(state_ready, 1)
                dve.wait_ge(gate_ready, at(i, 1, 1))
                z4 = ZB[:].rearrange("p (u t) -> p u t", u=4)
                x4 = xr[:].rearrange("p (u t) -> p u t", u=4)

                def late_mix(g, h):
                    if next_slabs:
                        mix(i + 1, g, h, pn)

                for g in range(GROUPS):
                    masks(i, g)
                    for k in range(LEVELS):
                        if k:
                            dve.wait_ge(z_full, at(i, 8 * GROUPS, 8 * g + k + 1))
                            src = z4
                        else:
                            dve.wait_ge(sc_free[0], at(i, USES, X0 + front(g) + 3))
                            dve.wait_ge(sc_free[1], at(i, USES, X0 + front(g) + 3))
                            src = scm[g % 2][:, :, 0:P]
                        nc.vector.tensor_tensor(x4, src, wide(cst[:, CN7 + k * P:CN7 + (k + 1) * P], 4),
                                                ALU.mult).then_inc(xt_ready, 1)
                        dve.wait_ge(dp_full[1], at(i, LEVELS * GROUPS, LEVELS * g + k + 1))
                        nc.vector.tensor_scalar(dpr[:, HALF:2 * HALF], DP[1][:], 1.0, None,
                                                ALU.mult).then_inc(dp_copied, 1)
                        if g == 0 and k in (2, 3):
                            h = k - 2
                            dve.wait_ge(ab_ready, at(i, 3, 3))
                            dve.wait_ge(kq_ready, at(i, 1, 1))
                            dve.wait_ge(sc_full[h], at(i, USES, X0 + U_BONUS + 1))
                            nc.vector.tensor_tensor(em[:, h * HALF:(h + 1) * HALF], SC[h][:],
                                                    vs[:, h * HALF:(h + 1) * HALF], ALU.mult).then_inc(sc_free[h], 1)
                        if g and k in (2, 5):
                            state(i, 2 * (g - 1) + k // 3)
                        if k == 1 and g:
                            late_mix(g - 1, 1)
                        if k == 5:
                            late_mix(g, 0)
                    dve.wait_ge(z_full, at(i, 8 * GROUPS, 8 * g + 8))
                    nc.vector.tensor_tensor(x4, wide(ident, 4), z4, ALU.subtract).then_inc(xt_ready, 1)
                    dve.wait_ge(corr_full, at(i, GROUPS, g + 1))
                    dve.wait_ge(dp_copied, at(i, 14 * GROUPS, 14 * g + 14))
                    nc.vector.tensor_tensor(pf[:, g % 2, :].rearrange("p (u t) -> p u t", u=4),
                                            dpr[:].rearrange("p (u a t) -> p u a t", u=4, a=2)[:, :, 1, :].bitcast(F32),
                                            DP[0][:].rearrange("p (u t) -> p u t", u=4), ALU.add).then_inc(pf_ready, 1)
                late_mix(GROUPS - 1, 1)
                for j in range(2):
                    state(i, NC - 2 + j)
                own.on(nc.vector.tensor_copy(ln[:], pp[:, LNW:LNB + 1]))
                if next_slabs:
                    own.wait()
                    nc.vector.tensor_copy(pp[:], pn[:]).then_inc(pp_ready, 1)
                    dve.wait_ge(pp_ready, at(i, 1, 2))
                    weights(i + 1)
                for h in range(2):
                    dve.wait_ge(sc_full[h], at(i, USES, X0 + U_MEAN + 1))
                    nc.vector.scalar_tensor_tensor(ysb[:, h * HALF:(h + 1) * HALF], SC[h][:], -1.0 / HD,
                                                   ysb[:, h * HALF:(h + 1) * HALF], ALU.mult,
                                                   ALU.add).then_inc(sc_free[h], 1)
                dve.wait_ge(ynorm_ready, at(i, 1, 1))
                own.on(nc.vector.scalar_tensor_tensor(ysb, ysb, ln[:, 0:1], kkb, ALU.mult, ALU.mult))
                own.wait()
                own.on(nc.vector.scalar_tensor_tensor(ysb, ysb, ln[:, 1:2], em, ALU.add, ALU.add))
                own.wait()
                nc.vector.tensor_tensor(yT[:, bass.ds(i, 1), :], ysb.rearrange("p (o t) -> p o t", o=1),
                                        gb.rearrange("p (o t) -> p o t", o=1), ALU.mult).then_inc(pair_done, 1)
                if next_slabs:
                    decays(i + 1)
                    centre(i + 1)
                    factors(i + 1)

            with dve.Fori(0, PAIRS - 1) as i:
                body(i, True)
                own.leave(PAIRS - 1)
            body(PAIRS - 1, False)

        SB = X0 + USES * PAIRS
        bias = zT[:, 0:2, :].rearrange("p a (b k) -> p (a b) k", b=4)
        kd = [zT[:, 2 + j, :] for j in range(KV)]
        qb = [zT[:, 4 + n, :] for n in range(4)]
        vch = work[:, 0:T]
        vtm = work[:, T:2 * T].rearrange("p (n c) -> p n c", n=NC)
        ps = work[:, 2 * T:4 * T].rearrange("p (g h k) -> p g h k", g=2, h=4)
        pt = work[:, 4 * T:6 * T].rearrange("p (g h a q) -> p g h a q", g=2, h=4, a=2)
        ob = work[:, 6 * T:6 * T + 512].rearrange("p (g c) -> p g c", g=2)
        GROUPS_B = KV * NC
        sm = soft[:]

        B_SLABS = [("g", 0), ("g", 1), ("g", 2), ("g", 3), ("v", 0), ("k", 0),
                   ("q", 0), ("q", 1), ("k", 1), ("q", 2), ("q", 3)]
        N_V, N_K0, N_Q0, B_FIRST = 4, 5, 6, 8

        def sync_b(sp):
            for n, (kind, a) in enumerate(B_SLABS):
                s = SLAB_B + n
                if n == B_FIRST:
                    sp.wait_ge(phase_done, 3 * 2)
                    sp.dma_start(bias[:], bass.AP(scratch.tensor, 127, [[8 * 384 - 1, P], [384, 8], [1, 256]])).then_inc(scr_in, 16)
                if kind == "k":
                    load_slab(sp, s, s % 2, columns(w_in0, COL_BK + a * HD, HD))
                    sp.dma_start(w_raw[:, s % 2, :, HD:P], columns(w_in0, COL_BK + a * HD, HD)).then_inc(w_in[s % 2], 16)
                else:
                    load_slab(sp, s, s % 2,
                              columns(w_in0, {"v": COL_BV, "q": COL_Q, "g": COL_BG}[kind] + a * P))

        def evacuate_b(act, n, h):
            kind, a = B_SLABS[n]
            dst = {"v": [vch], "k": kd, "q": qb, "g": [yT[:, 4 + m, :] for m in range(4)]}[kind][a]
            act.wait_ge(proj_full[h], SLAB_B + n + 1)
            nc.scalar.activation(dst[:, h * HALF:(h + 1) * HALF], PJ[h][:], ACT.Silu if kind == "g" else ACT.Copy,
                                 scale=HD ** -0.5 if kind == "q" else 1.0).then_inc(proj_free[h], 1)

        def pool_b(pool, own, first, last):
            extra = [0, 0]
            for n, (kind, a) in enumerate(B_SLABS):
                s = SLAB_B + n
                extra[s % 2] += kind == "k"
                if first <= n < last:
                    split_slab(pool, own, s, s % 2, s // 2 + extra[s % 2])

        def tensor_b_first(pe):
            project(pe, SLAB_B + N_Q0, (SLAB_B + N_Q0) % 2)

        def tensor_b(pe):
            for b in range(2):
                for m in range(4):
                    mm = nc.tensor.transpose(DP[b][:, m * P:(m + 1) * P], vch[:, (4 * b + m) * P:(4 * b + m + 1) * P],
                                             ident)
                mm.then_inc(vt_full, 1)
            for n in range(N_Q0 + 1, B_FIRST):
                project(pe, SLAB_B + n, (SLAB_B + n) % 2)

            def scores(grp):
                j, n = grp // NC, grp % NC
                if n == 0:
                    for h in range(2):
                        pe.wait_ge(proj_free[h], SLAB_B + (B_FIRST if j == 0 else len(B_SLABS)))
                for part in range(2):
                    hp = slice(part * HD, (part + 1) * HD)
                    pe.wait_ge(sc_free[part], SB + grp)
                    for qi in range(2):
                        w = P if n == 0 else 2 * P
                        mm = nc.tensor.matmul(SC[part][:, qi * 256 + 256 - w:qi * 256 + 256],
                                              qb[2 * j + qi][hp, n * P:(n + 1) * P],
                                              kd[j][hp, (n + 1) * P - w:(n + 1) * P], start=True, stop=True)
                    mm.then_inc(sc_full[part], 1)

            def turn_probs(grp):
                n = grp % NC
                halves = (1,) if n == 0 else (0, 1)
                pe.wait_ge(p_ready, 4 * (grp + 1))
                if grp == 0:
                    pe.wait_ge(vt_ready, 2)
                for qi in range(2):
                    if grp:
                        pe.wait_ge(pt_copied[qi], grp)
                    for part in range(2):
                        for a in halves:
                            mm = nc.tensor.transpose(DP[qi][:, (2 * part + a) * P:(2 * part + a + 1) * P],
                                                     ps[:, grp % 2, 2 * qi + part, a * P:(a + 1) * P], ident)
                    mm.then_inc(pt_full[qi], 1)

            def attend(grp):
                j, n = grp // NC, grp % NC
                halves = (1,) if n == 0 else (0, 1)
                for qi in range(2):
                    pe.wait_ge(pt_copied[qi], grp + 1)
                    if qi == 0 and grp:
                        pe.wait_ge(o_ready, grp)
                    for part in range(2):
                        h = 2 * qi + part
                        for a in halves:
                            mm = nc.tensor.matmul(SQ[:, h * HD:(h + 1) * HD], pt[:, grp % 2, h, a, :],
                                                  vtm[:, n - 1 + a, j * HD:(j + 1) * HD],
                                                  start=a == halves[0], stop=a == 1)
                mm.then_inc(o_full, 1)

            def turn(grp):
                pe.wait_ge(o_ready, grp + 1)
                if grp:
                    pe.wait_ge(y_out, grp)
                for qi in range(2):
                    mm = nc.tensor.transpose(ZB[:, qi * P:(qi + 1) * P], ob[:, grp % 2, qi * P:(qi + 1) * P], ident)
                mm.then_inc(ot_full, 1)

            scores(0)
            for grp in range(GROUPS_B + 2):
                if 1 <= grp <= GROUPS_B:
                    turn_probs(grp - 1)
                if grp + 1 < GROUPS_B:
                    scores(grp + 1)
                if 1 <= grp <= GROUPS_B:
                    attend(grp - 1)
                if grp >= 2:
                    turn(grp - 2)
                if grp < len(B_SLABS) - B_FIRST:
                    s = SLAB_B + B_FIRST + grp
                    project(pe, s, s % 2)

        def scalar_b(act, own):
            for b in range(2):
                act.wait_ge(vt_full, b + 1)
                nc.scalar.activation(vtm[:, 4 * b:4 * b + 4, :], DP[b][:].rearrange("p (n c) -> p n c", n=4),
                                     ACT.Copy).then_inc(vt_ready, 1)
            for n in range(N_Q0, B_FIRST):
                for h in range(2):
                    evacuate_b(act, n, h)

            def probs(grp):
                n = grp % NC
                lo = P if n == 0 else 0
                v = grp % 2
                act.wait_ge(m_ready, 2 * grp + 2)
                if grp >= 2:
                    act.wait_ge(pt_full[1], grp - 1)
                for h in range(4):
                    nc.scalar.activation(ps[:, v, h, lo:], ps[:, v, h, lo:], ACT.Exp, bias=sm[:, v, 4 + h:5 + h],
                                         accum_out=sm[:, v, 12 + h:13 + h]).then_inc(p_ready, 1)
                nc.scalar.activation(sm[:, v, 16:20], sm[:, v, 8:12], ACT.Exp).then_inc(es_ready, 1)

            def copy_p(grp):
                act.wait_ge(pt_full[1], grp + 1)
                if grp >= 2:
                    act.wait_ge(o_full, grp - 1)
                a = 1 if grp % NC == 0 else 0
                nc.scalar.activation(pt[:, grp % 2, 2:4, a:2, :],
                                     DP[1][:].rearrange("p (h a q) -> p h a q", h=2, a=2)[:, :, a:2, :],
                                     ACT.Copy).then_inc(pt_copied[1], 1)

            for grp in range(GROUPS_B + 1):
                if grp:
                    copy_p(grp - 1)
                if grp < GROUPS_B:
                    probs(grp)
                if grp < len(B_SLABS) - B_FIRST:
                    for h in range(2):
                        evacuate_b(act, B_FIRST + grp, h)

        def vector_b(dve, own):
            def row_max(grp):
                j, n = grp // NC, grp % NC
                v = grp % 2
                lo = P if n == 0 else 0
                if grp == 0:
                    dve.wait_ge(scr_in, 16)
                    dve.wait_ge(small_in, 16 * 5)
                if grp >= 2:
                    dve.wait_ge(pt_full[1], grp - 1)
                for part in range(2):
                    dve.wait_ge(sc_full[part], SB + grp + 1)
                    for qi in range(2):
                        h = 2 * qi + part
                        ins = nc.vector.tensor_tensor_reduce(
                            ps[:, v, h, lo:], SC[part][:, qi * 256 + lo:qi * 256 + 256], bias[:, 4 * j + h, lo:], 1.0,
                            sinkb[:, 4 * j + h:4 * j + h + 1], ALU.add, ALU.max, sm[:, v, h:h + 1])
                        if qi:
                            ins.then_inc(sc_free[part], 1)
                        else:
                            own.on(ins)
                dve.wait_ge(sc_free[0], SB + grp + 1)
                dve.wait_ge(sc_free[1], SB + grp + 1)
                own.wait()
                nc.vector.tensor_scalar(sm[:, v, 4:8], sm[:, v, 0:4], -1.0, None, ALU.mult).then_inc(m_ready, 1)
                nc.vector.tensor_tensor(sm[:, v, 8:12], sinkb[:, 4 * j:4 * j + 4], sm[:, v, 0:4],
                                        ALU.subtract).then_inc(m_ready, 1)

            def copy_p(grp):
                dve.wait_ge(pt_full[0], grp + 1)
                if grp >= 2:
                    dve.wait_ge(o_full, grp - 1)
                a = 1 if grp % NC == 0 else 0
                nc.vector.tensor_copy(pt[:, grp % 2, 0:2, a:2, :],
                                      DP[0][:].rearrange("p (h a q) -> p h a q", h=2, a=2)[:, :, a:2, :]
                                      ).then_inc(pt_copied[0], 1)
                v = grp % 2
                dve.wait_ge(es_ready, grp + 1)
                dve.wait_ge(p_ready, 4 * grp + 4)
                own.on(nc.vector.tensor_tensor(sm[:, v, 20:24], sm[:, v, 12:16], sm[:, v, 16:20], ALU.add))
                own.wait()
                own.on(nc.vector.reciprocal(sm[:, v, 20:24], sm[:, v, 20:24]))
                own.wait()

            def divide(grp):
                v = grp % 2
                dve.wait_ge(o_full, grp + 1)
                if grp >= 2:
                    dve.wait_ge(ot_full, grp - 1)
                nc.vector.tensor_tensor(ob[:, v, :].rearrange("p (h c) -> p h c", h=4),
                                        SQ[:, 0:256].rearrange("p (h c) -> p h c", h=4),
                                        each(sm[:, v, 20:24], HD), ALU.mult).then_inc(o_ready, 1)

            def gate(grp):
                j, n = grp // NC, grp % NC
                dve.wait_ge(ot_full, grp + 1)
                y = yT[:, 4 + 2 * j:6 + 2 * j, n * P:(n + 1) * P]
                nc.vector.tensor_tensor(y, ZB[:, 0:256].rearrange("p (a t) -> p a t", a=2), y, ALU.mult).then_inc(y_out, 1)

            row_max(0)
            for grp in range(GROUPS_B + 2):
                if 1 <= grp <= GROUPS_B:
                    copy_p(grp - 1)
                if grp + 1 < GROUPS_B:
                    row_max(grp + 1)
                if 1 <= grp <= GROUPS_B:
                    divide(grp - 1)
                if grp >= 2:
                    gate(grp - 2)

        sqb = [work[:, j * T:(j + 1) * T] for j in range(2)]
        rstd = work[:, 6 * T:7 * T]
        z_sum = work[:, 7 * T:8 * T]
        SO = [SB + GROUPS_B, SB + GROUPS_B + 2 + 4 * HEADS_C]
        xin = yT

        def sync_o(sp, layer, w_out):
            base = (SLAB_O0, SLAB_O1)[layer]
            with sp.Fori(0, 4) as i:
                for q in range(2):
                    s = base + q
                    load_slab(sp, at(i, 2, s), s % 2, columns_at(w_out, q * P, i, 2 * P))
            if layer == 0:
                sync_c_first(sp)
                sp.wait_ge(y_split, 8)
                for t in range(NC):
                    sp.dma_start(xin[:, t, :], x[t * P:(t + 1) * P, :]).then_inc(x_again, 16)
                for k in range(KT):
                    for h in range(2):
                        sp.wait_ge(xt_added[h], k + 1)
                    sp.dma_start(stream[k], zT[:, k, :]).then_inc(stream_out, 16)
                sp.wait_ge(stream_out, 16 * KT)
            else:
                sp.wait_ge(phase_done, 3 * 5)
                for k in range(KT):
                    sp.dma_start(zT[:, k, :], stream[k]).then_inc(stream_in, 16)

        def pool_o(pool, own, layer):
            base = (SLAB_O0, SLAB_O1)[layer]
            with pool.Fori(0, 4) as i:
                own.enter(i, 2)
                for q in range(2):
                    s = base + q
                    split_slab(pool, own, at(i, 2, s), s % 2, at(i, 1, s // 2 + 1))
                own.leave(4)
            if layer == 0:
                pool_c_first(pool, own)
                for k in range(0, KT, 2):
                    pool.wait_ge(h_hi_ready, k + 1)
                    nc.gpsimd.tensor_tensor(h_lo[:, k, :], h_stage[k % 4], h_hi[:, k, :],
                                            ALU.subtract).then_inc(h_lo_ready, 1)

            else:
                pool.wait_ge(stream_in, 16 * KT)
                for n in range(KT):
                    k, hs = 2 * (n % 4) + 1, slice(n // 4 * HALF, (n // 4 + 1) * HALF)
                    pool.wait_ge(z_scaled, n + 1)
                    nc.gpsimd.tensor_tensor(yT[:, k, hs], yT[:, k, hs], zT[:, k, hs], ALU.add).then_inc(final_odd, 1)

        h_stage = [work[:, (2 + j) * T:(3 + j) * T] for j in range(4)]

        def tensor_norm(pe, first, src):
            for h in range(2):
                pe.wait_ge(sc_free[h], first)
                nc.tensor.matmul(SC[h][:], ones_all[:], src[:, h * HALF:(h + 1) * HALF], start=True,
                                 stop=True).then_inc(sc_full[h], 1)

        def scalar_norm(act, first):
            for h in range(2):
                act.wait_ge(sc_full[h], first + 1)
                nc.scalar.activation(rstd[:, h * HALF:(h + 1) * HALF], SC[h][:], ACT.Ln, scale=1.0 / D,
                                     bias=eps[:, 0:1]).then_inc(sc_free[h], 1)
            act.wait_ge(sc_free[0], first + 1)
            act.wait_ge(sc_free[1], first + 1)
            nc.scalar.activation(rstd[:], rstd[:], ACT.Exp, scale=-0.5).then_inc(norm_ready, 1)

        def tensor_o(pe, layer):
            base = (SLAB_O0, SLAB_O1)[layer]
            project(pe, base, base % 2, ready=lambda k: pe.wait_ge(y_split, 8 * layer + k + 1))
            with pe.Fori(0, 3) as i:
                for q in (1, 2):
                    project(pe, at(i, 2, base + q), (base + q) % 2)
            project(pe, base + 7, (base + 7) % 2)
            pe.wait_ge(z_sum_ready, 9 * (layer + 1))
            tensor_norm(pe, SO[layer], z_sum)
            if layer == 0:
                def add_norm(k):
                    pe.wait_ge(sq_ready, k + 1)
                    for h in range(2):
                        if k == 0:
                            pe.wait_ge(sc_free[h], SO[0] + 1)
                        mm = nc.tensor.matmul(SC[h][:], ones_all[:], sqb[k % 2][:, h * HALF:(h + 1) * HALF],
                                              start=k == 0, stop=k == KT - 1)
                        if k == KT - 1:
                            mm.then_inc(sc_full[h], 1)
                        elif h:
                            mm.then_inc(sq_used, 1)

                pe.wait_ge(x_again, 16 * NC)
                for k in range(KT):
                    for h in range(2):
                        if k:
                            pe.wait_ge(xt_added[h], k)
                        for m in range(4):
                            mm = nc.tensor.transpose(DP[h][:, m * P:(m + 1) * P],
                                                     xin[:, 4 * h + m, k * P:(k + 1) * P], ident)
                        mm.then_inc(xt_full[h], 1)
                    if k:
                        add_norm(k - 1)
                add_norm(KT - 1)
            else:
                for t in range(NC):
                    for h in range(2):
                        if t:
                            pe.wait_ge(out_copied[h], t)
                        for m in range(4):
                            k = 4 * h + m
                            if t % 4 == 0 and h == 0 and m == 0:
                                pe.wait_ge(final_ready, KT // 2 * (t // 4 + 1))
                                pe.wait_ge(final_odd, KT // 2 * (t // 4 + 1))
                            mm = nc.tensor.transpose(DP[h][:, m * P:(m + 1) * P], yT[:, k, t * P:(t + 1) * P], ident)
                        mm.then_inc(out_full[h], 1)

        def scalar_o(act, own, layer):
            for k in range(KT):
                nc.scalar.activation(h_hi[:, k, :], yT[:, k, :], ACT.Copy).then_inc(y_hi, 1)
            base = (SLAB_O0, SLAB_O1)[layer]
            z = (zT, yT)[layer]
            for k in range(KT):
                for h in range(2):
                    act.wait_ge(proj_free[h], base + k + 1)
                if k >= 2:
                    act.wait_ge(z_sum_ready, 9 * layer + k)
                nc.scalar.activation(sqb[k % 2], z[:, k, :], ACT.Square).then_inc(z_sq_ready, 1)
            scalar_norm(act, SO[layer])
            if layer == 0:
                for k in range(KT):
                    for s in xt_added:
                        act.wait_ge(s, k + 1)
                    if k >= 2:
                        act.wait_ge(sq_used, k - 1)
                    nc.scalar.activation(sqb[k % 2], zT[:, k, :], ACT.Square).then_inc(sq_ready, 1)
                scalar_norm(act, SO[0] + 1)
                for k in range(KT):
                    act.wait_ge(h_ready, k + 1)
                    nc.scalar.activation(h_hi[:, k, :], h_stage[k % 4], ACT.Copy).then_inc(h_hi_ready, 1)
            else:
                for t in range(NC):
                    if t >= 2:
                        act.wait_ge(out_done[t % 2], 16 * (t // 2))
                    for b in (0, 1) if t < NC // 2 else (1,):
                        act.wait_ge(out_full[b], t + 1)
                        nc.scalar.activation(out_stage[t % 2][:, b * HALF:(b + 1) * HALF], DP[b][:],
                                             ACT.Copy).then_inc(out_copied[b], 1)

        def vector_o(dve, own, layer):
            base = (SLAB_O0, SLAB_O1)[layer]
            z = (zT, yT)[layer]
            for k in range(KT):
                dve.wait_ge(y_hi, 8 * layer + k + 1)
                nc.vector.tensor_tensor(h_lo[:, k, :], yT[:, k, :], h_hi[:, k, :], ALU.subtract).then_inc(y_split, 1)
            dve.wait_ge(y_split, 8 * layer + 8)

            def add_squares(i, q):
                dve.wait_ge(z_sum_ready, at(i, 2, 9 * layer + q + 1))
                dve.wait_ge(z_sq_ready, at(i, 2, 8 * layer + q + 1))
                nc.vector.tensor_tensor(z_sum, z_sum, sqb[q], ALU.add).then_inc(z_sum_ready, 1)

            nc.vector.memset(z_sum, 0.0).then_inc(z_sum_ready, 1)

            with dve.Fori(0, 4) as i:
                for q in range(2):
                    for h in range(2):
                        dve.wait_ge(proj_full[h], at(i, 2, base + q + 1))
                        nc.vector.tensor_scalar(z[:, bass.ds(i * 2 + q, 1), h * HALF:(h + 1) * HALF],
                                                PJ[h][:].rearrange("p (o t) -> p o t", o=1), 1.0, None,
                                                ALU.mult).then_inc(proj_free[h], 1)
                    add_squares(i, q)
            post = (POST0, POST1)[layer] - 44
            if layer == 1:
                dve.wait_ge(stream_in, 16 * KT)
            dve.wait_ge(norm_ready, 2 * layer + 1)
            for n in range(2 * KT if layer else 0):
                k, hs = n % KT, slice(n // KT * HALF, (n // KT + 1) * HALF)
                ins = nc.vector.scalar_tensor_tensor(z[:, k, hs], z[:, k, hs], oth[:, post + k:post + k + 1],
                                                     rstd[:, hs], ALU.mult, ALU.mult)
                if k % 2:
                    ins.then_inc(z_scaled, 1)
                else:
                    own.on(ins)
                    own.wait()
                    nc.vector.tensor_tensor(z[:, k, hs], z[:, k, hs], zT[:, k, hs], ALU.add).then_inc(final_ready, 1)
            for k in range(0 if layer else KT):
                own.on(nc.vector.scalar_tensor_tensor(z[:, k, :], z[:, k, :], oth[:, post + k:post + k + 1], rstd,
                                                      ALU.mult, ALU.mult))
                own.wait()
                for h in range(2):
                    dve.wait_ge(xt_full[h], k + 1)
                    nc.vector.tensor_tensor(z[:, k, h * HALF:(h + 1) * HALF], z[:, k, h * HALF:(h + 1) * HALF],
                                            DP[h][:], ALU.add).then_inc(xt_added[h], 1)
            if layer == 0:
                dve.wait_ge(norm_ready, 2)
                def split_odd(k):
                    dve.wait_ge(h_hi_ready, k + 1)
                    nc.vector.tensor_tensor(h_lo[:, k, :], h_stage[k % 4], h_hi[:, k, :],
                                            ALU.subtract).then_inc(h_lo_odd, 1)

                for k in range(KT):
                    if k >= 4:
                        dve.wait_ge(h_lo_odd if k % 2 else h_lo_ready, k // 2 - 1)
                    nc.vector.scalar_tensor_tensor(h_stage[k % 4], zT[:, k, :], oth[:, PRE1 - 44 + k:PRE1 - 43 + k], rstd,
                                                   ALU.mult, ALU.mult).then_inc(h_ready, 1)
                    if k % 2 == 0 and k:
                        split_odd(k - 1)
                split_odd(KT - 1)
            else:
                for t in range(NC // 2, NC):
                    dve.wait_ge(out_full[0], t + 1)
                    if t >= 2:
                        dve.wait_ge(out_done[t % 2], 16 * (t // 2))
                    nc.vector.tensor_copy(out_stage[t % 2][:, 0:HALF], DP[0][:]).then_inc(out_copied[0], 1)

        out_stage = [work[:, (4 + j) * T:(5 + j) * T] for j in range(2)]

        def sync_out(sp):
            for t in range(NC):
                sp.wait_ge(out_copied[0], t + 1)
                sp.wait_ge(out_copied[1], t + 1)
                sp.dma_start(out[t * P:(t + 1) * P, :], out_stage[t % 2]).then_inc(out_done[t % 2], 16)
            sp.wait_ge(out_done[0], 16 * NC // 2)
            sp.wait_ge(out_done[1], 16 * NC // 2)

        qs2, vc2, fc2, og2 = ([zT[:, 4 * v + n, :] for v in range(2)] for n in range(4))
        oc2 = [work[:, n * T:(n + 1) * T] for n in range(2)]
        ec, sp_, gcm, osq, orn = (work[:, n * T:(n + 1) * T] for n in range(2, 7))
        fac2 = work[:, 7 * T:7 * T + 64].rearrange("p (v k n) -> p v k n", v=2, k=2)
        masks_room = cst[:, CL:CL + T]
        tmc = masks_room[:, 0:512].rearrange("p (j n) -> p j n", j=2)
        sst = masks_room[:, 512:1024].rearrange("p (j n) -> p j n", j=4)
        stc, sc2_t = (yT[:, 7, n * 256:(n + 1) * 256].rearrange("p (j n) -> p j n", j=2) for n in range(2))
        C_COLS = (D, 0, 2 * D, 3 * D)
        H = C // 2
        INC = [SQ, DP[0]]
        NORM = DP[1]
        NS = 2 * NC
        SCC = SO[0] + 2
        CB = 4

        def nth(i, o, per, n):
            return at(i, 2 * per, o * per + n)

        def heads(eng, own, head, per):
            head(0, 0, first=True)
            with eng.Fori(0, HEADS_C // 2 - 1) as i:
                if own:
                    own.enter(i, per)
                head(i, 1)
                head(i, 2)
                if own:
                    own.leave(HEADS_C // 2 - 1)
            head(HEADS_C // 2 - 1, 1, last=True)

        def sync_c_first(sp):
            for q in range(2):
                load_slab(sp, SLAB_C + q, q, columns(w_in1, C_COLS[q]))

        def sync_c(sp):
            first = C_COLS[2] // P
            with sp.Fori(first, first + HEADS_C - 1) as i:
                for q in range(4):
                    col = C_COLS[(q + 2) % 4] + q // 2 * P - C_COLS[2]
                    load_slab(sp, at(i, 4, SLAB_C + 2 + q - 4 * first), q % 2, columns_at(w_in1, col, i, P))
            for q in (2, 3):
                load_slab(sp, SLAB_C + 4 * (HEADS_C - 1) + q, q % 2, columns(w_in1, C_COLS[q] + (HEADS_C - 1) * P))

        def pool_c_first(pool, own):
            for q in range(2):
                split_slab(pool, own, SLAB_C + q, q, (SLAB_C + q) // 2 + 1)

        def pool_c(pool, own):
            with pool.Fori(0, HEADS_C - 1) as i:
                own.enter(i, 4)
                for q in range(4):
                    split_slab(pool, own, at(i, 4, SLAB_C + 2 + q), q % 2, at(i, 2, (SLAB_C + 2 + q) // 2 + 1))
                own.leave(HEADS_C - 1)
            for q in (2, 3):
                s = SLAB_C + 4 * (HEADS_C - 1) + q
                split_slab(pool, own, s, s % 2, s // 2 + 1)

        def tensor_c_first(pe):
            project(pe, SLAB_C, 0, ready=lambda k: pe.wait_ge(h_lo_odd if k % 2 else h_lo_ready, k // 2 + 1))

        def tensor_c(pe):
            def norm(i, o, h):
                if h == 0:
                    pe.wait_ge(osq_ready, nth(i, o, 1, 1))
                else:
                    pe.wait_ge(norm_free, nth(i, o, 2, 1))
                nc.tensor.matmul(NORM[:], ones_all[:], osq[:, h * HALF:(h + 1) * HALF], start=True,
                                 stop=True).then_inc(norm_full, 1)

            def head(i, o, first=False, last=False):
                v = o % 2
                qs, vc, fc = qs2[v], vc2[v], fc2[v]
                pe.wait_ge(kc_ready, nth(i, o, 1, 1))
                pe.wait_ge(qc_ready, nth(i, o, 1, 1))
                pe.wait_ge(proj_free[0], nth(i, o, 4, SLAB_C + 3))
                pe.wait_ge(proj_free[1], nth(i, o, 4, SLAB_C + 3))

                def turn(c):
                    cs = slice(c * C, (c + 1) * C)
                    j = c % 2
                    pe.wait_ge(sc_free[j], nth(i, o, CB, SCC + c // 2))
                    nc.tensor.transpose(SC[j][:, 0:P], vc[:, cs], ident)
                    nc.tensor.transpose(SC[j][:, P:2 * P], fc[:, cs], ident)
                    for b in range(2):
                        hs = slice(c * C + b * H, c * C + (b + 1) * H)
                        mm = nc.tensor.matmul(SC[j][b * H:(b + 1) * H, 256 + b * H:256 + (b + 1) * H], fc[:, hs], qs[:, hs],
                                              start=True, stop=True)
                    mm.then_inc(sc_full[j], 1)

                def ahead(c, part):
                    if not last:
                        project_part(pe, nth(i, o, 4, SLAB_C + 4 + c // 2), c // 2 % 2, c % 2, 8 * part, 8)

                turn(0)
                for c in range(NC):
                    j = c % 2
                    ahead(c, 0)
                    if c + 1 < NC:
                        turn(c + 1)
                    if c == 1 and not first:
                        norm(i, o - 1, 0)
                    pe.wait_ge(tc_ready, nth(i, o, NC, c + 1))
                    pe.wait_ge(sc_state, nth(i, o, NS, 2 * c + 1))
                    for b in range(2):
                        hb = slice(b * H, (b + 1) * H)
                        nc.tensor.matmul(INC[b][:, 0:P], tmc[hb, j, P:2 * P], tmc[hb, j, 0:P], start=True,
                                         stop=True).then_inc(inc_full[b], 1)
                    ahead(c, 1)
                    pe.wait_ge(sc_free[j], nth(i, o, CB, SCC + c // 2 + 1))
                    pe.wait_ge(oc_copied, nth(i, o, NC, c + 1))
                    nc.tensor.matmul(ZB[:, 0:P], tmc[:, j, 0:P], stc[:, j, :], start=True, stop=True)
                    for b in range(2):
                        pe.wait_ge(sc_state, nth(i, o, NS, 2 * c + 1 + b))
                        mm = nc.tensor.matmul(ZB[:, b * H:(b + 1) * H], sst[:, (2 * c + b) % 4, :],
                                              qs[:, c * C + b * H:c * C + (b + 1) * H],
                                              start=False, stop=True, skip_group_check=True)
                    mm.then_inc(oc_full, 1)
                    ahead(c, 2)
                    if c == 1 and not first:
                        norm(i, o - 1, 1)

            for q in range(1, 4):
                project(pe, SLAB_C + q, q % 2)
            heads(pe, None, head, 0)
            for h in range(2):
                norm(HEADS_C // 2 - 1, 1, h)

        def scalar_c(act, own):
            nc.scalar.activation(eps[:, 3:4], eps[:, 3:4], ACT.Copy).then_inc(oc_copied, 1)
            act.wait_ge(lb_step, 2)
            nc.scalar.activation(lbp[:, 2:4, :], lbp[:, 2:4, :], ACT.Exp).then_inc(lb_exp, 1)
            act.wait_ge(lb_step, 3)
            nc.scalar.activation(lbp[:, 5, :], lbp[:, 5, :], ACT.Ln).then_inc(lb_exp, 1)

            def logs(i, o):
                for h in range(2):
                    act.wait_ge(proj_free[h], nth(i, o, 4, SLAB_C + 1))
                act.wait_ge(lb_ready, nth(i, o, 1, 1))
                own.on(nc.scalar.activation(ec, fc2[o % 2], ACT.Exp, scale=-1.0))
                own.wait()
                nc.scalar.activation(sp_, ec, ACT.Ln, bias=1.0).then_inc(ln_ready, 1)
                nc.scalar.activation(ec, ec, ACT.Ln, bias=1.0, scale=lbc[:, 0:1]).then_inc(ln_ready, 1)

            def query(i, o, h):
                act.wait_ge(proj_full[h], nth(i, o, 4, SLAB_C + 2))
                nc.scalar.activation(qs2[o % 2][:, h * HALF:(h + 1) * HALF], PJ[h][:], ACT.Silu).then_inc(proj_free[h], 1)

            def gate(i, o):
                for h in range(2):
                    act.wait_ge(proj_free[h], nth(i, o, 4, SLAB_C + 4))
                nc.scalar.activation(og2[o % 2], og2[o % 2], ACT.Silu).then_inc(gate_c_ready, 1)

            def decays(i, o, part):
                if part == 0:
                    act.wait_ge(gcc_ready, nth(i, o, 2, 1))
                    nc.scalar.activation(gcm, ec, ACT.Exp).then_inc(expc_ready, 1)
                    nc.scalar.activation(fac2[:, o % 2, 1, 0:NS - 1], fac2[:, o % 2, 0, 0:NS - 1],
                                         ACT.Exp).then_inc(expc_ready, 1)
                else:
                    act.wait_ge(gcc_ready, nth(i, o, 2, 2))
                    nc.scalar.activation(fc2[o % 2], fc2[o % 2], ACT.Exp, scale=-1.0, bias=lbc[:, 1:2]).then_inc(kc_ready, 1)

            def squares(i, o):
                act.wait_ge(oc_copied, nth(i, o, NC, NC + 1))
                nc.scalar.activation(osq, oc2[o % 2], ACT.Square).then_inc(osq_ready, 1)

            def norm(i, o, h):
                if h == 0:
                    act.wait_ge(head_done, nth(i, o, 1, 1))
                act.wait_ge(norm_full, nth(i, o, 2, h + 1))
                nc.scalar.activation(orn[:, h * HALF:(h + 1) * HALF], NORM[:], ACT.Ln, scale=1.0 / C,
                                     bias=eps[:, 0:1]).then_inc(norm_free, 1)
                if h:
                    act.wait_ge(norm_free, nth(i, o, 2, 2))
                    nc.scalar.activation(orn, orn, ACT.Exp, scale=-0.5).then_inc(orn_ready, 1)

            def head(i, o, first=False, last=False):
                if not first:
                    squares(i, o - 1)
                for c in range(NC):
                    j = c % 2
                    act.wait_ge(sc_full[j], nth(i, o, CB, SCC + c // 2 + 1))
                    nc.scalar.activation(tmc[:, j, :], SC[j][:, 0:256], ACT.Copy).then_inc(tc_ready, 1)
                    if c == 2 and not first:
                        for h in range(2):
                            norm(i, o - 1, h)
                    if c == 3:
                        if not last:
                            logs(i, o + 1)
                        nc.scalar.preload_act_table(ACT.Silu)
                        if not last:
                            query(i, o + 1, 0)
                        gate(i, o)
                    if c == 4 and not last:
                        query(i, o + 1, 1)
                        nc.scalar.preload_act_table_set("natural_log_exp_and_others")
                    if c == 6 and not last:
                        decays(i, o + 1, 0)
                    if c == 7 and not last:
                        decays(i, o + 1, 1)
                    act.wait_ge(oc_full, nth(i, o, NC, c + 1))
                    nc.scalar.activation(oc2[o % 2][:, c * C:(c + 1) * C], ZB[:, 0:P], ACT.Copy).then_inc(oc_copied, 1)

            act.wait_ge(stream_out, 16 * KT)
            act.wait_ge(h_lo_ready, KT // 2)
            logs(0, 0)
            nc.scalar.preload_act_table(ACT.Silu)
            for h in range(2):
                query(0, 0, h)
            nc.scalar.preload_act_table_set("natural_log_exp_and_others")
            for part in range(2):
                decays(0, 0, part)
            heads(act, own, head, 2)
            nc.scalar.preload_act_table_set("natural_log_exp_and_others")
            squares(HEADS_C // 2 - 1, 1)
            for h in range(2):
                norm(HEADS_C // 2 - 1, 1, h)

        def vector_c(dve, own):
            lb0, lb1 = oth[:, LB0 - 44:LB0 - 36], oth[:, LB1 - 44:LB1 - 36]
            own.on(nc.vector.tensor_tensor(lbp[:, 1, :], lb0, lb1, ALU.max))
            own.wait()
            nc.vector.tensor_tensor(lbp[:, 2, :], lb0, lbp[:, 1, :], ALU.subtract).then_inc(lb_step, 1)
            nc.vector.tensor_tensor(lbp[:, 3, :], lb1, lbp[:, 1, :], ALU.subtract).then_inc(lb_step, 1)
            dve.wait_ge(lb_exp, 1)
            own.on(nc.vector.tensor_tensor(lbp[:, 1, :], lbp[:, 2, :], lbp[:, 3, :], ALU.add))
            own.wait()
            own.on(nc.vector.reciprocal(lbp[:, 1, :], lbp[:, 1, :]))
            own.wait()
            own.on(nc.vector.tensor_tensor(lbp[:, 4, :], lbp[:, 3, :], lbp[:, 1, :], ALU.mult))
            nc.vector.tensor_tensor(lbp[:, 5, :], lbp[:, 2, :], lbp[:, 1, :], ALU.mult).then_inc(lb_step, 1)
            own.on(nc.vector.memset(stc, 0.0))
            nc.vector.memset(sc2_t, 0.0).then_inc(head_done, 1)
            own.on(nc.vector.memset(reset[:], 1.0))
            own.wait()
            own.on(nc.vector.memset(reset[:].rearrange("p (c t) -> p c t", t=H)[:, :, 0:1], 0.0))
            own.wait()
            dve.wait_ge(lb_exp, 2)

            def evacuate(i, o, q, h):
                dst = (fc2, None, vc2, og2)[q][o % 2][:, h * HALF:(h + 1) * HALF]
                dve.wait_ge(proj_full[h], nth(i, o, 4, SLAB_C + q + 1))
                if q == 0:
                    nc.vector.tensor_scalar(dst, PJ[h][:], -43.0, None, ALU.max).then_inc(proj_free[h], 1)
                else:
                    nc.vector.tensor_scalar(dst, PJ[h][:], 1.0, None, ALU.mult).then_inc(proj_free[h], 1)

            def bounds(i, o):
                n = bass.ds(at(i, 2, o), 1)
                nc.vector.tensor_scalar(lbc[:, 0:2].rearrange("p (k o) -> p k o", o=1), lbp[:, 4:6, n], 1.0,
                                        None, ALU.mult).then_inc(lb_ready, 1)

            def sums(i, o):
                dve.wait_ge(ln_ready, nth(i, o, 2, 2))
                own.on(nc.vector.tensor_tensor(ec, ec, sp_, ALU.subtract))
                own.on(nc.vector.tensor_tensor(fc2[o % 2], fc2[o % 2], sp_, ALU.add))
                own.wait()
                for h in range(2):
                    own.on(nc.vector.tensor_tensor_scan(gcm[:, h * HALF:(h + 1) * HALF], reset[:],
                                                        ec[:, h * HALF:(h + 1) * HALF], 0.0, ALU.mult, ALU.add))
                own.wait()

            def centre(i, o):
                g3 = gcm.rearrange("p (c t) -> p c t", c=NS)
                e3 = ec.rearrange("p (c t) -> p c t", c=NS)
                mid = H // 2 - 1
                own.on(nc.vector.tensor_tensor(e3, g3, g3[:, :, mid:mid + 1].broadcast_to([P, NS, H]), ALU.subtract))
                own.wait()
                nc.vector.tensor_tensor(fac2[:, o % 2, 0, 0:NS - 1], e3[:, 0:NS - 1, H - 1:H].rearrange("p c o -> p (c o)"),
                                        g3[:, 1:NS, mid:mid + 1].rearrange("p c o -> p (c o)"),
                                        ALU.add).then_inc(gcc_ready, 1)
                nc.vector.tensor_tensor(fc2[o % 2], fc2[o % 2], ec, ALU.add).then_inc(gcc_ready, 1)

            def decay_queries(i, o):
                dve.wait_ge(expc_ready, nth(i, o, 2, 2))
                nc.vector.tensor_tensor(qs2[o % 2], qs2[o % 2], gcm, ALU.mult).then_inc(qc_ready, 1)

            def finish(i, o):
                oc, og = oc2[o % 2], og2[o % 2]
                dve.wait_ge(orn_ready, nth(i, o, 1, 1))
                dve.wait_ge(gate_c_ready, nth(i, o, 1, 1))
                own.on(nc.vector.scalar_tensor_tensor(oc, oc, oth[:, CN - 44:CN - 43], orn, ALU.mult, ALU.mult))
                own.wait()
                nc.vector.tensor_tensor(yT[:, bass.ds(at(i, 2, o), 1), :], oc.rearrange("p (o t) -> p o t", o=1),
                                        og.rearrange("p (o t) -> p o t", o=1), ALU.mult).then_inc(head_done, 1)

            def head(i, o, first=False, last=False):
                fac = fac2[:, o % 2, 1, :]
                dve.wait_ge(oc_copied, nth(i, o, NC, 1))
                nc.vector.memset(sst[:, 0, :], 0.0).then_inc(sc_state, 1)
                for c in range(NC):
                    j = c % 2
                    dve.wait_ge(sc_full[j], nth(i, o, CB, SCC + c // 2 + 1))
                    dve.wait_ge(tc_ready, nth(i, o, NC, c + 1))
                    own.on(nc.vector.tensor_tensor(stc[0:64, j, 0:64], SC[j][0:64, 256:320], cst[0:64, CM + P:CM + P + 64],
                                                   ALU.mult))
                    nc.vector.tensor_tensor(stc[64:128, j, 64:128], SC[j][64:128, 320:384],
                                            cst[64:128, CM + P + 64:CM + 2 * P], ALU.mult).then_inc(sc_free[j], 1)
                    for b in range(2):
                        n = 2 * c + b
                        if n == NS - 1:
                            break
                        dve.wait_ge(inc_full[b], nth(i, o, NC, c + 1))
                        own.on(nc.vector.tensor_scalar(sc2_t[:, b, :], INC[b][:, 0:P], fac[:, n:n + 1], None, ALU.mult))
                        own.wait()
                        dve.wait_ge(sc_state, nth(i, o, NS, n + 1))
                        if c:
                            dve.wait_ge(oc_full, nth(i, o, NC, c))
                        nc.vector.scalar_tensor_tensor(sst[:, (n + 1) % 4, :], sst[:, n % 4, :], fac[:, n:n + 1],
                                                       sc2_t[:, b, :], ALU.mult, ALU.add).then_inc(sc_state, 1)
                    if not last:
                        if c == 1:
                            dve.wait_ge(kc_ready, nth(i, o, 1, 1))
                            bounds(i, o + 1)
                        if c in (1, 2):
                            evacuate(i, o + 1, 0, c - 1)
                        if c == 4:
                            sums(i, o + 1)
                        if c == 5:
                            centre(i, o + 1)
                        if c in (5, 6):
                            evacuate(i, o + 1, 2, c - 5)
                        if c == 6:
                            decay_queries(i, o + 1)
                        if c == 7:
                            for h in range(2):
                                evacuate(i, o + 1, 3, h)
                    if c == 3 and not first:
                        finish(i, o - 1)

            dve.wait_ge(stream_out, 16 * KT)
            dve.wait_ge(h_lo_ready, KT // 2)
            bounds(0, 0)
            for h in range(2):
                evacuate(0, 0, 0, h)
            sums(0, 0)
            for h in range(2):
                evacuate(0, 0, 2, h)
            centre(0, 0)
            decay_queries(0, 0)
            for h in range(2):
                evacuate(0, 0, 3, h)
            heads(dve, own, head, 2 * (NC + NS - 1 + 5 + 1))
            finish(HEADS_C // 2 - 1, 1)

        block = ctx.enter_context(nc.Block())

        @block.sync
        def _(sp):
            sync_0(sp)
            sync_a(sp)
            sync_b(sp)
            sync_o(sp, 0, w_out0)
            sync_c(sp)
            sync_o(sp, 1, w_out1)
            sync_out(sp)

        @block.gpsimd
        def _(pool):
            own = Steps(pool, own_pool)
            pool_0(pool, own)
            pool_a(pool, own)
            pool_b(pool, own, 2, len(B_SLABS))
            pool_o(pool, own, 0)
            pool_c(pool, own)
            pool_o(pool, own, 1)

        @block.tensor
        def _(pe):
            tensor_0(pe)
            phase_end(pe, 0, tensor_a_first)
            tensor_a(pe)
            phase_end(pe, 1, tensor_b_first)
            tensor_b(pe)
            phase_end(pe, 2)
            tensor_o(pe, 0)
            phase_end(pe, 3, tensor_c_first)
            tensor_c(pe)
            phase_end(pe, 4)
            tensor_o(pe, 1)

        @block.scalar
        def _(act):
            own = Steps(act, own_act)
            scalar_0(act, own)
            phase_end(act, 0)
            scalar_a(act, own)
            phase_end(act, 1)
            scalar_b(act, own)
            phase_end(act, 2)
            scalar_o(act, own, 0)
            phase_end(act, 3)
            scalar_c(act, own)
            phase_end(act, 4)
            scalar_o(act, own, 1)

        @block.vector
        def _(dve):
            own = Steps(dve, own_dve)
            vector_0(dve, own)
            phase_end(dve, 0)
            vector_a(dve, own)
            phase_end(dve, 1)
            vector_b(dve, own)
            phase_end(dve, 2)
            vector_o(dve, own, 0)
            phase_end(dve, 3)
            vector_c(dve, own)
            phase_end(dve, 4)
            vector_o(dve, own, 1)


_INS = ["x", "rel_bias_table", "lower_bounds", "l0_pre_norm", "l0_post_norm", "l0_w_in", "l0_w_out",
        "a_mu", "a_w0", "a_w2", "a_a0", "a_a2", "a_k_k", "a_k_a", "a_r_k", "a_ln_w", "a_ln_b", "b_sinks",
        "l1_pre_norm", "l1_post_norm", "l1_w_in", "l1_w_out", "c_norm_w"]


def kernel(**inputs):
    import concourse.bacc as bacc
    from concourse.bass_utils import run_bass_kernel_spmd

    nc = bacc.Bacc("TRN2", target_bir_lowering=False, num_devices=1)
    arrays = {name: np.ascontiguousarray(inputs[name]) for name in _INS}
    arrays["x"] = arrays["x"].reshape(T, D)
    arrays["constants"] = constants()
    arrays["buckets"] = bucket_table()
    args = [nc.dram_tensor(f"in_{name}", a.shape, F32, kind="ExternalInput").ap() for name, a in arrays.items()]
    args.append(nc.dram_tensor("bias_rows", (P, 8, 384), F32).ap())
    args.append(nc.dram_tensor("stream", (KT, P, T), F32).ap())
    out = nc.dram_tensor("out_0", (T, D), F32, kind="ExternalOutput").ap()
    trunk(nc, *args, out)
    r = run_bass_kernel_spmd(nc, [{f"in_{name}": a for name, a in arrays.items()}], core_ids=[0])
    return r.results[0]["out_0"].reshape(1, T, D)
```
